# Optimizing a Trainium2 kernel written in Bass

```python
import math
import jax
import jax.numpy as jnp
from jax import lax
import numpy as np

D_MODEL = 1024
BATCH = 1
SEQ = 1024
DEPTH = 1

MEM_LEN = 256
GROUP_WIDTH = 384
MIX_WIDTH = 4 * GROUP_WIDTH
SSD_HEAD_DIM = 64
SSD_HEADS = GROUP_WIDTH // SSD_HEAD_DIM
SSD_GROUPS = 2
SSD_STATE = 128
SSD_CONV = 4
SSD_CHUNK = 128
SSD_CONV_CH = GROUP_WIDTH + 2 * SSD_GROUPS * SSD_STATE
DT_MIN = 0.001
DT_MAX = 0.1
SC_WIDTH = 3
ATT_HEAD_DIM = 64
ATT_HEADS = 6
ATT_WIDTH = ATT_HEADS * ATT_HEAD_DIM
DILATED_PATTERNS = ((128, 1), (512, 4), (2048, 16))
CF_KERNEL = 31
IN_SIZES = (GROUP_WIDTH, SSD_CONV_CH, SSD_HEADS,
            GROUP_WIDTH, GROUP_WIDTH, GROUP_WIDTH,
            ATT_WIDTH, ATT_WIDTH, ATT_WIDTH,
            GROUP_WIDTH, GROUP_WIDTH)
N_IN = 6 * GROUP_WIDTH + SSD_CONV_CH + SSD_HEADS + 3 * ATT_WIDTH
CA_HEADS = 4
CA_HEAD_DIM = D_MODEL // CA_HEADS
N_EXPERT_GROUPS = 4
EXPERTS_PER_GROUP = 8
N_EXPERTS = N_EXPERT_GROUPS * EXPERTS_PER_GROUP
TOP_K = 2
EXPERT_HIDDEN = D_MODEL // 2
MOE_BLOCK = 256

RMS_EPS = 1e-6
LN_EPS = 1e-5

kernel_name = 'hymba_style_ssd_conv_dilated_attn_hmoe'

def rms_norm(x, g):
    xf = x.astype(jnp.float32)
    y = xf * lax.rsqrt(jnp.mean(xf * xf, axis=-1, keepdims=True) + RMS_EPS)
    return (y * g.astype(jnp.float32)).astype(x.dtype)

def layer_norm(x, g, b):
    xf = x.astype(jnp.float32)
    mu = jnp.mean(xf, axis=-1, keepdims=True)
    xc = xf - mu
    y = xc * lax.rsqrt(jnp.mean(xc * xc, axis=-1, keepdims=True) + LN_EPS)
    return (y * g.astype(jnp.float32) + b.astype(jnp.float32)).astype(x.dtype)

def split_last(t, sizes):
    out, o = [], 0
    for s in sizes:
        out.append(t[..., o:o + s])
        o += s
    return out

def causal_dwconv(x, w, b=None):
    k, c = w.shape
    y = lax.conv_general_dilated(x, w[:, None, :].astype(x.dtype), window_strides=(1,),
                                 padding=((k - 1, 0),), dimension_numbers=('NWC', 'WIO', 'NWC'),
                                 feature_group_count=c)
    if b is not None:
        y = y + b.astype(x.dtype)
    return y

def ssd_chunked(x, da, b, c):
    bsz, s, nh, p = x.shape
    g, n = b.shape[2], b.shape[3]
    j = nh // g
    q = SSD_CHUNK
    nc = s // q
    x = x.reshape(bsz, nc, q, g, j, p)
    b = b.reshape(bsz, nc, q, g, n)
    c = c.reshape(bsz, nc, q, g, n)
    a_cs = jnp.cumsum(da.reshape(bsz, nc, q, g, j).transpose(0, 3, 4, 1, 2), axis=-1)
    tril = jnp.tril(jnp.ones((q, q), dtype=bool))
    seg = jnp.exp(jnp.where(tril, a_cs[..., :, None] - a_cs[..., None, :], -jnp.inf))
    cb = jnp.einsum('bclgn,bcsgn->bcgls', c, b)
    y_diag = jnp.einsum('bcgls,bgjcls,bcsgjp->bclgjp', cb, seg, x)
    decay = jnp.exp(a_cs[..., -1:] - a_cs)
    states = jnp.einsum('bclgn,bgjcl,bclgjp->bcgjpn', b, decay, x)
    chunk_decay = jnp.exp(a_cs[..., -1])

    def step(h, inp):
        st, dec = inp
        return h * dec[..., None, None] + st, h

    _, prev = lax.scan(step, jnp.zeros_like(states[:, 0]),
                       (jnp.moveaxis(states, 1, 0), jnp.moveaxis(chunk_decay, -1, 0)))
    prev = jnp.moveaxis(prev, 0, 1)
    y_off = jnp.einsum('bclgn,bcgjpn,bgjcl->bclgjp', c, prev, jnp.exp(a_cs))
    return (y_diag + y_off).reshape(bsz, s, nh, p)

def dilated_branch(q, k, v, window, dilation):
    bsz, s, nh, dh = q.shape
    n = window // dilation
    blk = n
    span = dilation * blk
    sp = -(-s // span) * span
    nb = sp // span

    def to_blocks(t):
        t = jnp.pad(t.astype(jnp.float32), ((0, 0), (0, sp - s), (0, 0), (0, 0)))
        return t.reshape(bsz, nb, blk, dilation, nh, dh).transpose(0, 3, 4, 1, 2, 5)

    def band(t):
        prev = jnp.pad(t, ((0, 0), (0, 0), (0, 0), (1, 0), (0, 0), (0, 0)))[:, :, :, :-1]
        return jnp.concatenate([prev, t], axis=4)

    qb = to_blocks(q)
    kb = band(to_blocks(k))
    vb = band(to_blocks(v))
    sc = jnp.einsum('brhnqe,brhnke->brhnqk', qb, kb) * (ATT_HEAD_DIM ** -0.5)
    bi = jnp.arange(nb)[:, None, None]
    qq = jnp.arange(blk)[None, :, None]
    kk = jnp.arange(2 * blk)[None, None, :]
    rel = qq + blk - kk
    valid = (rel >= 0) & (rel <= n) & ((bi > 0) | (kk >= blk))
    sc = jnp.where(valid, sc, -jnp.inf)
    m = jnp.max(sc, axis=-1, keepdims=True)
    pr = jnp.exp(sc - m)
    den = jnp.sum(pr, axis=-1)
    o = jnp.einsum('brhnqk,brhnke->brhnqe', pr, vb) / den[..., None]
    lse = m[..., 0] + jnp.log(den)
    o = o.transpose(0, 3, 4, 1, 2, 5).reshape(bsz, sp, nh, dh)[:, :s]
    lse = lse.transpose(0, 3, 4, 1, 2).reshape(bsz, sp, nh)[:, :s]
    return o, lse

def dilated_attention(q, k, v, q_norm, k_norm):
    bsz, s, _ = q.shape
    q = rms_norm(q.reshape(bsz, s, ATT_HEADS, ATT_HEAD_DIM), q_norm)
    k = rms_norm(k.reshape(bsz, s, ATT_HEADS, ATT_HEAD_DIM), k_norm)
    v = v.reshape(bsz, s, ATT_HEADS, ATT_HEAD_DIM)
    outs, lses = [], []
    for window, dilation in DILATED_PATTERNS:
        o, l = dilated_branch(q, k, v, window, dilation)
        outs.append(o)
        lses.append(l)
    wts = jax.nn.softmax(jnp.stack(lses, axis=0), axis=0)
    o = jnp.sum(wts[..., None] * jnp.stack(outs, axis=0), axis=0)
    return o.reshape(bsz, s, ATT_WIDTH).astype(v.dtype)

def hybrid_mixer(h, w_in, ssd_conv_w, ssd_conv_b, ssd_dt_bias, ssd_a_log, ssd_d, ssd_norm,
                 sc_conv_w, attn_q_norm, attn_k_norm, cf_conv_w, cf_conv_b, cf_ln_g, cf_ln_b, w_out):
    bsz, s, _ = h.shape
    proj = h @ w_in
    (z, xbc, dt_raw, sc_b, sc_c, sc_h, q, k, v, cf_a, cf_g) = split_last(proj, IN_SIZES)

    xbc = jax.nn.silu(causal_dwconv(xbc, ssd_conv_w, ssd_conv_b))
    xs, bm, cm = split_last(xbc, (GROUP_WIDTH, SSD_GROUPS * SSD_STATE, SSD_GROUPS * SSD_STATE))
    xs = xs.reshape(bsz, s, SSD_HEADS, SSD_HEAD_DIM).astype(jnp.float32)
    bm = bm.reshape(bsz, s, SSD_GROUPS, SSD_STATE).astype(jnp.float32)
    cm = cm.reshape(bsz, s, SSD_GROUPS, SSD_STATE).astype(jnp.float32)
    dt = jax.nn.softplus(dt_raw.astype(jnp.float32) + ssd_dt_bias.astype(jnp.float32))
    a = -jnp.exp(ssd_a_log.astype(jnp.float32))
    y = ssd_chunked(xs * dt[..., None], dt * a, bm, cm) + xs * ssd_d.astype(jnp.float32)[:, None]
    y = y.reshape(bsz, s, GROUP_WIDTH)
    y_ssd = rms_norm(y * jax.nn.silu(z.astype(jnp.float32)), ssd_norm).astype(h.dtype)

    y_sc = sc_b * causal_dwconv(sc_c * sc_h, sc_conv_w)

    y_att = dilated_attention(q, k, v, attn_q_norm, attn_k_norm)

    u = causal_dwconv(cf_a * jax.nn.sigmoid(cf_g), cf_conv_w, cf_conv_b)
    y_cf = jax.nn.silu(layer_norm(u, cf_ln_g, cf_ln_b))

    return jnp.concatenate([y_ssd, y_sc, y_att, y_cf], axis=-1) @ w_out

def memory_cross_attention(h, mem_n, wq, wkv, q_norm, k_norm, wo):
    bsz, s, _ = h.shape
    m = mem_n.shape[1]
    q = rms_norm((h @ wq).reshape(bsz, s, CA_HEADS, CA_HEAD_DIM), q_norm)
    k, v = split_last(mem_n @ wkv, (D_MODEL, D_MODEL))
    k = rms_norm(k.reshape(bsz, m, CA_HEADS, CA_HEAD_DIM), k_norm)
    v = v.reshape(bsz, m, CA_HEADS, CA_HEAD_DIM)
    sc = jnp.einsum('bshe,bmhe->bhsm', q.astype(jnp.float32), k.astype(jnp.float32)) * (CA_HEAD_DIM ** -0.5)
    pr = jax.nn.softmax(sc, axis=-1)
    o = jnp.einsum('bhsm,bmhe->bshe', pr, v.astype(jnp.float32)).astype(h.dtype)
    return o.reshape(bsz, s, D_MODEL) @ wo

def hierarchical_moe(h, wg, bg, we, be, w_gate, w_up, w_down):
    bsz, s, d = h.shape
    t = bsz * s
    ht = h.reshape(t, d)
    g_prob = jax.nn.softmax((ht @ wg + bg).astype(jnp.float32), axis=-1)
    g_p, g_idx = lax.top_k(g_prob, 1)
    e_logits = (ht @ we + be).astype(jnp.float32).reshape(t, N_EXPERT_GROUPS, EXPERTS_PER_GROUP)
    e_in = e_logits[jnp.arange(t), g_idx[:, 0]]
    e_p, e_loc = lax.top_k(jax.nn.softmax(e_in, axis=-1), TOP_K)
    gates = g_p * e_p / jnp.sum(e_p, axis=-1, keepdims=True)
    expert = g_idx * EXPERTS_PER_GROUP + e_loc

    a = t * TOP_K
    flat_e = expert.reshape(a)
    flat_tok = jnp.repeat(jnp.arange(t), TOP_K)
    flat_g = gates.reshape(a)
    order = jnp.argsort(flat_e)
    e_s, tok_s, g_s = flat_e[order], flat_tok[order], flat_g[order]
    counts = jnp.zeros((N_EXPERTS,), jnp.int32).at[flat_e].add(1)
    padded = ((counts + MOE_BLOCK - 1) // MOE_BLOCK) * MOE_BLOCK
    ends_pad = jnp.cumsum(padded)
    starts_pad = ends_pad - padded
    starts = jnp.cumsum(counts) - counts
    dest = starts_pad[e_s] + jnp.arange(a) - starts[e_s]
    p_rows = (-(-a // MOE_BLOCK)) * MOE_BLOCK + N_EXPERTS * MOE_BLOCK
    n_blocks = p_rows // MOE_BLOCK
    buf = jnp.zeros((p_rows, d), h.dtype).at[dest].set(ht[tok_s])
    blk_e = jnp.minimum(jnp.searchsorted(ends_pad, jnp.arange(n_blocks) * MOE_BLOCK, side='right'),
                        N_EXPERTS - 1)

    def expert_block(args):
        xb, e = args
        hid = jax.nn.silu(xb @ w_gate[e]) * (xb @ w_up[e])
        return hid @ w_down[e]

    yb = lax.map(expert_block, (buf.reshape(n_blocks, MOE_BLOCK, d), blk_e)).reshape(p_rows, d)
    y = jnp.zeros((t, d), h.dtype).at[tok_s].add(yb[dest] * g_s[:, None].astype(h.dtype))
    return y.reshape(bsz, s, d)

def setup_inputs(seed: int = 0) -> dict:
    key = jax.random.key(seed)
    keys = iter(jax.random.split(key, 48))
    f32 = jnp.float32
    L = DEPTH

    def normal(shape, scale):
        return jax.random.normal(next(keys), shape, f32) * scale

    def gain(shape):
        return 1.0 + normal(shape, 0.02)

    x = normal((BATCH, SEQ, D_MODEL), 1.0)
    mem = normal((BATCH, MEM_LEN, D_MODEL), 1.0)
    dt_init = jnp.exp(jax.random.uniform(next(keys), (L, SSD_HEADS), f32,
                                         math.log(DT_MIN), math.log(DT_MAX)))
    ssd_dt_bias = dt_init + jnp.log(-jnp.expm1(-dt_init))
    ssd_a_log = jnp.log(jax.random.uniform(next(keys), (L, SSD_HEADS), f32, 1.0, 16.0))
    return {
        'x': x,
        'mem': mem,
        'norm_mix': gain((L, D_MODEL)),
        'w_in': normal((L, D_MODEL, N_IN), D_MODEL ** -0.5),
        'ssd_conv_w': normal((L, SSD_CONV, SSD_CONV_CH), SSD_CONV ** -0.5),
        'ssd_conv_b': normal((L, SSD_CONV_CH), 0.02),
        'ssd_dt_bias': ssd_dt_bias,
        'ssd_a_log': ssd_a_log,
        'ssd_d': 1.0 + normal((L, SSD_HEADS), 0.1),
        'ssd_norm': gain((L, GROUP_WIDTH)),
        'sc_conv_w': normal((L, SC_WIDTH, GROUP_WIDTH), SC_WIDTH ** -0.5),
        'attn_q_norm': gain((L, ATT_HEAD_DIM)),
        'attn_k_norm': gain((L, ATT_HEAD_DIM)),
        'cf_conv_w': normal((L, CF_KERNEL, GROUP_WIDTH), CF_KERNEL ** -0.5),
        'cf_conv_b': normal((L, GROUP_WIDTH), 0.02),
        'cf_ln_g': gain((L, GROUP_WIDTH)),
        'cf_ln_b': normal((L, GROUP_WIDTH), 0.02),
        'w_out': normal((L, MIX_WIDTH, D_MODEL), MIX_WIDTH ** -0.5),
        'norm_ca': gain((L, D_MODEL)),
        'norm_mem': gain((L, D_MODEL)),
        'ca_wq': normal((L, D_MODEL, D_MODEL), D_MODEL ** -0.5),
        'ca_wkv': normal((L, D_MODEL, 2 * D_MODEL), D_MODEL ** -0.5),
        'ca_q_norm': gain((L, CA_HEAD_DIM)),
        'ca_k_norm': gain((L, CA_HEAD_DIM)),
        'ca_wo': normal((L, D_MODEL, D_MODEL), D_MODEL ** -0.5),
        'norm_ffn': gain((L, D_MODEL)),
        'router_group_w': normal((L, D_MODEL, N_EXPERT_GROUPS), D_MODEL ** -0.5),
        'router_group_b': normal((L, N_EXPERT_GROUPS), 0.01),
        'router_expert_w': normal((L, D_MODEL, N_EXPERTS), D_MODEL ** -0.5),
        'router_expert_b': normal((L, N_EXPERTS), 0.01),
        'exp_w_gate': normal((L, N_EXPERTS, D_MODEL, EXPERT_HIDDEN), D_MODEL ** -0.5),
        'exp_w_up': normal((L, N_EXPERTS, D_MODEL, EXPERT_HIDDEN), D_MODEL ** -0.5),
        'exp_w_down': normal((L, N_EXPERTS, EXPERT_HIDDEN, D_MODEL), EXPERT_HIDDEN ** -0.5),
    }

def reference(x, mem, norm_mix, w_in, ssd_conv_w, ssd_conv_b, ssd_dt_bias, ssd_a_log, ssd_d, ssd_norm,
              sc_conv_w, attn_q_norm, attn_k_norm, cf_conv_w, cf_conv_b, cf_ln_g, cf_ln_b, w_out,
              norm_ca, norm_mem, ca_wq, ca_wkv, ca_q_norm, ca_k_norm, ca_wo,
              norm_ffn, router_group_w, router_group_b, router_expert_w, router_expert_b,
              exp_w_gate, exp_w_up, exp_w_down):
    for l in range(DEPTH):
        h = rms_norm(x, norm_mix[l])
        x = x + hybrid_mixer(h, w_in[l], ssd_conv_w[l], ssd_conv_b[l], ssd_dt_bias[l], ssd_a_log[l],
                             ssd_d[l], ssd_norm[l], sc_conv_w[l], attn_q_norm[l], attn_k_norm[l],
                             cf_conv_w[l], cf_conv_b[l], cf_ln_g[l], cf_ln_b[l], w_out[l])
        h = rms_norm(x, norm_ca[l])
        x = x + memory_cross_attention(h, rms_norm(mem, norm_mem[l]), ca_wq[l], ca_wkv[l],
                                       ca_q_norm[l], ca_k_norm[l], ca_wo[l])
        h = rms_norm(x, norm_ffn[l])
        x = x + hierarchical_moe(h, router_group_w[l], router_group_b[l], router_expert_w[l],
                                 router_expert_b[l], exp_w_gate[l], exp_w_up[l], exp_w_down[l])
    return x


_drawn_inputs = setup_inputs


def setup_inputs(seed=0):
    import zlib

    import numpy as np

    out = dict(_drawn_inputs(seed))
    spreads = {}
    factors = {'ssd_norm': 3.968,
     'attn_q_norm': 5.535,
     'attn_k_norm': 8.0,
     'cf_conv_b': 3.386,
     'cf_ln_g': 4.076,
     'cf_ln_b': 5.214,
     'norm_ca': 8.0,
     'norm_mem': 5.591,
     'ca_q_norm': 8.0,
     'ca_k_norm': 8.0,
     'router_group_b': 32.704,
     'router_expert_b': 34.04,
     'norm_ffn': 8.0}
    for name, (base, spread) in spreads.items():
        noise = np.random.default_rng([zlib.crc32(name.encode()), seed]).standard_normal(out[name].shape)
        drawn = base * np.exp(spread * noise) if base else spread * noise
        out[name] = jnp.asarray(drawn.astype(out[name].dtype))
    for name, factor in factors.items():
        out[name] = (out[name] * factor).astype(out[name].dtype)
    return out
```

```python
from collections import namedtuple
from contextlib import ExitStack

import numpy as np
import concourse.bass as bass
import concourse.mybir as mybir
from concourse.alu_op_type import AluOpType as ALU

F32 = mybir.dt.float32
I32 = mybir.dt.int32
ACT = mybir.ActivationFunctionType
LN_EXP = "natural_log_exp_and_others"
AX = mybir.AxisListType.X
ds = bass.ds

P = 128
D = 1024
SEQ = 1024
MEM = 256
KD = D // P
NT = SEQ // P
GW = 384
GT = GW // P
HEADS = 6
SSD_NG = 2
HD = 64
XBC_T = 7
CF_K, SSD_K, SC_K = 31, 4, 3
CA_H, CA_D = 4, 256
NG, EPG = 4, 8
NE = NG * EPG
EH = 512
RMS_EPS, LN_EPS = 1e-6, 1e-5
BIG = 1.0e30
TOK_COLS = 4 * GW + HEADS
NFEAT = 3 * XBC_T + 1
MAX_BLOCKS = SEQ // P
MAX_OVER = 2 * SEQ // P - 1
SKIP = 1 << 20

PC = {}
_at = 0
for _n, _w in (("g_mix", KD), ("g_ca", KD), ("g_mem", KD), ("g_ffn", KD), ("cf_w", GT * CF_K), ("cf_b", GT),
               ("ln_g", GT), ("ln_b", GT), ("ssd_w", XBC_T * SSD_K), ("ssd_b", XBC_T), ("sc_w", GT * SC_K),
               ("ssd_g", GT), ("att_q", 1), ("att_k", 1), ("ca_q", 2), ("ca_k", 2)):
    PC[_n] = _at
    _at += _w
NPAR = _at
RC = {}
_at = 0
for _n, _w in (("dt_b", HEADS), ("a_log", HEADS), ("ssd_d", HEADS), ("r_b", NG + NE), ("rank_g", NG), ("rank_e", NE), ("eps_rms", 1), ("eps_ln", 1)):
    RC[_n] = _at
    _at += _w
NROW = _at

AT_CONST = 0
AT_PAR = 1664
AT_ROW = AT_PAR + 192
AT_KEEP = 1952
AT_HT = 2048
AT_QT, AT_KT, AT_V, AT_Z, AT_DT = 10240, 13312, 16384, 19456, 22528
AT_B = 22592
ARENA = 53100


def done(t, m=1, n=None):
    return (t + 2) * m + (m if n is None else n + 1)


class Env:
    pass


def bc(ap, shape):
    return ap.to_broadcast(shape)


def cut(ap, t):
    return ap[:, ds(t, 1), :].rearrange("p o n -> p (o n)")


def prime(eng, *sems):
    for s in sems:
        s, m = s if isinstance(s, tuple) else (s, 1)
        eng.sem_inc(s, 2 * m)


def newton(v, r, ss, tmp, n, eps=RMS_EPS):
    v.tensor_tensor(tmp, r, r, ALU.mult)
    v.drain()
    v.scalar_tensor_tensor(tmp, ss, float(n) * eps, tmp, ALU.add, ALU.mult)
    v.drain()
    v.tensor_scalar(tmp, tmp, -0.5 / n, 1.5, ALU.mult, ALU.add)
    v.drain()
    v.tensor_tensor(r, r, tmp, ALU.mult)
    v.drain()


def rstd(act, r, ss, n, eps):
    act.activation(r, ss, ACT.Ln, scale=1.0 / n, bias=eps)
    act.drain()
    return act.activation(r, r, ACT.Exp, scale=-0.5)


def phase_tokens(nc, e):
    A = e.A
    HT = A(AT_HT, KD, SEQ)
    QT, KT = A(AT_QT, GT, SEQ), A(AT_KT, GT, SEQ)
    V, Z, DT = A(AT_V, NT, GW), A(AT_Z, NT, GW), A(AT_DT, NT, HEADS)
    at = AT_B
    W = A(at, KD, TOK_COLS); at += KD * TOK_COLS
    X = [A(at + D * p, D) for p in (0, 1)]; at += 2 * D
    H = [A(at + D * p, D) for p in (0, 1)]; at += 2 * D
    HC = [A(at + D * p, KD, P) for p in (0, 1)]; at += 2 * D
    Y = [A(at + 1536 * p, 1536) for p in (0, 1)]; at += 3072
    SQ = A(at, 2 * GW); at += 2 * GW
    ZT = A(at, GW); at += GW
    junk = A(at, D); at += D
    TB = A(at, 1024); at += 1024
    ZROW = A(at, 1024); at += 1024
    ss, rs = A(at, 2), A(at + 2, 2)
    qss, qr, qt = A(at + 4, 12), A(at + 16, 12), A(at + 28, 12)
    assert at + 64 <= ARENA
    S = e.sems("tok", "const_ld par_ld row_ld w_ld x_ld0 x_ld1 tab_init tab_st r_ready h_ready T_psum hT_ready ht_copied "
               "proj_psum dt_psum y_ready z_exp z_done qss_ready qr_ready qn_ready qk_psum qk_done dt_done")
    x_ld = [S.x_ld0, S.x_ld1]
    PH = e.pair(0)
    PQK = e.pair(3)
    PP = [e.PS[:, 2 + n, :] for n in range(3)]
    PDT = e.PS[:, 5, 0:HEADS]
    half = NT // 2

    with nc.Block() as block:
        @block.sync
        def _(sp):
            sp.dma_start(e.arena[:, AT_CONST:AT_PAR], e.d.consts).then_inc(S.const_ld, 16)
            sp.dma_start(e.par, e.d.par).then_inc(S.par_ld, 16)
            sp.dma_start(e.row, e.d.row.partition_broadcast(P)).then_inc(S.row_ld, 16)
            for p in (0, 1):
                sp.dma_start(X[p], e.d.x[p * P:(p + 1) * P, :]).then_inc(x_ld[p], 16)
            sp.dma_start(W, e.d.w_tok).then_inc(S.w_ld, 16)
            with sp.Fori(1, half) as i:
                for p in (0, 1):
                    t = 2 * i + p
                    sp.wait_ge(S.h_ready, done(t - 2))
                    sp.dma_start(X[p], e.d.x[ds(t * P, P), :]).then_inc(x_ld[p], 16)
            sp.wait_ge(S.tab_init, 4)
            sp.dma_start(e.d.tab.rearrange("(p r) c -> p (r c)", p=P), TB.bitcast(I32)).then_inc(S.tab_st, 16)
            sp.dma_start(e.d.h3[SEQ:SEQ + 1, :], ZROW[0:1, :]).then_inc(S.tab_st, 16)
            sp.wait_ge(S.tab_st, 32)

        @block.gpsimd
        def _(g):
            tb = TB.bitcast(I32).rearrange("p (r c) -> p r c", c=4)
            g.memset(ZROW[0:1, :], 0.0).then_inc(S.tab_init, 1)
            g.memset(TB.bitcast(I32), 0).then_inc(S.tab_init, 1)
            g.wait_ge(S.tab_init, 2)
            g.memset(tb[:, :, 0:1], SEQ).then_inc(S.tab_init, 1)
            g.memset(tb[:, :, 1:2], SKIP).then_inc(S.tab_init, 1)
            prime(g, S.ht_copied)
            with g.Fori(0, half) as i:
                for p in (0, 1):
                    t = 2 * i + p
                    g.wait_ge(S.hT_ready, done(t))
                    g.tensor_copy(HT[:, :, ds(t * P, P)], HC[p]).then_inc(S.ht_copied, 1)

        @block.scalar
        def _(act):
            def rms(p, n):
                act.wait_ge(x_ld[p], n)
                act.activation(junk, X[p], ACT.Square, accum_out=ss[:, p:p + 1])
                act.drain()
                rstd(act, rs[:, p:p + 1], ss[:, p:p + 1], D, e.eps_rms).then_inc(S.r_ready, 1)

            def body(i, p, last):
                t = 2 * i + p
                if not last:
                    rms(1 - p, 16 * i + 16 * (p + 1))
                act.wait_ge(S.qk_psum, done(t - 2))
                act.wait_ge(S.z_done, done(t - 2))
                for n in range(3):
                    act.wait_ge(S.proj_psum, done(t, 3, n))
                    act.activation(Y[p][:, 512 * n:512 * n + 512], PP[n], ACT.Copy).then_inc(S.y_ready, 1)
                act.drain()
                act.wait_ge(S.qss_ready, done(t))
                rstd(act, qr, qss, HD, e.eps_rms).then_inc(S.qr_ready, 1)
                act.wait_ge(S.z_done, done(t - 1))
                act.activation(ZT, Y[p][:, 3 * GW:4 * GW], ACT.Exp, scale=-1.0).then_inc(S.z_exp, 1)
                act.activation(cut(V, t), Y[p][:, 2 * GW:3 * GW], ACT.Copy)
                act.drain()

            act.preload_act_table_set(LN_EXP)
            prime(act, S.r_ready, (S.y_ready, 3), S.qr_ready, S.z_exp)
            act.wait_ge(S.row_ld, 16)
            rms(0, 16)
            with act.Fori(0, half - 1) as i:
                body(i, 0, False)
                body(i, 1, False)
            body(half - 1, 0, False)
            body(half - 1, 1, True)

        @block.tensor
        def _(pe):
            def transposes(p, t):
                pe.wait_ge(S.h_ready, done(t))
                pe.wait_ge(S.hT_ready, done(t - 1))
                for k in range(KD):
                    ins = pe.transpose(PH[:, k * P:(k + 1) * P], H[p][:, k * P:(k + 1) * P], e.ident)
                ins.then_inc(S.T_psum, 1)

            def body(i, p, last):
                t = 2 * i + p
                pe.wait_ge(S.hT_ready, done(t))
                for n in range(3):
                    pe.wait_ge(S.y_ready, done(t - 1, 3, n))
                    for k in range(KD):
                        ins = pe.matmul(PP[n], HC[p][:, k, :], W[:, k, 512 * n:512 * n + 512], start=k == 0, stop=k == KD - 1)
                    ins.then_inc(S.proj_psum, 1)
                pe.wait_ge(S.dt_done, done(t - 1))
                for k in range(KD):
                    ins = pe.matmul(PDT, HC[p][:, k, :], W[:, k, 4 * GW:TOK_COLS], start=k == 0, stop=k == KD - 1)
                ins.then_inc(S.dt_psum, 1)
                if not last:
                    transposes(1 - p, t + 1)
                pe.wait_ge(S.qn_ready, done(t))
                pe.wait_ge(S.qk_done, done(t - 1))
                for k in range(2 * GT):
                    ins = pe.transpose(PQK[:, k * P:(k + 1) * P], Y[p][:, k * P:(k + 1) * P], e.ident)
                ins.then_inc(S.qk_psum, 1)

            prime(pe, S.T_psum, (S.proj_psum, 3), S.dt_psum, S.qk_psum)
            pe.wait_ge(S.const_ld, 16)
            transposes(0, 0)
            pe.wait_ge(S.w_ld, 16)
            with pe.Fori(0, half - 1) as i:
                body(i, 0, False)
                body(i, 1, False)
            body(half - 1, 0, False)
            body(half - 1, 1, True)

        @block.vector
        def _(v):
            def scale_h(p, t):
                v.wait_ge(S.r_ready, done(t))
                v.wait_ge(S.T_psum, done(t - 2))
                v.tensor_scalar(H[p], X[p], rs[:, p:p + 1], None, ALU.mult).then_inc(S.h_ready, 1)

            def evac_h(p, t):
                v.wait_ge(S.T_psum, done(t))
                v.wait_ge(S.ht_copied, done(t - 2))
                v.wait_ge(S.dt_psum, done(t - 2))
                v.tensor_tensor(HC[p], PH.rearrange("p (k n) -> p k n", n=P),
                                bc(e.pcol("g_mix", KD).unsqueeze(2), [P, KD, P]), ALU.mult).then_inc(S.hT_ready, 1)

            def body(i, p, last):
                t = 2 * i + p
                if not last:
                    scale_h(1 - p, t + 1)
                v.wait_ge(S.y_ready, done(t, 3, 1))
                v.tensor_tensor(SQ, Y[p][:, 0:2 * GW], Y[p][:, 0:2 * GW], ALU.mult)
                v.drain()
                v.tensor_reduce(qss, SQ.rearrange("p (h n) -> p h n", n=HD), AX, ALU.add).then_inc(S.qss_ready, 1)
                v.wait_ge(S.qr_ready, done(t))
                newton(v, qr, qss, qt, HD)
                yq = Y[p][:, 0:2 * GW].rearrange("p (h n) -> p h n", n=HD)
                v.tensor_tensor(yq, yq, bc(qr.unsqueeze(2), [P, 12, HD]), ALU.mult).then_inc(S.qn_ready, 1)
                if not last:
                    evac_h(1 - p, t + 1)
                v.wait_ge(S.dt_psum, done(t))
                v.tensor_tensor(cut(DT, t), PDT, e.rowp("dt_b", HEADS), ALU.add).then_inc(S.dt_done, 1)
                v.wait_ge(S.z_exp, done(t))
                v.tensor_scalar(ZT, ZT, 1.0, None, ALU.add)
                v.drain()
                v.reciprocal(ZT, ZT)
                v.drain()
                v.tensor_tensor(cut(Z, t), Y[p][:, 3 * GW:4 * GW], ZT, ALU.mult).then_inc(S.z_done, 1)
                v.wait_ge(S.qk_psum, done(t))
                for n, (T, g) in enumerate(((QT, "att_q"), (KT, "att_k"))):
                    ins = v.tensor_scalar(T[:, :, ds(t * P, P)], PQK[:, n * GW:(n + 1) * GW].rearrange("p (k n) -> p k n", n=P),
                                          e.pcol(g, 1), None, ALU.mult)
                ins.then_inc(S.qk_done, 1)
                v.drain()

            prime(v, S.h_ready, S.hT_ready, S.qss_ready, S.qn_ready, S.z_done, S.qk_done, S.dt_done)
            v.wait_ge(S.par_ld, 16)
            v.wait_ge(S.row_ld, 16)
            v.tensor_scalar(e.pcol("att_q", 1), e.pcol("att_q", 1), HD ** -0.5, None, ALU.mult)
            v.tensor_scalar(e.pcol("ca_q", 2), e.pcol("ca_q", 2), CA_D ** -0.5, None, ALU.mult)
            v.drain()
            scale_h(0, 0)
            evac_h(0, 0)
            with v.Fori(0, half - 1) as i:
                body(i, 0, False)
                body(i, 1, False)
            body(half - 1, 0, False)
            body(half - 1, 1, True)


def phase_features(nc, e):
    A = e.A
    HT = A(AT_HT, KD, SEQ)
    at = AT_B
    UP = A(at, GT, SEQ + 32); at += GT * (SEQ + 32)
    U2 = A(e.at_U2, GT, SEQ); YSC = A(e.at_YSC, GT, SEQ); XBC = A(e.at_XBC, XBC_T, SEQ)
    at = e.at_XBC + XBC_T * SEQ
    W = [A(at + D * j, KD, P) for j in range(3)]; at += 3 * D
    EG = A(at, SEQ); at += SEQ
    AS = A(at, SEQ); at += SEQ
    SP_ = A(at, SEQ + 4); at += SEQ + 4
    XR = [A(at + (SEQ + 4) * p, SEQ + 4) for p in (0, 1)]; at += 2 * (SEQ + 4)
    AC = [A(at + SEQ * p, SEQ) for p in (0, 1)]; at += 2 * SEQ
    assert at <= ARENA, at
    SCC, SCH, SCT = EG, AS, AC[0]
    CFP, SCP, SSP = CF_K - 1, SC_K - 1, SSD_K - 1
    S = e.sems("feat", "w_ld0 w_ld1 w_ld2 pads f_psum f_evac u_ready sc_done acc_ready acc_exp silu_done")
    w_ld = [S.w_ld0, S.w_ld1, S.w_ld2]

    with nc.Block() as block:
        @block.sync
        def _(sp):
            def load(n, j):
                sp.wait_ge(S.f_psum, n + 1)
                sp.dma_start(W[j].rearrange("p k n -> p (k n)"), e.d.w_feat[ds(n, 1)].rearrange("o p n -> p (o n)")).then_inc(w_ld[j], 16)

            with sp.Fori(0, GT) as c:
                for j in range(2):
                    load(2 * c + j, j)
            with sp.Fori(0, GT) as c:
                for j in range(3):
                    load(2 * GT + 3 * c + j, j)
            with sp.Fori(0, XBC_T // 2) as i:
                for j in range(2):
                    load(5 * GT + 2 * i + j, j)
            load(NFEAT - 1, 0)

        @block.gpsimd
        def _(g):
            g.memset(UP[:, :, 0:CFP], 0.0)
            g.memset(SP_[:, 0:SCP], 0.0)
            for p in (0, 1):
                ins = g.memset(XR[p][:, 0:SSP], 0.0)
            g.drain()
            g.sem_inc(S.pads, 1)

        @block.tensor
        def _(pe):
            def tile(n, j, loads):
                pe.wait_ge(w_ld[j], loads)
                pe.wait_ge(S.f_evac, n + 1)
                for h in range(2):
                    for k in range(KD):
                        ins = pe.matmul(e.PS[:, 2 * j + h, :], W[j][:, k, :], HT[:, k, 512 * h:512 * h + 512], start=k == 0, stop=k == KD - 1)
                ins.then_inc(S.f_psum, 1)

            prime(pe, S.f_psum)
            with pe.Fori(0, GT) as c:
                for j in range(2):
                    tile(2 * c + j, j, 16 * c + 16)
            with pe.Fori(0, GT) as c:
                for j in range(3):
                    tile(2 * GT + 3 * c + j, j, 16 * c + 16 * (GT + 1 if j < 2 else 1))
            with pe.Fori(0, XBC_T // 2) as i:
                for j in range(2):
                    tile(5 * GT + 2 * i + j, j, 16 * i + 16 * (2 * GT + 1))
            tile(NFEAT - 1, 0, 16 * (2 * GT + 1 + XBC_T // 2))

        @block.scalar
        def _(act):
            def evac(n, j, out, func=ACT.Copy, scale=1.0):
                act.wait_ge(S.f_psum, n + 3)
                act.activation(out, e.pair(j), func, scale=scale).then_inc(S.f_evac, 1)

            prime(act, S.f_evac, S.acc_exp)
            with act.Fori(0, GT) as c:
                act.wait_ge(S.u_ready, done(c - 1))
                evac(2 * c, 0, AS)
                evac(2 * c + 1, 1, EG, ACT.Exp, -1.0)
            with act.Fori(0, GT) as c:
                act.wait_ge(S.u_ready, GT + 2)
                act.wait_ge(S.sc_done, done(c - 1))
                evac(2 * GT + 3 * c, 0, cut(YSC, c))
                evac(2 * GT + 3 * c + 1, 1, SCC)
                evac(2 * GT + 3 * c + 2, 2, SCH)
            act.drain()

            def xbc(m, i, j):
                act.wait_ge(S.acc_ready, done(m - 2))
                act.wait_ge(S.sc_done, GT + 2)
                evac(5 * GT + m, j, XR[j][:, SSP:SSP + SEQ])
                act.wait_ge(S.acc_ready, done(m))
                act.wait_ge(S.silu_done, done(m - 2))
                act.activation((EG, AS)[j], AC[j], ACT.Exp, scale=-1.0).then_inc(S.acc_exp, 1)
                act.drain()

            with act.Fori(0, XBC_T // 2) as i:
                for j in range(2):
                    xbc(2 * i + j, i, j)
            xbc(XBC_T - 1, XBC_T // 2, 0)

        @block.vector
        def _(v):
            def taps(out, src, w, K):
                for k in range(1, K):
                    v.drain()
                    ins = v.scalar_tensor_tensor(out, src(k), w(k), out, ALU.mult, ALU.add)
                return ins

            def col(name, at):
                o = PC[name]
                return e.par[:, ds(o + at, 1)] if not isinstance(at, int) else e.par[:, o + at:o + at + 1]

            prime(v, S.u_ready, S.sc_done, S.acc_ready, S.silu_done)
            v.wait_ge(S.pads, 1)
            with v.Fori(0, GT) as c:
                v.wait_ge(S.f_evac, 2 * c + 4)
                v.tensor_scalar(EG, EG, 1.0, None, ALU.add)
                v.drain()
                v.reciprocal(EG, EG)
                v.drain()
                v.tensor_tensor(UP[:, ds(c, 1), CFP:CFP + SEQ].rearrange("p o n -> p (o n)"), AS, EG, ALU.mult).then_inc(S.u_ready, 1)
                v.drain()
            with v.Fori(0, GT) as c:
                v.wait_ge(S.f_evac, 2 * GT + 3 * c + 5)
                v.tensor_tensor(SP_[:, SCP:SCP + SEQ], SCC, SCH, ALU.mult)
                v.drain()
                v.tensor_scalar(SCT, SP_[:, 0:SEQ], col("sc_w", c * SC_K), None, ALU.mult)
                taps(SCT, lambda k: SP_[:, k:k + SEQ], lambda k: col("sc_w", c * SC_K + k), SC_K)
                v.drain()
                v.tensor_tensor(cut(YSC, c), cut(YSC, c), SCT, ALU.mult).then_inc(S.sc_done, 1)
                v.drain()
                u = lambda k: UP[:, ds(c, 1), k:k + SEQ].rearrange("p o n -> p (o n)")
                v.tensor_scalar(cut(U2, c), u(0), col("cf_w", c * CF_K), col("cf_b", c), ALU.mult, ALU.add)
                taps(cut(U2, c), u, lambda k: col("cf_w", c * CF_K + k), CF_K)
                v.drain()

            def xbc(m, j):
                v.wait_ge(S.f_evac, 5 * GT + m + 3)
                v.tensor_scalar(AC[j], XR[j][:, 0:SEQ], col("ssd_w", m * SSD_K), col("ssd_b", m), ALU.mult, ALU.add)
                taps(AC[j], lambda k: XR[j][:, k:k + SEQ], lambda k: col("ssd_w", m * SSD_K + k), SSD_K).then_inc(S.acc_ready, 1)
                v.wait_ge(S.acc_exp, done(m))
                E = (EG, AS)[j]
                v.tensor_scalar(E, E, 1.0, None, ALU.add)
                v.drain()
                v.reciprocal(E, E)
                v.drain()
                v.tensor_tensor(cut(XBC, m) if not isinstance(m, int) else XBC[:, m, :], AC[j], E, ALU.mult).then_inc(S.silu_done, 1)
                v.drain()

            with v.Fori(0, XBC_T // 2) as i:
                for j in range(2):
                    xbc(2 * i + j, j)
            xbc(XBC_T - 1, 0)


def phase_ssd(nc, e):
    A = e.A
    XBC = A(e.at_XBC, XBC_T, SEQ)
    Z, DT = A(AT_Z, NT, GW), A(AT_DT, NT, HEADS)
    Y_T = A(e.at_CAT_SSD, GT, SEQ)
    at = e.at_XBC + XBC_T * SEQ
    XC = [A(at + 896 * p, XBC_T, P) for p in (0, 1)]; at += 1792
    XB = A(at, 640); at += 640
    RD = A(at, HEADS, P); at += 768
    EX = A(at, HEADS, P); at += 768
    MT = A(at, HEADS, P); at += 768
    CB = A(at, SSD_NG, P); at += 256
    XDT = A(at, HEADS, HD); at += GW
    XDD = A(at, HEADS, HD); at += GW
    Y = A(at, HEADS, HD); at += GW
    T2 = A(at, HEADS, HD); at += GW
    YN = A(at, GW); at += GW
    ST = A(at, HEADS, HD); at += GW
    TS = A(at, NT, HEADS); at += 48
    DA = A(at, NT, HEADS); at += 48
    AN = A(at, HEADS); at += 8
    CS = A(at, 3, HEADS); at += 24
    ssy, ry = A(at, 1), A(at + 1, 1); at += 2
    assert at <= ARENA
    S = e.sems("ssd", "dt_abs dt_exp dt_one dt_ln a_exp da_ready xc_ready tr_psum xb_ready rd_ready cb_psum cb_read d_psum d_exp "
               "cs_exp mt_ready xdt_ready xdd_ready y_psum yo_psum st_psum y_read st_ready ss_ready r_ready yn_ready yT_psum yT_done")
    PTR = e.PS[:, 0:2, :].rearrange("p a b -> p (a b)")[:, 0:640]
    PYT = e.PS[:, 1, P:P + GW]
    PCB = e.PS[:, 2, 0:SSD_NG * P]
    PCS = e.PS[:, 7, GW:GW + 3 * HEADS]
    PDD = e.PS[:, 3:5, 0:GW]
    PY, PYO, PST = e.PS[:, 5, 0:GW], e.PS[:, 6, 0:GW], e.PS[:, 7, 0:GW]
    JG = HEADS // SSD_NG
    JW = JG * HD

    with nc.Block() as block:
        @block.sync
        def _(sp):
            pass

        @block.gpsimd
        def _(g):
            prime(g, S.xc_ready)
            with g.Fori(0, NT // 2) as i:
                for p in (0, 1):
                    c = 2 * i + p
                    g.wait_ge(S.st_psum, done(c - 2))
                    g.tensor_copy(XC[p], XBC[:, :, ds(c * P, P)]).then_inc(S.xc_ready, 1)

        @block.scalar
        def _(act):
            act.wait_ge(S.dt_abs, 1)
            act.activation(TS, TS, ACT.Exp, scale=-1.0).then_inc(S.dt_exp, 1)
            act.activation(AN, e.rowp("a_log", HEADS), ACT.Exp).then_inc(S.a_exp, 1)
            act.wait_ge(S.dt_one, 1)
            act.activation(TS, TS, ACT.Ln).then_inc(S.dt_ln, 1)
            prime(act, S.xb_ready, S.d_exp, S.cs_exp, S.r_ready)
            with act.Fori(0, NT) as c:
                act.wait_ge(S.tr_psum, done(c))
                act.wait_ge(S.y_read, done(c - 1))
                act.wait_ge(S.st_psum, done(c - 1))
                act.activation(XB, PTR, ACT.Copy).then_inc(S.xb_ready, 1)
                act.wait_ge(S.cb_psum, done(c))
                act.activation(CS.rearrange("p a h -> p (a h)"), PCS, ACT.Exp).then_inc(S.cs_exp, 1)
                act.wait_ge(S.d_psum, done(c))
                act.wait_ge(S.mt_ready, done(c - 1))
                act.activation(EX.rearrange("p (a h) n -> p a (h n)", a=2), PDD, ACT.Exp).then_inc(S.d_exp, 1)
                act.wait_ge(S.ss_ready, done(c))
                rstd(act, ry, ssy, GW, e.eps_rms).then_inc(S.r_ready, 1)

        @block.tensor
        def _(pe):
            prime(pe, S.tr_psum, S.cb_psum, S.d_psum, S.y_psum, S.yo_psum, S.st_psum, S.yT_psum)
            with pe.Fori(0, NT // 2) as i:
                for p in (0, 1):
                    c = 2 * i + p
                    pe.wait_ge(S.xc_ready, done(c))
                    pe.wait_ge(S.xb_ready, done(c - 1))
                    pe.wait_ge(S.yT_done, done(c - 1))
                    for k in range(5):
                        ins = pe.transpose(PTR[:, k * P:(k + 1) * P], XC[p][:, k, :], e.ident)
                    ins.then_inc(S.tr_psum, 1)
                    pe.wait_ge(S.cb_read, done(c - 1))
                    pe.wait_ge(S.st_ready, done(c - 1))
                    for g in range(SSD_NG):
                        pe.matmul(PCB[:, g * P:(g + 1) * P], XC[p][:, 3 + g, :], XC[p][:, 5 + g, :], start=True, stop=True)
                    for n, m in enumerate((e.tri_le, e.tri_gt, e.ones)):
                        ins = pe.matmul(PCS[:, n * HEADS:(n + 1) * HEADS], m, cut(DA, c), start=True, stop=True)
                    ins.then_inc(S.cb_psum, 1)
                    pe.wait_ge(S.rd_ready, done(c))
                    pe.wait_ge(S.d_exp, done(c - 1))
                    for n in range(2):
                        ins = pe.matmul(PDD[:, n, :], e.tri_gt, RD[:, 3 * n:3 * n + 3, :].rearrange("p h n -> p (h n)"), start=True, stop=True)
                    ins.then_inc(S.d_psum, 1)
                    pe.wait_ge(S.y_read, done(c - 1))
                    for g in range(SSD_NG):
                        ins = pe.matmul(PYO[:, g * JW:(g + 1) * JW], XC[p][:, 5 + g, :], ST[:, g * JG:(g + 1) * JG, :].rearrange("p h n -> p (h n)"), start=True, stop=True)
                    ins.then_inc(S.yo_psum, 1)
                    pe.wait_ge(S.mt_ready, done(c))
                    pe.wait_ge(S.xdt_ready, done(c))
                    for h in range(HEADS):
                        ins = pe.matmul(PY[:, h * HD:(h + 1) * HD], MT[:, h, :], XDT[:, h, :], start=True, stop=True)
                    ins.then_inc(S.y_psum, 1)
                    pe.wait_ge(S.xdd_ready, done(c))
                    for g in range(SSD_NG):
                        ins = pe.matmul(PST[:, g * JW:(g + 1) * JW], XB[:, GW + g * P:GW + (g + 1) * P], XDD[:, g * JG:(g + 1) * JG, :].rearrange("p h n -> p (h n)"), start=True, stop=True)
                    ins.then_inc(S.st_psum, 1)
                    pe.wait_ge(S.yn_ready, done(c))
                    for k in range(GT):
                        ins = pe.transpose(PYT[:, k * P:(k + 1) * P], YN[:, k * P:(k + 1) * P], e.ident)
                    ins.then_inc(S.yT_psum, 1)

        @block.vector
        def _(v):
            v.tensor_scalar(TS, DT, -1.0, None, ALU.mult)
            v.drain()
            v.tensor_tensor(TS, TS, DT, ALU.max).then_inc(S.dt_abs, 1)
            v.wait_ge(S.dt_exp, 1)
            v.tensor_scalar(TS, TS, 1.0, None, ALU.add).then_inc(S.dt_one, 1)
            v.wait_ge(S.dt_ln, 1)
            v.tensor_scalar(DT, DT, 0.0, None, ALU.max)
            v.drain()
            v.tensor_tensor(DT, DT, TS, ALU.add)
            v.wait_ge(S.a_exp, 1)
            v.tensor_scalar(AN, AN, -1.0, None, ALU.mult)
            v.memset(ST, 0.0)
            v.drain()
            v.tensor_tensor(DA, DT, bc(AN.unsqueeze(1), [P, NT, HEADS]), ALU.mult)
            v.drain()
            prime(v, S.rd_ready, S.cb_read, S.mt_ready, S.xdt_ready, S.xdd_ready, S.y_read, S.st_ready, S.ss_ready, S.yn_ready, S.yT_done)
            per_head = lambda ap, n: bc(ap.unsqueeze(2), [P, HEADS, n])
            with v.Fori(0, NT) as c:
                v.tensor_tensor(RD, bc(e.tri_le.unsqueeze(1), [P, HEADS, P]), per_head(cut(DA, c), P), ALU.mult).then_inc(S.rd_ready, 1)
                v.wait_ge(S.cb_psum, done(c))
                v.tensor_tensor(CB, PCB.rearrange("p (g n) -> p g n", n=P), bc(e.tri_le.unsqueeze(1), [P, SSD_NG, P]), ALU.mult).then_inc(S.cb_read, 1)
                xs = XB[:, 0:GW].rearrange("p (h n) -> p h n", n=HD)
                v.wait_ge(S.xb_ready, done(c))
                v.wait_ge(S.y_psum, done(c - 1))
                v.tensor_tensor(XDT, xs, per_head(cut(DT, c), HD), ALU.mult).then_inc(S.xdt_ready, 1)
                v.drain()
                v.wait_ge(S.d_exp, done(c))
                for g in range(SSD_NG):
                    ins = v.tensor_tensor(MT[:, g * JG:(g + 1) * JG, :], EX[:, g * JG:(g + 1) * JG, :], bc(CB[:, g:g + 1, :], [P, JG, P]), ALU.mult)
                ins.then_inc(S.mt_ready, 1)
                v.wait_ge(S.cs_exp, done(c))
                v.wait_ge(S.st_psum, done(c - 1))
                v.tensor_tensor(XDD, XDT, per_head(CS[:, 1, :], HD), ALU.mult).then_inc(S.xdd_ready, 1)
                v.wait_ge(S.yo_psum, done(c))
                v.tensor_tensor(Y, PYO.rearrange("p (h n) -> p h n", n=HD), per_head(CS[:, 0, :], HD), ALU.mult)
                v.tensor_tensor(T2, xs, per_head(e.rowp("ssd_d", HEADS), HD), ALU.mult)
                v.drain()
                v.wait_ge(S.y_psum, done(c))
                v.tensor_tensor(Y, Y, PY.rearrange("p (h n) -> p h n", n=HD), ALU.add)
                v.drain()
                v.tensor_tensor(Y, Y, T2, ALU.add).then_inc(S.y_read, 1)
                v.tensor_tensor(ST, ST, per_head(CS[:, 2, :], HD), ALU.mult)
                v.drain()
                v.wait_ge(S.st_psum, done(c))
                v.tensor_tensor(ST, ST, PST.rearrange("p (h n) -> p h n", n=HD), ALU.add).then_inc(S.st_ready, 1)
                y = Y.rearrange("p h n -> p (h n)")
                v.tensor_tensor(y, y, cut(Z, c), ALU.mult)
                v.drain()
                v.wait_ge(S.yT_psum, done(c - 1))
                v.tensor_tensor_reduce(YN, y, y, 1.0, 0.0, ALU.mult, ALU.add, ssy).then_inc(S.ss_ready, 1)
                v.drain()
                v.wait_ge(S.r_ready, done(c))
                v.tensor_scalar(YN, y, ry, None, ALU.mult).then_inc(S.yn_ready, 1)
                v.wait_ge(S.yT_psum, done(c))
                v.tensor_tensor(Y_T[:, :, ds(c * P, P)], PYT.rearrange("p (k n) -> p k n", n=P), bc(e.pcol("ssd_g", GT).unsqueeze(2), [P, GT, P]), ALU.mult).then_inc(S.yT_done, 1)
                v.drain()


def phase_attention(nc, e):
    A = e.A
    QT, KT, V = A(AT_QT, GT, SEQ), A(AT_KT, GT, SEQ), A(AT_V, NT, GW)
    at = e.at_XBC
    ATT = A(at, NT, GW); at += NT * GW
    QP = A(at, SEQ); at += SEQ
    KP = A(at, SEQ); at += SEQ
    VP = A(at, NT, P); at += SEQ
    SM = [A(at + SEQ * p, SEQ) for p in (0, 1)]; at += 2 * SEQ
    PR = [A(at + SEQ * p, SEQ) for p in (0, 1)]; at += 2 * SEQ
    PT = [A(at + SEQ * p, SEQ) for p in (0, 1)]; at += 2 * SEQ
    mx = A(at, 2); den = A(at + 2, 4); rden = A(at + 6, 2); at += 8
    assert at <= ARENA
    S = e.sems("att", "settled qkv_ready s_psum m_ready p_ready t_psum pt_ready o_psum o_read")
    PSS = [e.pair(0), e.pair(1)]
    PTT = e.pair(2)
    PO = [e.PS[:, 6, 0:HD], e.PS[:, 7, 0:HD]]
    NS = 2 * NT
    e.ATT = ATT

    with nc.Block() as block:
        @block.sync
        def _(sp):
            pass

        @block.gpsimd
        def _(g):
            with g.Fori(0, HEADS // 2) as j:
                g.wait_ge(S.o_psum, NS * j + 2)
                g.tensor_copy(QP, cut(QT, j))
                g.tensor_copy(KP, cut(KT, j))
                g.tensor_copy(VP, V[:, :, ds(j * P, P)])
                g.drain()
                g.sem_inc(S.qkv_ready, 1)

        @block.tensor
        def _(pe):
            def scores(j, s):
                h, i, p = s // NT, s % NT, s % 2
                g = NS * j + s
                pe.wait_ge(S.m_ready, done(g - 2))
                rows = slice(h * HD, (h + 1) * HD)
                n = (i + 1) * P
                for a in range(0, n, 512):
                    b = min(n, a + 512)
                    ins = pe.matmul(PSS[p][:, a:b], QP[rows, i * P:(i + 1) * P], KP[rows, a:b], start=True, stop=True)
                ins.then_inc(S.s_psum, 1)

            def transposes(j, s):
                i, p = s % NT, s % 2
                g = NS * j + s
                pe.wait_ge(S.p_ready, done(g))
                pe.wait_ge(S.pt_ready, done(g - 1))
                for k in range(i + 1):
                    ins = pe.transpose(PTT[:, k * P:(k + 1) * P], PR[p][:, k * P:(k + 1) * P], e.ident)
                ins.then_inc(S.t_psum, 1)

            def values(j, s):
                h, i, p = s // NT, s % NT, s % 2
                g = NS * j + s
                pe.wait_ge(S.pt_ready, done(g))
                pe.wait_ge(S.o_read, g + 3)
                for k in range(i + 1):
                    ins = pe.matmul(PO[p], PT[p][:, k * P:(k + 1) * P], VP[:, k, h * HD:(h + 1) * HD], start=k == 0, stop=k == i)
                ins.then_inc(S.o_psum, 1)

            prime(pe, S.s_psum, S.t_psum, S.o_psum)
            with pe.Fori(0, HEADS // 2) as j:
                pe.wait_ge(S.qkv_ready, j + 1)
                for s in range(NS + 2):
                    if s < NS:
                        scores(j, s)
                    if 0 <= s - 1 < NS:
                        transposes(j, s - 1)
                    if s >= 2:
                        values(j, s - 2)

        @block.vector
        def _(v):
            def maximum(j, s):
                i, p = s % NT, s % 2
                g = NS * j + s
                n = (i + 1) * P
                v.wait_ge(S.s_psum, done(g))
                v.wait_ge(S.p_ready, done(g - 2))
                v.sem_inc(S.settled, 1)
                v.tensor_tensor_reduce(SM[p][:, 0:n], PSS[p][:, 0:n], e.mask[:, SEQ - n:SEQ], 1.0, -BIG, ALU.add, ALU.max, mx[:, p:p + 1])
                v.drain()
                v.tensor_scalar(mx[:, p:p + 1], mx[:, p:p + 1], -1.0, None, ALU.mult).then_inc(S.m_ready, 1)

            def output(j, s):
                h, i, p = s // NT, s % NT, s % 2
                g = NS * j + s
                v.wait_ge(S.o_psum, done(g))
                v.reciprocal(rden[:, p:p + 1], den[:, s % 4:s % 4 + 1])
                v.drain()
                v.tensor_scalar(ATT[:, i, ds(j * P + h * HD, HD)], PO[p], rden[:, p:p + 1], None, ALU.mult).then_inc(S.o_read, 1)

            prime(v, S.m_ready)
            v.sem_inc(S.o_read, 4)
            with v.Fori(0, HEADS // 2) as j:
                for s in range(NS + 3):
                    if s < NS:
                        maximum(j, s)
                    if s >= 3:
                        output(j, s - 3)
                v.drain()

        @block.scalar
        def _(act):
            def probs(j, s):
                i, p = s % NT, s % 2
                g = NS * j + s
                n = (i + 1) * P
                act.wait_ge(S.m_ready, done(g))
                act.wait_ge(S.t_psum, done(g - 2))
                act.wait_ge(S.o_read, g + 1)
                act.activation(PR[p][:, 0:n], SM[p][:, 0:n], ACT.Exp, bias=mx[:, p:p + 1],
                               accum_out=den[:, s % 4:s % 4 + 1]).then_inc(S.p_ready, 1)

            def copy_out(j, s):
                i, p = s % NT, s % 2
                g = NS * j + s
                n = (i + 1) * P
                act.wait_ge(S.t_psum, done(g))
                act.wait_ge(S.o_psum, done(g - 2))
                act.activation(PT[p][:, 0:n], PTT[:, 0:n], ACT.Copy).then_inc(S.pt_ready, 1)

            prime(act, S.p_ready, S.pt_ready)
            with act.Fori(0, HEADS // 2) as j:
                for s in range(NS + 1):
                    if s < NS:
                        probs(j, s)
                    if s >= 1:
                        copy_out(j, s - 1)


def phase_norm_cf(nc, e):
    A = e.A
    U2 = A(e.at_U2, GT, SEQ)
    CF = A(e.at_CAT_CF, GT, SEQ)
    AT_T = A(e.at_CAT_ATT, GT, SEQ)
    ATT = e.ATT
    at = e.at_XBC + NT * GW
    XC = A(at, GT, SEQ); at += GT * SEQ
    SQ = A(at, GT, SEQ); at += GT * SEQ
    R = A(at, SEQ); at += SEQ
    G = A(at, GT, SEQ); at += GT * SEQ
    assert at <= ARENA
    S = e.sems("cf", "mu_psum xc_ready sq_ready var_psum r_ready n_ready e_ready at_psum at_done")
    with nc.Block() as block:
        @block.sync
        def _(sp):
            pass

        @block.gpsimd
        def _(g):
            pass

        @block.tensor
        def _(pe):
            for h in range(2):
                for k in range(GT):
                    ins = pe.matmul(e.PS[:, h, :], e.ones, U2[:, k, 512 * h:512 * h + 512], start=k == 0, stop=k == GT - 1)
            ins.then_inc(S.mu_psum, 1)
            for t in range(NT):
                q = 4 + t % 4
                if t >= 4:
                    pe.wait_ge(S.at_done, t - 3)
                for k in range(GT):
                    ins = pe.transpose(e.PS[:, q, k * P:(k + 1) * P], ATT[:, t, k * P:(k + 1) * P], e.ident)
                ins.then_inc(S.at_psum, 1)
            pe.wait_ge(S.sq_ready, 1)
            for h in range(2):
                for k in range(GT):
                    ins = pe.matmul(e.PS[:, 2 + h, :], e.ones, SQ[:, k, 512 * h:512 * h + 512], start=k == 0, stop=k == GT - 1)
            ins.then_inc(S.var_psum, 1)

        @block.vector
        def _(v):
            v.wait_ge(S.mu_psum, 1)
            for k in range(GT):
                v.scalar_tensor_tensor(XC[:, k, :], e.pair(0), -1.0 / GW, U2[:, k, :], ALU.mult, ALU.add)
            v.drain()
            v.tensor_tensor(SQ, XC, XC, ALU.mult).then_inc(S.sq_ready, 1)
            v.wait_ge(S.r_ready, 1)
            v.tensor_tensor(XC, XC, bc(R.unsqueeze(1), [P, GT, SEQ]), ALU.mult)
            v.drain()
            for k in range(GT):
                ins = v.tensor_scalar(XC[:, k, :], XC[:, k, :], e.pcol("ln_g", GT)[:, k:k + 1], e.pcol("ln_b", GT)[:, k:k + 1], ALU.mult, ALU.add)
            ins.then_inc(S.n_ready, 1)
            v.wait_ge(S.e_ready, 1)
            v.tensor_scalar(G, G, 1.0, None, ALU.add)
            v.drain()
            v.reciprocal(G, G)
            v.drain()
            v.tensor_tensor(CF, XC, G, ALU.mult)

        @block.scalar
        def _(act):
            for t in range(NT):
                act.wait_ge(S.at_psum, t + 1)
                act.activation(AT_T[:, :, t * P:(t + 1) * P], e.PS[:, 4 + t % 4, 0:GW].rearrange("p (k n) -> p k n", n=P), ACT.Copy).then_inc(S.at_done, 1)
            act.wait_ge(S.var_psum, 1)
            rstd(act, R, e.pair(1), GW, e.eps_ln).then_inc(S.r_ready, 1)
            act.wait_ge(S.n_ready, 1)
            act.activation(G, XC, ACT.Exp, scale=-1.0).then_inc(S.e_ready, 1)


def phase_out(nc, e):
    A = e.A
    X1 = A(e.at_X1, NT, D)
    CAT = e.CAT
    NC = len(CAT) * GT
    at = e.at_XBC + NT * GW
    W = A(at, NC, D); at += NC * D
    assert at <= ARENA, at
    XI = [A(e.at_work_out + D * p, D) for p in (0, 1)]
    CC = [A(e.at_work_out + 2 * D + NC * P * p, NC, P) for p in (0, 1)]
    S = e.sems("out", "w_ld x_ld0 x_ld1 cc_ready o_psum x1_ready")
    x_ld = [S.x_ld0, S.x_ld1]
    with nc.Block() as block:
        @block.sync
        def _(sp):
            for p in (0, 1):
                sp.dma_start(XI[p], e.d.x[p * P:(p + 1) * P, :]).then_inc(x_ld[p], 16)
            sp.dma_start(W, e.d.w_out.rearrange("(k p) n -> p k n", p=P)).then_inc(S.w_ld, 16)
            with sp.Fori(1, NT // 2) as i:
                for p in (0, 1):
                    t = 2 * i + p
                    sp.wait_ge(S.x1_ready, done(t - 2))
                    sp.dma_start(XI[p], e.d.x[ds(t * P, P), :]).then_inc(x_ld[p], 16)

        @block.gpsimd
        def _(g):
            prime(g, (S.cc_ready, len(CAT)))
            with g.Fori(0, NT // 2) as i:
                for p in (0, 1):
                    t = 2 * i + p
                    g.wait_ge(S.o_psum, done(t - 2))
                    for n, c in enumerate(CAT):
                        g.tensor_copy(CC[p][:, n * GT:(n + 1) * GT, :], c[:, :, ds(t * P, P)]).then_inc(S.cc_ready, 1)

        @block.scalar
        def _(act):
            pass

        @block.tensor
        def _(pe):
            prime(pe, S.o_psum)
            pe.wait_ge(S.w_ld, 16)
            with pe.Fori(0, NT // 2) as i:
                for p in (0, 1):
                    t = 2 * i + p
                    pe.wait_ge(S.cc_ready, done(t, len(CAT)))
                    pe.wait_ge(S.x1_ready, done(t - 2))
                    for h in range(2):
                        for k in range(NC):
                            ins = pe.matmul(e.PS[:, 2 * p + h, :], CC[p][:, k, :], W[:, k, 512 * h:512 * h + 512], start=k == 0, stop=k == NC - 1)
                    ins.then_inc(S.o_psum, 1)

        @block.vector
        def _(v):
            prime(v, S.x1_ready)
            with v.Fori(0, NT // 2) as i:
                for p in (0, 1):
                    t = 2 * i + p
                    v.wait_ge(S.o_psum, done(t))
                    v.wait_ge(x_ld[p], 16 * i + 16)
                    v.tensor_tensor(cut(X1, t), e.pair(p), XI[p], ALU.add).then_inc(S.x1_ready, 1)


def phase_memory(nc, e):
    A = e.A
    KM, VM = A(e.at_KM, KD, MEM), A(e.at_VM, 2, D)
    at = e.at_ca
    W = [A(at + 4096 * p, KD, 512) for p in (0, 1)]; at += 8192
    X = [A(at + D * p, D) for p in (0, 1)]; at += 2 * D
    H = [A(at + D * p, D) for p in (0, 1)]; at += 2 * D
    MT = A(at, KD, MEM); at += KD * MEM
    K = [A(at + D * p, D) for p in (0, 1)]; at += 2 * D
    SQ = A(at, D); at += D
    ss, rs = A(at, 2), A(at + 2, 2)
    ks, kr, kt = [A(at + 4 + 12 * p, 4) for p in (0, 1)], [A(at + 8 + 12 * p, 4) for p in (0, 1)], A(at + 28, 4)
    assert at + 32 <= ARENA
    S = e.sems("mem", "x_ld w_ld0 w_ld1 r_ready h_ready T_psum mT_ready kv_psum kv_out kss_ready kr_ready kn_ready kT_psum kT_done")
    w_ld = [S.w_ld0, S.w_ld1]
    with nc.Block() as block:
        @block.sync
        def _(sp):
            for p in (0, 1):
                sp.dma_start(X[p], e.d.mem[p * P:(p + 1) * P, :]).then_inc(S.x_ld, 16)
            for n in range(4):
                if n >= 2:
                    sp.wait_ge(S.kv_psum, 2 * (n - 2) + 2)
                sp.dma_start(W[n % 2], e.d.ca_wkv.rearrange("(k p) n -> p k n", p=P)[:, :, 512 * n:512 * n + 512]).then_inc(w_ld[n % 2], 16)

        @block.gpsimd
        def _(g):
            pass

        @block.scalar
        def _(act):
            act.wait_ge(S.x_ld, 32)
            for p in (0, 1):
                act.activation(SQ, X[p], ACT.Square, accum_out=ss[:, p:p + 1])
                act.drain()
            rstd(act, rs, ss, D, e.eps_rms).then_inc(S.r_ready, 1)
            for n in range(4):
                for m in range(2):
                    act.wait_ge(S.kv_psum, 2 * n + m + 1)
                    out = K[m][:, 512 * n:512 * n + 512] if n < 2 else VM[:, m, 512 * (n - 2):512 * (n - 1)]
                    act.activation(out, e.PS[:, 4 + (2 * n + m) % 2, :], ACT.Copy).then_inc(S.kv_out, 1)
            for m in range(2):
                act.wait_ge(S.kss_ready, m + 1)
                rstd(act, kr[m], ks[m], CA_D, e.eps_rms).then_inc(S.kr_ready, 1)

        @block.tensor
        def _(pe):
            for m in range(2):
                pe.wait_ge(S.h_ready, m + 1)
                for k in range(KD):
                    ins = pe.transpose(e.pair(m)[:, k * P:(k + 1) * P], H[m][:, k * P:(k + 1) * P], e.ident)
                ins.then_inc(S.T_psum, 1)
            pe.wait_ge(S.mT_ready, 2)
            for n in range(4):
                pe.wait_ge(w_ld[n % 2], 16 * (n // 2) + 16)
                for m in range(2):
                    if 2 * n + m >= 2:
                        pe.wait_ge(S.kv_out, 2 * n + m - 1)
                    for k in range(KD):
                        ins = pe.matmul(e.PS[:, 4 + (2 * n + m) % 2, :], MT[:, k, m * P:(m + 1) * P], W[n % 2][:, k, :], start=k == 0, stop=k == KD - 1)
                    ins.then_inc(S.kv_psum, 1)
            for m in range(2):
                pe.wait_ge(S.kn_ready, m + 1)
                for k in range(KD):
                    ins = pe.transpose(e.pair(m)[:, k * P:(k + 1) * P], K[m][:, k * P:(k + 1) * P], e.ident)
                ins.then_inc(S.kT_psum, 1)

        @block.vector
        def _(v):
            v.wait_ge(S.r_ready, 1)
            for m in range(2):
                v.tensor_scalar(H[m], X[m], rs[:, m:m + 1], None, ALU.mult).then_inc(S.h_ready, 1)
            for m in range(2):
                v.wait_ge(S.T_psum, m + 1)
                v.tensor_tensor(MT[:, :, m * P:(m + 1) * P], e.pair(m).rearrange("p (k n) -> p k n", n=P),
                                bc(e.pcol("g_mem", KD).unsqueeze(2), [P, KD, P]), ALU.mult).then_inc(S.mT_ready, 1)
            v.wait_ge(S.kv_out, 4)
            for m in range(2):
                v.drain()
                v.tensor_tensor(H[m], K[m], K[m], ALU.mult)
                v.drain()
                v.tensor_reduce(ks[m], H[m].rearrange("p (h n) -> p h n", n=CA_D), AX, ALU.add).then_inc(S.kss_ready, 1)
                v.wait_ge(S.kr_ready, m + 1)
                newton(v, kr[m], ks[m], kt, CA_D)
                kh = K[m].rearrange("p (h n) -> p h n", n=CA_D)
                v.tensor_tensor(kh, kh, bc(kr[m].unsqueeze(2), [P, CA_H, CA_D]), ALU.mult).then_inc(S.kn_ready, 1)
            for m in range(2):
                v.wait_ge(S.kT_psum, m + 1)
                for q in range(2):
                    v.tensor_scalar(KM.rearrange("p (h q) m -> p q h m", q=2)[:, q, :, m * P:(m + 1) * P],
                                    e.pair(m).rearrange("p (h q n) -> p q h n", q=2, n=P)[:, q], e.pcol("ca_k", 2)[:, q:q + 1], None, ALU.mult)


def phase_cross(nc, e):
    A = e.A
    X1, KM, VM = A(e.at_X1, NT, D), A(e.at_KM, KD, MEM), A(e.at_VM, 2, D)
    LG = A(e.at_LG, NT, NG + NE)
    at = e.at_ca
    WQ = A(at, KD, D); at += KD * D
    WO = A(at, KD, D); at += KD * D
    WR = A(at, KD, NG + NE); at += KD * (NG + NE)
    H = A(at, D); at += D
    HT = A(at, KD, P); at += D
    Q = A(at, D); at += D
    SQ = A(at, D); at += D
    QT = A(at, KD, P); at += D
    PR = A(at, D); at += D
    PT = A(at, KD, P); at += D
    O = A(at, D); at += D
    OT = A(at, KD, P); at += D
    H3 = [A(at + D * p, D) for p in (0, 1)]; at += 2 * D
    RT = A(at, KD, P); at += D
    junk = SQ
    ss, rs, ss3, rs3 = A(at, 1), A(at + 1, 1), A(at + 2, 1), A(at + 3, 1)
    qs, qr, qt, mx, den = (A(at + 4 + 4 * n, 4) for n in range(5))
    assert at + 32 <= ARENA, at
    S = e.sems("ca", "settled wq_ld wo_ld wr_ld r_ready h_ready hT_psum hT_ready q_psum q_out qss_ready qr_ready qn_ready qT_psum qT_ready "
               "s_psum sm_ready p_ready pT_psum pT_ready o_psum on_ready oT_psum oT_ready wo_psum x_ready r3_ready h3_ready "
               "h3T_psum h3T_ready lg_psum lg_done h3_st0 h3_st1")
    h3_st = [S.h3_st0, S.h3_st1]
    heads = lambda ap: ap.rearrange("p (h n) -> p h n", n=CA_D)
    PA, PB, PC_, PD_ = e.pair(0), e.pair(1), e.pair(2), e.pair(3)
    with nc.Block() as block:
        @block.sync
        def _(sp):
            sp.dma_start(WQ, e.d.ca_wq.rearrange("(k p) n -> p k n", p=P)).then_inc(S.wq_ld, 16)
            sp.dma_start(WO, e.d.ca_wo.rearrange("(k p) n -> p k n", p=P)).then_inc(S.wo_ld, 16)
            sp.dma_start(WR[:, :, 0:NG], e.d.wg.rearrange("(k p) n -> p k n", p=P)).then_inc(S.wr_ld, 16)
            sp.dma_start(WR[:, :, NG:], e.d.we.rearrange("(k p) n -> p k n", p=P)).then_inc(S.wr_ld, 16)
            with sp.Fori(0, NT // 2) as i:
                for p in (0, 1):
                    t = 2 * i + p
                    sp.wait_ge(S.h3_ready, done(t))
                    sp.dma_start(e.d.h3[ds(t * P, P), :], H3[p]).then_inc(h3_st[p], 16)
            for p in (0, 1):
                sp.wait_ge(h3_st[p], 16 * (NT // 2))

        @block.gpsimd
        def _(g):
            pass

        @block.scalar
        def _(act):
            prime(act, S.r_ready, S.q_out, S.qr_ready, S.p_ready, S.pT_ready, S.oT_ready, S.r3_ready)
            with act.Fori(0, NT) as t:
                act.activation(junk, cut(X1, t), ACT.Square, accum_out=ss)
                act.drain()
                rstd(act, rs, ss, D, e.eps_rms).then_inc(S.r_ready, 1)
                act.wait_ge(S.q_psum, done(t))
                act.activation(Q, PB, ACT.Copy).then_inc(S.q_out, 1)
                act.wait_ge(S.qss_ready, done(t))
                rstd(act, qr, qs, CA_D, e.eps_rms).then_inc(S.qr_ready, 1)
                act.wait_ge(S.sm_ready, done(t))
                act.activation(PR, PR, ACT.Exp).then_inc(S.p_ready, 1)
                act.wait_ge(S.pT_psum, done(t))
                act.activation(PT.rearrange("p k n -> p (k n)"), PD_, ACT.Copy).then_inc(S.pT_ready, 1)
                act.wait_ge(S.oT_psum, done(t))
                act.activation(OT.rearrange("p k n -> p (k n)"), PA, ACT.Copy).then_inc(S.oT_ready, 1)
                act.wait_ge(S.x_ready, done(t))
                act.sem_inc(S.settled, 1)
                act.activation(junk, cut(X1, t), ACT.Square, accum_out=ss3)
                act.drain()
                rstd(act, rs3, ss3, D, e.eps_rms).then_inc(S.r3_ready, 1)
                act.drain()

        @block.tensor
        def _(pe):
            def transposes(out, src, sem):
                for k in range(KD):
                    ins = pe.transpose(out[:, k * P:(k + 1) * P], src[:, k * P:(k + 1) * P], e.ident)
                ins.then_inc(sem, 1)

            prime(pe, S.hT_psum, S.q_psum, S.qT_psum, S.s_psum, S.pT_psum, S.o_psum, S.oT_psum, S.wo_psum, S.h3T_psum, S.lg_psum)
            pe.wait_ge(S.wq_ld, 16)
            pe.wait_ge(S.wo_ld, 16)
            pe.wait_ge(S.wr_ld, 32)
            with pe.Fori(0, NT) as t:
                pe.wait_ge(S.h_ready, done(t))
                transposes(PA, H, S.hT_psum)
                pe.wait_ge(S.hT_ready, done(t))
                for h in range(2):
                    for k in range(KD):
                        ins = pe.matmul(PB[:, 512 * h:512 * h + 512], HT[:, k, :], WQ[:, k, 512 * h:512 * h + 512], start=k == 0, stop=k == KD - 1)
                ins.then_inc(S.q_psum, 1)
                pe.wait_ge(S.qn_ready, done(t))
                transposes(PA, Q, S.qT_psum)
                pe.wait_ge(S.qT_ready, done(t))
                for h in range(CA_H):
                    for q in range(2):
                        ins = pe.matmul(PC_[:, MEM * h:MEM * h + MEM], QT[:, 2 * h + q, :], KM[:, 2 * h + q, :], start=q == 0, stop=q == 1)
                ins.then_inc(S.s_psum, 1)
                pe.wait_ge(S.p_ready, done(t))
                transposes(PD_, PR, S.pT_psum)
                pe.wait_ge(S.pT_ready, done(t))
                for h in range(CA_H):
                    for m in range(2):
                        ins = pe.matmul(PC_[:, CA_D * h:CA_D * h + CA_D], PT[:, 2 * h + m, :], VM[:, m, CA_D * h:CA_D * h + CA_D], start=m == 0, stop=m == 1)
                ins.then_inc(S.o_psum, 1)
                pe.wait_ge(S.on_ready, done(t))
                transposes(PA, O, S.oT_psum)
                pe.wait_ge(S.oT_ready, done(t))
                for h in range(2):
                    for k in range(KD):
                        ins = pe.matmul(PB[:, 512 * h:512 * h + 512], OT[:, k, :], WO[:, k, 512 * h:512 * h + 512], start=k == 0, stop=k == KD - 1)
                ins.then_inc(S.wo_psum, 1)
                pe.wait_ge(S.h3_ready, done(t))
                transposes(PA, H, S.h3T_psum)
                pe.wait_ge(S.h3T_ready, done(t))
                for k in range(KD):
                    ins = pe.matmul(PD_[:, 0:NG + NE], RT[:, k, :], WR[:, k, :], start=k == 0, stop=k == KD - 1)
                ins.then_inc(S.lg_psum, 1)

        @block.vector
        def _(v):
            gain = lambda ap, name: v.tensor_tensor(ap, PA.rearrange("p (k n) -> p k n", n=P), bc(e.pcol(name, KD).unsqueeze(2), [P, KD, P]), ALU.mult)
            prime(v, S.h_ready, S.hT_ready, S.qss_ready, S.qn_ready, S.qT_ready, S.sm_ready, S.on_ready, S.x_ready, S.h3_ready, S.h3T_ready, S.lg_done)

            def body(i, p):
                t = 2 * i + p
                x = cut(X1, t)
                v.wait_ge(S.r_ready, done(t))
                v.tensor_scalar(H, x, rs, None, ALU.mult).then_inc(S.h_ready, 1)
                v.wait_ge(S.hT_psum, done(t))
                gain(HT, "g_ca").then_inc(S.hT_ready, 1)
                v.wait_ge(S.q_out, done(t))
                v.tensor_tensor(SQ, Q, Q, ALU.mult)
                v.drain()
                v.tensor_reduce(qs, heads(SQ), AX, ALU.add).then_inc(S.qss_ready, 1)
                v.wait_ge(S.qr_ready, done(t))
                newton(v, qr, qs, qt, CA_D)
                v.tensor_tensor(heads(Q), heads(Q), bc(qr.unsqueeze(2), [P, CA_H, CA_D]), ALU.mult).then_inc(S.qn_ready, 1)
                v.wait_ge(S.qT_psum, done(t))
                v.tensor_tensor(QT.rearrange("p (h q) n -> p h q n", q=2), PA.rearrange("p (h q n) -> p h q n", q=2, n=P),
                                bc(e.pcol("ca_q", 2).unsqueeze(1).unsqueeze(3), [P, CA_H, 2, P]), ALU.mult).then_inc(S.qT_ready, 1)
                v.wait_ge(S.s_psum, done(t))
                v.tensor_reduce(mx, heads(PC_), AX, ALU.max)
                v.drain()
                v.tensor_tensor(heads(PR), heads(PC_), bc(mx.unsqueeze(2), [P, CA_H, MEM]), ALU.subtract).then_inc(S.sm_ready, 1)
                v.wait_ge(S.p_ready, done(t))
                v.tensor_reduce(den, heads(PR), AX, ALU.add)
                v.drain()
                v.reciprocal(den, den)
                v.drain()
                v.wait_ge(S.o_psum, done(t))
                v.tensor_tensor(heads(O), heads(PC_), bc(den.unsqueeze(2), [P, CA_H, CA_D]), ALU.mult).then_inc(S.on_ready, 1)
                v.wait_ge(S.wo_psum, done(t))
                v.tensor_tensor(x, x, PB, ALU.add).then_inc(S.x_ready, 1)
                v.drain()
                v.wait_ge(S.r3_ready, done(t))
                v.tensor_scalar(H, x, rs3, None, ALU.mult)
                v.tensor_scalar(H3[p], x, rs3, None, ALU.mult).then_inc(S.h3_ready, 1)
                v.wait_ge(S.h3T_psum, done(t))
                gain(RT, "g_ffn").then_inc(S.h3T_ready, 1)
                v.wait_ge(S.lg_psum, done(t))
                v.tensor_tensor(cut(LG, t), PD_[:, 0:NG + NE], e.rowp("r_b", NG + NE), ALU.add).then_inc(S.lg_done, 1)
                v.drain()

            body(0, 0)
            body(0, 1)
            with v.Fori(1, NT // 2) as i:
                for p in (0, 1):
                    v.wait_ge(h3_st[p], 16 * i)
                    body(i, p)


def phase_route(nc, e):
    A = e.A
    LG = A(e.at_LG, NT, NG + NE)
    at = e.at_ca
    def new(*s):
        nonlocal at
        n = int(np.prod(s))
        r = A(at, *s)
        at += n
        return r
    EL, OH1, OH2, AS, CUM, T = (new(NT, NE) for _ in range(6))
    OG, EG, TG = new(NT, NG), new(NT, NG), new(NT, NG)
    gmax, gsum, rank, l1, l2, r, g1, g2, i1, i2, p1, p2, s1, s2 = (new(NT) for _ in range(14))
    ROW = new(2, NT, 4)
    SLOT = new(2, NT)
    CNT, CNI, NO, CO, TO, OL = new(NE), new(NE), new(NE), new(NE), new(NE, MAX_OVER + 1), new(4, MAX_OVER + 1)
    rowi, sloti = ROW.bitcast(I32), SLOT.bitcast(I32)
    PG, PN = e.PS[:, 0, 0:NT * NE], e.PS[:, 1, 0:NE]
    S = e.sems("route", "iota_done g_ready g_exp e_ready e_exp a_ready pos_psum row_ready tab_st cnt_psum")
    OV = A(e.at_over, 4, MAX_OVER + 1)
    with nc.Block() as block:
        @block.sync
        def _(sp):
            pass

        @block.gpsimd
        def _(g):
            for k in range(2):
                g.iota(rowi[:, k, :, 0:1], pattern=[[P, NT], [0, 1]], base=0, channel_multiplier=1)
                g.iota(rowi[:, k, :, 1:2], pattern=[[P, NT], [0, 1]], base=k * SEQ, channel_multiplier=1)
                g.memset(rowi[:, k, :, 3:4], 0)
            g.iota(OL.bitcast(I32)[:, 0, :], pattern=[[1, MAX_OVER + 1]], base=0, channel_multiplier=0)
            g.iota(OL.bitcast(I32)[:, 1, 0:1], pattern=[[1, 1]], base=0, channel_multiplier=0)
            g.drain()
            g.sem_inc(S.iota_done, 1)
            g.wait_ge(S.row_ready, 1)
            for k in range(2):
                for t in range(NT):
                    g.indirect_dma_start(out=e.d.tab, out_offset=bass.IndirectOffsetOnAxis(ap=sloti[:, k, t:t + 1], axis=0),
                                         in_=rowi[:, k, t, :], in_offset=None).then_inc(S.tab_st, 16)
            g.wait_ge(S.tab_st, 16 * 2 * NT)

        @block.scalar
        def _(act):
            act.wait_ge(S.g_ready, 1)
            act.activation(EG, EG, ACT.Exp).then_inc(S.g_exp, 1)
            act.wait_ge(S.e_ready, 1)
            act.activation(r, r, ACT.Exp).then_inc(S.e_exp, 1)

        @block.tensor
        def _(pe):
            pe.wait_ge(S.a_ready, 1)
            flat = lambda ap: ap.rearrange("p t n -> p (t n)")
            pe.matmul(PG, e.tri_lt, flat(AS), start=True, stop=False)
            pe.matmul(PG, e.ones, flat(CUM), start=False, stop=True).then_inc(S.pos_psum, 1)
            pe.matmul(PN, e.ones, CUM[:, NT - 1, :], start=True, stop=False)
            pe.matmul(PN, e.ones, AS[:, NT - 1, :], start=False, stop=True).then_inc(S.cnt_psum, 1)

        @block.vector
        def _(v):
            over = lambda ap, n: bc(ap.unsqueeze(2), [P, NT, n])
            def op(out, a, b, o):
                v.tensor_tensor(out, a, b, o)
                v.drain()
            def red(out, a, o):
                v.tensor_reduce(out, a, AX, o)
                v.drain()
            def first(onehot, x, best, n, ranks, tmp):
                op(onehot, x, over(best, n), ALU.is_equal)
                op(tmp, onehot, bc(ranks.unsqueeze(1), [P, NT, n]), ALU.mult)
                red(rank, tmp, ALU.max)
                op(onehot, over(rank, n), bc(ranks.unsqueeze(1), [P, NT, n]), ALU.is_equal)

            GL, XL = LG[:, :, 0:NG], LG[:, :, NG:]
            red(gmax, GL, ALU.max)
            first(OG, GL, gmax, NG, e.rowp("rank_g", NG), TG)
            v.tensor_tensor(EG, GL, over(gmax, NG), ALU.subtract).then_inc(S.g_ready, 1)
            v.wait_ge(S.g_exp, 1)
            red(gsum, EG, ALU.add)
            v.tensor_scalar(TG, OG, BIG, -BIG, ALU.mult, ALU.add)
            v.drain()
            eg = lambda ap: ap.rearrange("p t (g n) -> p t g n", g=NG)
            for t in range(NT):
                v.tensor_tensor(eg(T)[:, t], eg(XL)[:, t], bc(OG[:, t, :].unsqueeze(2), [P, NG, EPG]), ALU.mult)
            v.drain()
            for t in range(NT):
                v.tensor_tensor(eg(EL)[:, t], eg(T)[:, t], bc(TG[:, t, :].unsqueeze(2), [P, NG, EPG]), ALU.add)
            v.drain()
            red(l1, EL, ALU.max)
            first(OH1, EL, l1, NE, e.rowp("rank_e", NE), T)
            v.tensor_scalar(i1, rank, -1.0, float(NE), ALU.mult, ALU.add)
            v.scalar_tensor_tensor(EL, OH1, -2.0 * BIG, EL, ALU.mult, ALU.add)
            v.drain()
            red(l2, EL, ALU.max)
            first(OH2, EL, l2, NE, e.rowp("rank_e", NE), T)
            v.tensor_scalar(i2, rank, -1.0, float(NE), ALU.mult, ALU.add)
            v.tensor_tensor(r, l2, l1, ALU.subtract).then_inc(S.e_ready, 1)
            op(AS, OH1, OH2, ALU.add)
            v.memset(CUM[:, 0, :], 0.0)
            v.drain()
            for t in range(1, NT):
                op(CUM[:, t, :], CUM[:, t - 1, :], AS[:, t - 1, :], ALU.add)
            v.sem_inc(S.a_ready, 1)
            v.wait_ge(S.e_exp, 1)
            v.tensor_scalar(g1, r, 1.0, None, ALU.add)
            v.drain()
            op(g1, g1, gsum, ALU.mult)
            v.reciprocal(g1, g1)
            v.drain()
            op(g2, g1, r, ALU.mult)
            v.wait_ge(S.pos_psum, 1)
            pos = PG.rearrange("p (t n) -> p t n", n=NE)
            v.wait_ge(S.iota_done, 1)
            for k, (oh, i, g) in enumerate(((OH1, i1, g1), (OH2, i2, g2))):
                op(T, oh, pos, ALU.mult)
                red(p1, T, ALU.add)
                v.scalar_tensor_tensor(s1, i, float(SEQ), p1, ALU.mult, ALU.add)
                v.drain()
                v.tensor_copy(sloti[:, k, :], s1)
                v.tensor_copy(ROW[:, k, :, 2:3].rearrange("p t o -> p (t o)"), g)
                v.drain()
            v.sem_inc(S.row_ready, 1)
            v.wait_ge(S.cnt_psum, 1)
            v.tensor_scalar(CNT, PN, float(P), None, ALU.is_gt)
            v.drain()
            v.tensor_copy(NO, CNT)
            v.drain()
            for b in range(2, MAX_BLOCKS):
                v.tensor_scalar(CNT, PN, float(P * b), None, ALU.is_gt)
                v.drain()
                op(NO, NO, CNT, ALU.add)
            v.tensor_copy(CO[:, 0:1], NO[:, 0:1])
            v.drain()
            for x in range(1, NE):
                op(CO[:, x:x + 1], CO[:, x - 1:x], NO[:, x:x + 1], ALU.add)
            N = OL[:, 2, :]
            v.tensor_copy(N, OL.bitcast(I32)[:, 0, :])
            v.drain()
            nb = MAX_OVER + 1
            before = TO
            op(before, bc(CO.unsqueeze(2), [P, NE, nb]), bc(N.unsqueeze(1), [P, NE, nb]), ALU.is_le)
            red(OV[:, 3, :], before.rearrange("p x n -> p n x"), ALU.add)
            op(before, before, bc(NO.unsqueeze(2), [P, NE, nb]), ALU.mult)
            red(OL[:, 3, :], before.rearrange("p x n -> p n x"), ALU.add)
            op(N, N, OL[:, 3, :], ALU.subtract)
            v.tensor_scalar(N, N, float(P), float(P), ALU.mult, ALU.add)
            v.tensor_scalar(OV[:, 3, :], OV[:, 3, :], float(NE - 1), None, ALU.min)
            v.drain()
            v.scalar_tensor_tensor(N, OV[:, 3, :], float(SEQ), N, ALU.mult, ALU.add)
            v.drain()
            v.tensor_scalar(N, N, float(NE * SEQ - P), None, ALU.min)
            v.drain()
            v.tensor_copy(OV.bitcast(I32)[:, 0, :], OV[:, 3, :])
            v.tensor_copy(OV.bitcast(I32)[:, 1, :], N)
            v.tensor_copy(OV.bitcast(I32)[:, 2, 0:1], CO[:, NE - 1:NE])
            v.drain()


def phase_experts(nc, e):
    A = e.A
    at = e.at_ca
    W = []
    for p in (0, 1):
        W.append((A(at, KD, EH), A(at + 4096, KD, EH), A(at + 8192, EH // P, D)))
        at += 12288
    XT = [A(at + D * p, KD, P) for p in (0, 1)]; at += 2 * D
    E_ = A(at, EH); at += EH
    HID = [A(at + EH * p, EH) for p in (0, 1)]; at += 2 * EH
    HT = [A(at + EH * p, EH // P, P) for p in (0, 1)]; at += 2 * EH
    Y = [A(at + D * p, D) for p in (0, 1)]; at += 2 * D
    assert at <= ARENA, at
    at = AT_HT
    XG = [A(at + D * p, D) for p in (0, 1)]; at += 2 * D
    IX = A(at, NE, 4); at += NE * 4
    IG = [A(at + 4 * p, 4) for p in (0, 1)]; at += 8
    IS = [A(at + 4 * p, 4) for p in (0, 1)]; at += 8
    assert at <= e.at_X1
    IXI = IX.bitcast(I32)
    IGI, ISI = [a.bitcast(I32) for a in IG], [a.bitcast(I32) for a in IS]
    S = e.sems("exp", "ix_ld wg_ld0 wg_ld1 wu_ld0 wu_ld1 wd_ld0 wd_ld1 xg_ld0 xg_ld1 y_st0 y_st1 xT_psum xT_ready gu_psum g_exp gu_read "
               "hT_psum hT_ready y_psum y_out")
    wg_ld, wu_ld, wd_ld = (S.wg_ld0, S.wg_ld1), (S.wu_ld0, S.wu_ld1), (S.wd_ld0, S.wd_ld1)
    xg_ld, y_st = (S.xg_ld0, S.xg_ld1), (S.y_st0, S.y_st1)
    PX, PY = e.pair(0), e.pair(3)
    PH = e.PS[:, 0, :]
    PGU = [(e.PS[:, 2 + 2 * p, :], e.PS[:, 3 + 2 * p, :]) for p in (0, 1)]
    last = NE // 2 - 1

    def steps(eng, step):
        for x in range(4):
            step(x, x // 2, x % 2, x == 0, False)
        with eng.Fori(2, last) as i:
            for p in (0, 1):
                step(2 * i + p, i, p, False, False)
        step(2 * last, last, 0, False, False)
        step(2 * last + 1, last, 1, False, True)

    with nc.Block() as block:
        @block.sync
        def _(sp):
            w = lambda src, x, n: src[ds(x, 1)].rearrange("o (k p) n -> p (o k) n", p=P)

            def load(x, p):
                sp.dma_start(W[p][0], w(e.d.w_gate, x, EH)).then_inc(wg_ld[p], 16)
                sp.dma_start(W[p][1], w(e.d.w_up, x, EH)).then_inc(wu_ld[p], 16)

            def load_down(x, p):
                sp.dma_start(W[p][2], w(e.d.w_down, x, D)).then_inc(wd_ld[p], 16)

            for p in (0, 1):
                load(p, p)
                load_down(p, p)
            with sp.Fori(1, NE // 2) as i:
                for p in (0, 1):
                    x = 2 * i + p
                    sp.wait_ge(S.gu_psum, done(x - 2))
                    load(x, p)
                    sp.wait_ge(S.y_psum, done(x - 2))
                    load_down(x, p)

        @block.gpsimd
        def _(g):
            def gather(x, p):
                g.wait_ge(S.xT_psum, done(x - 2))
                g.tensor_copy(IGI[p], IXI[:, ds(x, 1), :].rearrange("p o n -> p (o n)"))
                g.drain()
                g.indirect_dma_start(out=XG[p], out_offset=None, in_=e.d.h3,
                                     in_offset=bass.IndirectOffsetOnAxis(ap=IGI[p][:, 0:1], axis=0)).then_inc(xg_ld[p], 16)

            def scatter(x, p):
                g.wait_ge(S.y_out, done(x))
                g.tensor_copy(ISI[p], IXI[:, ds(x, 1), :].rearrange("p o n -> p (o n)"))
                g.drain()
                g.indirect_dma_start(out=e.d.yc, out_offset=bass.IndirectOffsetOnAxis(ap=ISI[p][:, 1:2], axis=0), in_=Y[p],
                                     in_offset=None, bounds_check=2 * SEQ - 1, oob_is_err=False).then_inc(y_st[p], 16)

            g.dma_start(IXI, e.d.tab.rearrange("(x r) c -> r x c", r=SEQ)[0:P]).then_inc(S.ix_ld, 16)
            g.wait_ge(S.ix_ld, 16)

            def step(x, i, p, first, end):
                if not end:
                    if not first:
                        g.wait_ge(xg_ld[1 - p], 16 * i + 16 * p)
                    gather(x + 1, 1 - p)
                if not first:
                    if not (isinstance(x, int) and x <= 2):
                        g.wait_ge(y_st[1 - p], 16 * i - 16 + 16 * p)
                    scatter(x - 1, 1 - p)

            gather(0, 0)
            steps(g, step)
            g.wait_ge(y_st[1], 16 * last)
            scatter(NE - 1, 1)
            for p in (0, 1):
                g.wait_ge(y_st[p], 16 * (NE // 2))

        @block.scalar
        def _(act):
            def hidden_out(x, p):
                act.wait_ge(S.hT_psum, done(x))
                act.wait_ge(S.y_psum, done(x - 2))
                act.activation(HT[p].rearrange("p k n -> p (k n)"), PH, ACT.Copy).then_inc(S.hT_ready, 1)

            def y_out(x, p, stores):
                act.wait_ge(S.y_psum, done(x))
                if stores is not None:
                    act.wait_ge(y_st[p], stores)
                act.activation(Y[p], PY, ACT.Copy, scale=IX[:, ds(x, 1), 2:3].rearrange("p o n -> p (o n)")).then_inc(S.y_out, 1)

            def step(x, i, p, first, end):
                if not first:
                    hidden_out(x - 1, 1 - p)
                act.wait_ge(S.gu_psum, done(x))
                act.wait_ge(S.gu_read, done(x - 1))
                act.activation(E_, PGU[p][0], ACT.Exp, scale=-1.0).then_inc(S.g_exp, 1)
                if not first:
                    y_out(x - 1, 1 - p, None if isinstance(x, int) and x <= 2 else 16 * i - 16 + 16 * p)

            prime(act, S.hT_ready, S.g_exp, S.y_out)
            act.wait_ge(S.ix_ld, 16)
            steps(act, step)
            hidden_out(NE - 1, 1)
            y_out(NE - 1, 1, 16 * last)

        @block.tensor
        def _(pe):
            def tokens(x, p, loads):
                pe.wait_ge(xg_ld[p], loads)
                pe.wait_ge(S.hT_ready, done(x - 2))
                for k in range(KD):
                    ins = pe.transpose(PX[:, k * P:(k + 1) * P], XG[p][:, k * P:(k + 1) * P], e.ident)
                ins.then_inc(S.xT_psum, 1)

            def hidden(x, p):
                pe.wait_ge(S.gu_read, done(x))
                for k in range(EH // P):
                    ins = pe.transpose(PH[:, k * P:(k + 1) * P], HID[p][:, k * P:(k + 1) * P], e.ident)
                ins.then_inc(S.hT_psum, 1)

            def down(x, p, loads):
                pe.wait_ge(wd_ld[p], loads)
                pe.wait_ge(S.hT_ready, done(x))
                pe.wait_ge(S.y_out, done(x - 1))
                for h in range(2):
                    for k in range(EH // P):
                        ins = pe.matmul(PY[:, 512 * h:512 * h + 512], HT[p][:, k, :], W[p][2][:, k, 512 * h:512 * h + 512], start=k == 0, stop=k == EH // P - 1)
                ins.then_inc(S.y_psum, 1)

            def step(x, i, p, first, end):
                pe.wait_ge(S.xT_ready, done(x))
                if not first:
                    hidden(x - 1, 1 - p)
                for n, ld in enumerate((wg_ld, wu_ld)):
                    pe.wait_ge(ld[p], 16 * i + 16)
                    if n == 0:
                        pe.wait_ge(S.gu_read, done(x - 2))
                    for k in range(KD):
                        ins = pe.matmul(PGU[p][n], XT[p][:, k, :], W[p][n][:, k, :], start=k == 0, stop=k == KD - 1)
                ins.then_inc(S.gu_psum, 1)
                if not end:
                    tokens(x + 1, 1 - p, 16 * i + 16 + 16 * p)
                if not first:
                    down(x - 1, 1 - p, 16 * i + 16 * p)

            prime(pe, S.xT_psum, S.gu_psum, S.hT_psum, S.y_psum)
            tokens(0, 0, 16)
            steps(pe, step)
            hidden(NE - 1, 1)
            down(NE - 1, 1, 16 * (NE // 2))

        @block.vector
        def _(v):
            def tokens_out(x, p):
                v.wait_ge(S.xT_psum, done(x))
                v.wait_ge(S.gu_psum, done(x - 2))
                v.tensor_tensor(XT[p], PX.rearrange("p (k n) -> p k n", n=P), bc(e.pcol("g_ffn", KD).unsqueeze(2), [P, KD, P]), ALU.mult).then_inc(S.xT_ready, 1)

            def step(x, i, p, first, end):
                if not end:
                    tokens_out(x + 1, 1 - p)
                v.wait_ge(S.g_exp, done(x))
                v.tensor_scalar(E_, E_, 1.0, None, ALU.add)
                v.drain()
                v.reciprocal(E_, E_)
                v.drain()
                v.wait_ge(S.hT_psum, done(x - 2))
                v.tensor_tensor(HID[p], E_, PGU[p][0], ALU.mult)
                v.drain()
                v.tensor_tensor(HID[p], HID[p], PGU[p][1], ALU.mult).then_inc(S.gu_read, 1)
                v.drain()

            prime(v, S.xT_ready, S.gu_read)
            tokens_out(0, 0)
            steps(v, step)
    e.exp = dict(W=W[0], XT=XT[0], E=E_, HID=HID[0], HT=HT[0], Y=Y[0], XG=XG[0], IX=IX[:, 0, :])


def phase_overflow(nc, e):
    A = e.A
    b = e.exp
    W, XT, E_, HID, HT, Y, XG, IX = (b[k] for k in ("W", "XT", "E", "HID", "HT", "Y", "XG", "IX"))
    OV = A(e.at_over, 4, MAX_OVER + 1).bitcast(I32)
    PX, PY = e.pair(0), e.pair(3)
    G, U, PH = e.PS[:, 2, :], e.PS[:, 3, :], e.PS[:, 4, :]
    S = e.sems("over", "settled w_ld ix_ld xg_ld y_st xT_psum xT_ready gu_psum g_exp hid_ready hT_psum hT_ready y_psum y_out")
    number = lambda eng: eng.value_load(OV[0:1, 2, 0:1], min_val=0, max_val=MAX_OVER)

    def loop(eng, body):
        n_over = number(eng)
        with eng.Fori(0, MAX_OVER) as n:
            with eng.If(n_over > n):
                body(n)

    with nc.Block() as block:
        @block.sync
        def _(sp):
            def body(n):
                x = sp.value_load(OV[0:1, 0, ds(n, 1)], min_val=0, max_val=NE - 1)
                sp.wait_ge(S.y_out, n + 1)
                for m, src in enumerate((e.d.w_gate, e.d.w_up, e.d.w_down)):
                    sp.dma_start(W[m], src[ds(x, 1)].rearrange("o (k p) n -> p (o k) n", p=P)).then_inc(S.w_ld, 16)
            loop(sp, body)

        @block.gpsimd
        def _(g):
            def body(n):
                row = g.value_load(OV[0:1, 1, ds(n, 1)], min_val=0, max_val=NE * SEQ - P)
                g.wait_ge(S.y_out, n + 1)
                g.dma_start(IX.bitcast(I32), e.d.tab[ds(row, P), :]).then_inc(S.ix_ld, 16)
                g.wait_ge(S.ix_ld, 16 * n + 16)
                g.sem_inc(S.settled, 1)
                g.indirect_dma_start(out=XG, out_offset=None, in_=e.d.h3,
                                     in_offset=bass.IndirectOffsetOnAxis(ap=IX.bitcast(I32)[:, 0:1], axis=0)).then_inc(S.xg_ld, 16)
                g.wait_ge(S.y_out, n + 2)
                g.sem_inc(S.settled, 1)
                g.indirect_dma_start(out=e.d.yc, out_offset=bass.IndirectOffsetOnAxis(ap=IX.bitcast(I32)[:, 1:2], axis=0), in_=Y,
                                     in_offset=None, bounds_check=2 * SEQ - 1, oob_is_err=False).then_inc(S.y_st, 16)
                g.wait_ge(S.y_st, 16 * n + 16)
                g.sem_inc(S.settled, 1)
            loop(g, body)

        @block.scalar
        def _(act):
            def body(n):
                act.wait_ge(S.gu_psum, n + 1)
                act.activation(E_, G, ACT.Exp, scale=-1.0).then_inc(S.g_exp, 1)
                act.wait_ge(S.hT_psum, n + 1)
                act.activation(HT.rearrange("p k n -> p (k n)"), PH, ACT.Copy).then_inc(S.hT_ready, 1)
                act.wait_ge(S.y_psum, n + 1)
                act.activation(Y, PY, ACT.Copy, scale=IX[:, 2:3]).then_inc(S.y_out, 1)
            act.sem_inc(S.y_out, 1)
            loop(act, body)

        @block.tensor
        def _(pe):
            def body(n):
                pe.wait_ge(S.xg_ld, 16 * n + 16)
                for k in range(KD):
                    ins = pe.transpose(PX[:, k * P:(k + 1) * P], XG[:, k * P:(k + 1) * P], e.ident)
                ins.then_inc(S.xT_psum, 1)
                pe.wait_ge(S.xT_ready, n + 1)
                pe.wait_ge(S.w_ld, 48 * n + 48)
                for m, out in enumerate((G, U)):
                    for k in range(KD):
                        ins = pe.matmul(out, XT[:, k, :], W[m][:, k, :], start=k == 0, stop=k == KD - 1)
                ins.then_inc(S.gu_psum, 1)
                pe.wait_ge(S.hid_ready, n + 1)
                for k in range(EH // P):
                    ins = pe.transpose(PH[:, k * P:(k + 1) * P], HID[:, k * P:(k + 1) * P], e.ident)
                ins.then_inc(S.hT_psum, 1)
                pe.wait_ge(S.hT_ready, n + 1)
                for h in range(2):
                    for k in range(EH // P):
                        ins = pe.matmul(PY[:, 512 * h:512 * h + 512], HT[:, k, :], W[2][:, k, 512 * h:512 * h + 512], start=k == 0, stop=k == EH // P - 1)
                ins.then_inc(S.y_psum, 1)
            loop(pe, body)

        @block.vector
        def _(v):
            def body(n):
                v.wait_ge(S.xT_psum, n + 1)
                v.tensor_tensor(XT, PX.rearrange("p (k n) -> p k n", n=P), bc(e.pcol("g_ffn", KD).unsqueeze(2), [P, KD, P]), ALU.mult).then_inc(S.xT_ready, 1)
                v.wait_ge(S.g_exp, n + 1)
                v.tensor_scalar(E_, E_, 1.0, None, ALU.add)
                v.drain()
                v.reciprocal(E_, E_)
                v.drain()
                v.tensor_tensor(HID, E_, G, ALU.mult)
                v.drain()
                v.tensor_tensor(HID, HID, U, ALU.mult).then_inc(S.hid_ready, 1)
            loop(v, body)


def phase_final(nc, e):
    A = e.A
    X1 = A(e.at_X1, NT, D)
    at = e.at_ca
    YC = [A(at + 2 * D * p, 2, D) for p in (0, 1)]; at += 4 * D
    O = [A(at + D * p, D) for p in (0, 1)]
    S = e.sems("fin", "y_ld0 y_ld1 added out_st0 out_st1")
    y_ld, out_st = (S.y_ld0, S.y_ld1), (S.out_st0, S.out_st1)
    yc = e.d.yc.rearrange("(k r) n -> r k n", k=2)
    with nc.Block() as block:
        @block.sync
        def _(sp):
            for p in (0, 1):
                sp.dma_start(YC[p], yc[p * P:(p + 1) * P]).then_inc(y_ld[p], 16)
            with sp.Fori(1, NT // 2) as i:
                for p in (0, 1):
                    t = 2 * i + p
                    sp.wait_ge(S.added, t - 1)
                    sp.dma_start(YC[p], yc[ds(t * P, P)]).then_inc(y_ld[p], 16)

        @block.scalar
        def _(act):
            with act.Fori(0, NT // 2) as i:
                for p in (0, 1):
                    t = 2 * i + p
                    act.wait_ge(S.added, t + 1)
                    act.dma_start(e.d.out[ds(t * P, P), :], O[p]).then_inc(out_st[p], 16)
            for p in (0, 1):
                act.wait_ge(out_st[p], 16 * (NT // 2))

        @block.gpsimd
        def _(g):
            pass

        @block.tensor
        def _(pe):
            pass

        @block.vector
        def _(v):
            def body(t, p, loads):
                v.wait_ge(y_ld[p], loads)
                v.tensor_tensor(O[p], cut(X1, t), YC[p][:, 0, :], ALU.add)
                v.drain()
                v.tensor_tensor(O[p], O[p], YC[p][:, 1, :], ALU.add).then_inc(S.added, 1)

            body(0, 0, 16)
            body(1, 1, 16)
            with v.Fori(1, NT // 2) as i:
                for p in (0, 1):
                    v.wait_ge(out_st[p], 16 * i)
                    body(2 * i + p, p, 16 * i + 16)


def build(nc, d):
    e = Env()
    e.d = d
    ctx = ExitStack()
    with ctx:
        e.arena = ctx.enter_context(nc.sbuf_tensor("arena", [P, ARENA], F32))
        e.PS = ctx.enter_context(nc.psum_tensor("psum", [P, 8, 512], F32))

        def A(at, *shape):
            n = int(np.prod(shape))
            ap = e.arena[:, at:at + n]
            if len(shape) == 2:
                ap = ap.rearrange("p (a b) -> p a b", a=shape[0])
            elif len(shape) == 3:
                ap = ap.rearrange("p (a b c) -> p a b c", a=shape[0], b=shape[1])
            return ap

        def sems(phase, names):
            s = namedtuple(phase, names)(*[nc.alloc_semaphore(f"{phase}_{n}") for n in names.split()])
            e.used += list(s)
            return s

        e.A, e.sems = A, sems
        e.pair = lambda n: e.PS[:, 2 * n:2 * n + 2, :].rearrange("p a b -> p (a b)")
        e.ident, e.tri_le, e.tri_gt, e.ones, e.tri_lt = (A(AT_CONST + P * n, P) for n in range(5))
        e.mask = A(AT_CONST + 5 * P, SEQ)
        e.par, e.row = A(AT_PAR, NPAR), A(AT_ROW, NROW)
        e.pcol = lambda n, w: e.par[:, PC[n]:PC[n] + w]
        e.rowp = lambda n, w: e.row[:, RC[n]:RC[n] + w]
        e.eps_rms, e.eps_ln = e.rowp("eps_rms", 1), e.rowp("eps_ln", 1)
        e.at_U2 = AT_B + GT * (SEQ + 32)
        e.at_YSC = e.at_U2 + GT * SEQ
        e.at_XBC = e.at_YSC + GT * SEQ
        e.at_CAT_SSD, e.at_CAT_ATT, e.at_CAT_CF = AT_HT, AT_HT + GT * SEQ, AT_B
        e.CAT = [A(a, GT, SEQ) for a in (e.at_CAT_SSD, e.at_YSC, e.at_CAT_ATT, e.at_CAT_CF)]
        e.at_X1 = AT_QT
        e.at_work_out = e.at_XBC + NT * GW + 12 * D
        e.at_KM, e.at_VM = AT_HT, AT_HT + KD * MEM
        e.at_LG = e.at_VM + 2 * D
        e.at_over = e.at_LG + NT * (NG + NE)
        e.at_ca = e.at_X1 + NT * D
        e.used = []
        for phase in PHASES:
            if phase == phase_experts:
                nc.clear_and_free_semaphores(e.used)
                nc.all_engine_barrier()
                e.used = []
            phase(nc, e)


PHASES = [phase_tokens, phase_features, phase_ssd, phase_attention, phase_norm_cf, phase_out, phase_memory, phase_cross,
          phase_route, phase_experts, phase_overflow, phase_final]


def constants():
    k, n = np.arange(P)[:, None], np.arange(P)[None, :]
    delta = 7 * P + k - np.arange(SEQ)[None, :]
    count = ((delta >= 0) & (delta <= 128)) * 1 + ((delta >= 0) & (delta <= 512) & (delta % 4 == 0)) * 1 \
        + ((delta >= 0) & (delta <= 2048) & (delta % 16 == 0)) * 1
    mask = np.where(count > 0, np.log(np.maximum(count, 1)), -BIG)
    parts = [k == n, k <= n, k > n, np.ones((P, P)), k < n, mask]
    return np.concatenate([np.asarray(a, np.float32) for a in parts], axis=1)


def kernel(**a):
    import concourse.bacc as bacc
    from concourse.bass_utils import run_bass_kernel_spmd

    f = {n: np.asarray(v) for n, v in a.items()}
    cols = lambda v: v.reshape(-1, P).T
    w_in = f["w_in"][0]
    sizes = [GW, XBC_T * P, HEADS, GW, GW, GW, GW, GW, GW, GW, GW]
    o = np.concatenate([[0], np.cumsum(sizes)])
    z, xbc, dt, sb, sc, sh, q, k, v, ca, cg = (w_in[:, o[n]:o[n + 1]] for n in range(11))
    w_tok = np.concatenate([q, k, v, z, dt], axis=1).reshape(KD, P, TOK_COLS).transpose(1, 0, 2)
    tile = lambda w, n: w[:, n * P:(n + 1) * P]
    feats = [tile(w, n) for n in range(GT) for w in (ca, cg)] + [tile(w, n) for n in range(GT) for w in (sb, sc, sh)] \
        + [tile(xbc, n) for n in range(XBC_T)]
    w_feat = np.stack(feats).reshape(NFEAT, KD, P, P).transpose(0, 2, 1, 3).reshape(NFEAT, P, KD * P)
    taps = lambda w: w.reshape(w.shape[0], -1, P).transpose(2, 1, 0).reshape(P, -1)
    twice = lambda g: np.concatenate([g, g]).reshape(P, 1)
    par = np.concatenate([cols(f["norm_mix"][0]), cols(f["norm_ca"][0]), cols(f["norm_mem"][0]), cols(f["norm_ffn"][0]),
                          taps(f["cf_conv_w"][0]), cols(f["cf_conv_b"][0]), cols(f["cf_ln_g"][0]), cols(f["cf_ln_b"][0]),
                          taps(f["ssd_conv_w"][0]), cols(f["ssd_conv_b"][0]), taps(f["sc_conv_w"][0]), cols(f["ssd_norm"][0]),
                          twice(f["attn_q_norm"][0]), twice(f["attn_k_norm"][0]), cols(f["ca_q_norm"][0]), cols(f["ca_k_norm"][0])], axis=1)
    rank = np.concatenate([NG - np.arange(NG), NE - np.arange(NE), [RMS_EPS, LN_EPS]]).astype(np.float32)
    row = np.concatenate([f["ssd_dt_bias"][0], f["ssd_a_log"][0], f["ssd_d"][0], f["router_group_b"][0], f["router_expert_b"][0], rank])
    arrays = dict(x=f["x"][0], mem=f["mem"][0], consts=constants(), par=par, row=row, w_tok=w_tok, w_feat=w_feat,
                  w_out=f["w_out"][0], ca_wq=f["ca_wq"][0], ca_wkv=f["ca_wkv"][0], ca_wo=f["ca_wo"][0],
                  wg=f["router_group_w"][0], we=f["router_expert_w"][0],
                  w_gate=f["exp_w_gate"][0], w_up=f["exp_w_up"][0], w_down=f["exp_w_down"][0])
    arrays = {n: np.ascontiguousarray(x) for n, x in arrays.items()}
    nc = bacc.Bacc("TRN2", target_bir_lowering=False, num_devices=1)
    dram = {n: nc.dram_tensor(n, x.shape, F32, kind="ExternalInput").ap() for n, x in arrays.items()}
    dram["tab"] = nc.dram_tensor("tab", [NE * SEQ, 4], I32, kind="Internal").ap()
    dram["h3"] = nc.dram_tensor("h3", [SEQ + 1, D], F32, kind="Internal").ap()
    dram["yc"] = nc.dram_tensor("yc", [2 * SEQ, D], F32, kind="Internal").ap()
    dram["out"] = nc.dram_tensor("out", [SEQ, D], F32, kind="ExternalOutput").ap()
    d = namedtuple("Dram", list(dram))(**dram)
    build(nc, d)
    r = run_bass_kernel_spmd(nc, [arrays], core_ids=[0])
    return r.results[0]["out"].reshape(1, SEQ, D)
```

```python
from collections import namedtuple
from contextlib import ExitStack

import numpy as np
import concourse.bass as bass
import concourse.mybir as mybir
from concourse.alu_op_type import AluOpType as ALU

F32 = mybir.dt.float32
I32 = mybir.dt.int32
ACT = mybir.ActivationFunctionType
LN_EXP = "natural_log_exp_and_others"
AX = mybir.AxisListType.X
ds = bass.ds

P = 128
D = 1024
SEQ = 1024
MEM = 256
KD = D // P
NT = SEQ // P
GW = 384
GT = GW // P
HEADS = 6
SSD_NG = 2
HD = 64
XBC_T = 7
CF_K, SSD_K, SC_K = 31, 4, 3
CA_H, CA_D = 4, 256
NG, EPG = 4, 8
NE = NG * EPG
EH = 512
RMS_EPS, LN_EPS = 1e-6, 1e-5
BIG = 1.0e30
TOK_COLS = 4 * GW + HEADS
NFEAT = 3 * XBC_T + 1
MAX_BLOCKS = SEQ // P
MAX_OVER = 2 * SEQ // P - 1
SKIP = 1 << 20

PC = {}
_at = 0
for _n, _w in (("g_mix", KD), ("g_ca", KD), ("g_mem", KD), ("g_ffn", KD), ("cf_w", GT * CF_K), ("cf_b", GT),
               ("ln_g", GT), ("ln_b", GT), ("ssd_w", XBC_T * SSD_K), ("ssd_b", XBC_T), ("sc_w", GT * SC_K),
               ("ssd_g", GT), ("att_q", 1), ("att_k", 1), ("ca_q", 2), ("ca_k", 2)):
    PC[_n] = _at
    _at += _w
NPAR = _at
RC = {}
_at = 0
for _n, _w in (("dt_b", HEADS), ("a_log", HEADS), ("ssd_d", HEADS), ("r_b", NG + NE), ("rank_g", NG), ("rank_e", NE), ("eps_rms", 1), ("eps_ln", 1)):
    RC[_n] = _at
    _at += _w
NROW = _at

AT_CONST = 0
AT_PAR = 1664
AT_ROW = AT_PAR + 192
AT_KEEP = 1952
AT_HT = 2048
AT_QT, AT_KT, AT_V, AT_Z, AT_DT = 10240, 13312, 16384, 19456, 22528
AT_B = 22592
ARENA = 53100


def done(t, m=1, n=None):
    return (t + 2) * m + (m if n is None else n + 1)


class Env:
    pass


def bc(ap, shape):
    return ap.to_broadcast(shape)


def cut(ap, t):
    return ap[:, ds(t, 1), :].rearrange("p o n -> p (o n)")


def prime(eng, *sems):
    for s in sems:
        s, m = s if isinstance(s, tuple) else (s, 1)
        eng.sem_inc(s, 2 * m)


def newton(v, r, ss, tmp, n, eps=RMS_EPS):
    v.tensor_tensor(tmp, r, r, ALU.mult)
    v.drain()
    v.scalar_tensor_tensor(tmp, ss, float(n) * eps, tmp, ALU.add, ALU.mult)
    v.drain()
    v.tensor_scalar(tmp, tmp, -0.5 / n, 1.5, ALU.mult, ALU.add)
    v.drain()
    v.tensor_tensor(r, r, tmp, ALU.mult)
    v.drain()


def rstd(act, r, ss, n, eps):
    act.activation(r, ss, ACT.Ln, scale=1.0 / n, bias=eps)
    act.drain()
    return act.activation(r, r, ACT.Exp, scale=-0.5)


def phase_tokens(nc, e):
    A = e.A
    HT = A(AT_HT, KD, SEQ)
    QT, KT = A(AT_QT, GT, SEQ), A(AT_KT, GT, SEQ)
    V, Z, DT = A(AT_V, NT, GW), A(AT_Z, NT, GW), A(AT_DT, NT, HEADS)
    at = AT_B
    W = A(at, KD, TOK_COLS); at += KD * TOK_COLS
    X = [A(at + D * p, D) for p in (0, 1)]; at += 2 * D
    H = [A(at + D * p, D) for p in (0, 1)]; at += 2 * D
    HC = [A(at + D * p, KD, P) for p in (0, 1)]; at += 2 * D
    Y = [A(at + 1536 * p, 1536) for p in (0, 1)]; at += 3072
    SQ = A(at, 2 * GW); at += 2 * GW
    junk = A(at, D); at += D
    TB = A(at, 1024); at += 1024
    ZROW = A(at, 1024); at += 1024
    ss, rs = A(at, 2), A(at + 2, 2)
    qss, qr, qt = A(at + 4, 12), A(at + 16, 12), A(at + 28, 12)
    e.W_feat = [A(ARENA - D * (j + 1), KD, P) for j in range(3)]
    e.feat_ld = e.sems("feat_ld", "w_ld0 w_ld1 w_ld2")
    assert at + 64 <= ARENA - 3 * D
    S = e.sems("tok", "const_ld par_ld row_ld w_ld0 w_ld1 w_ld2 x_ld0 x_ld1 tab_init tab_st r_ready h_ready T_psum hT_ready ht_copied "
               "proj_psum dt_psum y_ready qss_ready qr_ready qn_ready qk_psum qk_done dt_done")
    x_ld = [S.x_ld0, S.x_ld1]
    PH = e.pair(0)
    PQK = e.pair(3)
    PP = [e.PS[:, 2 + n, :] for n in range(3)]
    PDT = e.PS[:, 5, 0:HEADS]
    half = NT // 2

    with nc.Block() as block:
        @block.sync
        def _(sp):
            sp.dma_start(e.arena[:, AT_CONST:AT_PAR], e.d.consts).then_inc(S.const_ld, 16)
            sp.dma_start(e.par, e.d.par).then_inc(S.par_ld, 16)
            sp.dma_start(e.row, e.d.row.partition_broadcast(P)).then_inc(S.row_ld, 16)
            for p in (0, 1):
                sp.dma_start(X[p], e.d.x[p * P:(p + 1) * P, :]).then_inc(x_ld[p], 16)
            for n in range(3):
                cols = slice(512 * n, 512 * n + 512 if n < 2 else TOK_COLS)
                sp.dma_start(W[:, :, cols], e.d.w_tok[:, :, cols]).then_inc((S.w_ld0, S.w_ld1, S.w_ld2)[n], 16)
            with sp.Fori(1, half) as i:
                for p in (0, 1):
                    t = 2 * i + p
                    sp.wait_ge(S.h_ready, done(t - 2))
                    sp.dma_start(X[p], e.d.x[ds(t * P, P), :]).then_inc(x_ld[p], 16)
            for j in range(2):
                sp.dma_start(e.W_feat[j].rearrange("p k n -> p (k n)"), e.d.w_feat[j]).then_inc(e.feat_ld[j], 16)
            sp.wait_ge(S.tab_init, 4)
            sp.dma_start(e.d.tab.rearrange("(p r) c -> p (r c)", p=P), TB.bitcast(I32)).then_inc(S.tab_st, 16)
            sp.dma_start(e.d.h3[SEQ:SEQ + 1, :], ZROW[0:1, :]).then_inc(S.tab_st, 16)
            sp.wait_ge(S.tab_st, 32)

        @block.gpsimd
        def _(g):
            tb = TB.bitcast(I32).rearrange("p (r c) -> p r c", c=4)
            g.memset(ZROW[0:1, :], 0.0).then_inc(S.tab_init, 1)
            g.memset(TB.bitcast(I32), 0).then_inc(S.tab_init, 1)
            g.wait_ge(S.tab_init, 2)
            g.memset(tb[:, :, 0:1], SEQ).then_inc(S.tab_init, 1)
            g.memset(tb[:, :, 1:2], SKIP).then_inc(S.tab_init, 1)
            prime(g, S.ht_copied)
            with g.Fori(0, half) as i:
                for p in (0, 1):
                    t = 2 * i + p
                    g.wait_ge(S.hT_ready, done(t))
                    g.tensor_copy(HT[:, :, ds(t * P, P)], HC[p]).then_inc(S.ht_copied, 1)

        @block.scalar
        def _(act):
            def rms(p, n):
                act.wait_ge(x_ld[p], n)
                act.activation(junk, X[p], ACT.Square, accum_out=ss[:, p:p + 1])
                act.drain()
                rstd(act, rs[:, p:p + 1], ss[:, p:p + 1], D, e.eps_rms).then_inc(S.r_ready, 1)

            def body(i, p, last):
                t = 2 * i + p
                if not last:
                    rms(1 - p, 16 * i + 16 * (p + 1))
                act.wait_ge(S.qk_psum, done(t - 2))
                for n in range(3):
                    act.wait_ge(S.proj_psum, done(t, 3, n))
                    act.activation(Y[p][:, 512 * n:512 * n + 512], PP[n], ACT.Copy).then_inc(S.y_ready, 1)
                act.drain()
                act.wait_ge(S.qss_ready, done(t))
                rstd(act, qr, qss, HD, e.eps_rms).then_inc(S.qr_ready, 1)
                act.activation(cut(Z, t), Y[p][:, 3 * GW:4 * GW], ACT.Copy)
                act.activation(cut(V, t), Y[p][:, 2 * GW:3 * GW], ACT.Copy)
                act.drain()

            act.preload_act_table_set(LN_EXP)
            prime(act, S.r_ready, (S.y_ready, 3), S.qr_ready)
            act.wait_ge(S.row_ld, 16)
            rms(0, 16)
            with act.Fori(0, half - 1) as i:
                body(i, 0, False)
                body(i, 1, False)
            body(half - 1, 0, False)
            body(half - 1, 1, True)

        @block.tensor
        def _(pe):
            def transposes(p, t):
                pe.wait_ge(S.h_ready, done(t))
                pe.wait_ge(S.hT_ready, done(t - 1))
                for k in range(KD):
                    ins = pe.transpose(PH[:, k * P:(k + 1) * P], H[p][:, k * P:(k + 1) * P], e.ident)
                ins.then_inc(S.T_psum, 1)

            def body(i, p, last, first=False):
                t = 2 * i + p
                pe.wait_ge(S.hT_ready, done(t))
                for n in range(3):
                    if first:
                        pe.wait_ge((S.w_ld0, S.w_ld1, S.w_ld2)[n], 16)
                    pe.wait_ge(S.y_ready, done(t - 1, 3, n))
                    for k in range(KD):
                        ins = pe.matmul(PP[n], HC[p][:, k, :], W[:, k, 512 * n:512 * n + 512], start=k == 0, stop=k == KD - 1)
                    ins.then_inc(S.proj_psum, 1)
                pe.wait_ge(S.dt_done, done(t - 1))
                for k in range(KD):
                    ins = pe.matmul(PDT, HC[p][:, k, :], W[:, k, 4 * GW:TOK_COLS], start=k == 0, stop=k == KD - 1)
                ins.then_inc(S.dt_psum, 1)
                if not last:
                    transposes(1 - p, t + 1)
                pe.wait_ge(S.qn_ready, done(t))
                pe.wait_ge(S.qk_done, done(t - 1))
                for k in range(2 * GT):
                    ins = pe.transpose(PQK[:, k * P:(k + 1) * P], Y[p][:, k * P:(k + 1) * P], e.ident)
                ins.then_inc(S.qk_psum, 1)

            prime(pe, S.T_psum, (S.proj_psum, 3), S.dt_psum, S.qk_psum)
            pe.wait_ge(S.const_ld, 16)
            transposes(0, 0)
            body(0, 0, False, True)
            body(0, 1, False)
            with pe.Fori(1, half - 1) as i:
                body(i, 0, False)
                body(i, 1, False)
            body(half - 1, 0, False)
            body(half - 1, 1, True)

        @block.vector
        def _(v):
            def scale_h(p, t):
                v.wait_ge(S.r_ready, done(t))
                v.wait_ge(S.T_psum, done(t - 2))
                v.tensor_scalar(H[p], X[p], rs[:, p:p + 1], None, ALU.mult).then_inc(S.h_ready, 1)

            def evac_h(p, t):
                v.wait_ge(S.T_psum, done(t))
                v.wait_ge(S.ht_copied, done(t - 2))
                v.wait_ge(S.dt_psum, done(t - 2))
                v.tensor_tensor(HC[p], PH.rearrange("p (k n) -> p k n", n=P),
                                bc(e.pcol("g_mix", KD).unsqueeze(2), [P, KD, P]), ALU.mult).then_inc(S.hT_ready, 1)

            def body(i, p, last):
                t = 2 * i + p
                if not last:
                    scale_h(1 - p, t + 1)
                v.wait_ge(S.y_ready, done(t, 3, 1))
                v.tensor_tensor(SQ, Y[p][:, 0:2 * GW], Y[p][:, 0:2 * GW], ALU.mult)
                v.drain()
                v.tensor_reduce(qss, SQ.rearrange("p (h n) -> p h n", n=HD), AX, ALU.add).then_inc(S.qss_ready, 1)
                v.wait_ge(S.qr_ready, done(t))
                newton(v, qr, qss, qt, HD)
                yq = Y[p][:, 0:2 * GW].rearrange("p (h n) -> p h n", n=HD)
                v.tensor_tensor(yq, yq, bc(qr.unsqueeze(2), [P, 12, HD]), ALU.mult).then_inc(S.qn_ready, 1)
                if not last:
                    evac_h(1 - p, t + 1)
                v.wait_ge(S.dt_psum, done(t))
                v.tensor_tensor(cut(DT, t), PDT, e.rowp("dt_b", HEADS), ALU.add).then_inc(S.dt_done, 1)
                v.wait_ge(S.qk_psum, done(t))
                for n, (T, g) in enumerate(((QT, "att_q"), (KT, "att_k"))):
                    ins = v.tensor_scalar(T[:, :, ds(t * P, P)], PQK[:, n * GW:(n + 1) * GW].rearrange("p (k n) -> p k n", n=P),
                                          e.pcol(g, 1), None, ALU.mult)
                ins.then_inc(S.qk_done, 1)
                v.drain()

            prime(v, S.h_ready, S.hT_ready, S.qss_ready, S.qn_ready, S.qk_done, S.dt_done)
            v.wait_ge(S.par_ld, 16)
            v.wait_ge(S.row_ld, 16)
            v.tensor_scalar(e.pcol("att_q", 1), e.pcol("att_q", 1), HD ** -0.5, None, ALU.mult)
            v.tensor_scalar(e.pcol("ca_q", 2), e.pcol("ca_q", 2), CA_D ** -0.5, None, ALU.mult)
            v.drain()
            scale_h(0, 0)
            evac_h(0, 0)
            with v.Fori(0, half - 1) as i:
                body(i, 0, False)
                body(i, 1, False)
            body(half - 1, 0, False)
            body(half - 1, 1, True)


def phase_features(nc, e):
    A = e.A
    HT, Z = A(AT_HT, KD, SEQ), A(AT_Z, NT, GW)
    at = AT_B
    UP = A(at, GT, SEQ + 32); at += GT * (SEQ + 32)
    U2 = A(e.at_U2, GT, SEQ); YSC = A(e.at_YSC, GT, SEQ); XBC = A(e.at_XBC, XBC_T, SEQ)
    at = e.at_XBC + XBC_T * SEQ
    W = e.W_feat
    EG = A(at, SEQ); at += SEQ
    AS = A(at, SEQ); at += SEQ
    SP_ = A(at, SEQ + 4); at += SEQ + 4
    XR = [A(at + (SEQ + 4) * p, SEQ + 4) for p in (0, 1)]; at += 2 * (SEQ + 4)
    AC = [A(at + SEQ * p, SEQ) for p in (0, 1)]; at += 2 * SEQ
    assert at <= ARENA - 3 * D, at
    SCC, SCH, SCT = EG, AS, AC[0]
    CFP, SCP, SSP = CF_K - 1, SC_K - 1, SSD_K - 1
    S = e.sems("feat", "pads f_psum f_evac u_ready sc_done acc_ready silu_done")
    w_ld = e.feat_ld

    with nc.Block() as block:
        @block.sync
        def _(sp):
            def load(n, j):
                sp.wait_ge(S.f_psum, n + 1)
                sp.dma_start(W[j].rearrange("p k n -> p (k n)"), e.d.w_feat[ds(n, 1)].rearrange("o p n -> p (o n)")).then_inc(w_ld[j], 16)

            with sp.Fori(1, GT) as c:
                for j in range(2):
                    load(2 * c + j, j)
            with sp.Fori(0, GT) as c:
                for j in range(3):
                    load(2 * GT + 3 * c + j, j)
            with sp.Fori(0, XBC_T // 2) as i:
                for j in range(2):
                    load(5 * GT + 2 * i + j, j)
            load(NFEAT - 1, 0)

        @block.gpsimd
        def _(g):
            g.memset(UP[:, :, 0:CFP], 0.0)
            g.memset(SP_[:, 0:SCP], 0.0)
            for p in (0, 1):
                ins = g.memset(XR[p][:, 0:SSP], 0.0)
            g.drain()
            g.sem_inc(S.pads, 1)

        @block.tensor
        def _(pe):
            def tile(n, j, loads):
                pe.wait_ge(w_ld[j], loads)
                pe.wait_ge(S.f_evac, n + 1)
                for h in range(2):
                    for k in range(KD):
                        ins = pe.matmul(e.PS[:, 2 * j + h, :], W[j][:, k, :], HT[:, k, 512 * h:512 * h + 512], start=k == 0, stop=k == KD - 1)
                ins.then_inc(S.f_psum, 1)

            prime(pe, S.f_psum)
            with pe.Fori(0, GT) as c:
                for j in range(2):
                    tile(2 * c + j, j, 16 * c + 16)
            with pe.Fori(0, GT) as c:
                for j in range(3):
                    tile(2 * GT + 3 * c + j, j, 16 * c + 16 * (GT + 1 if j < 2 else 1))
            with pe.Fori(0, XBC_T // 2) as i:
                for j in range(2):
                    tile(5 * GT + 2 * i + j, j, 16 * i + 16 * (2 * GT + 1))
            tile(NFEAT - 1, 0, 16 * (2 * GT + 1 + XBC_T // 2))

        @block.scalar
        def _(act):
            def evac(n, j, out, func=ACT.Copy):
                act.wait_ge(S.f_psum, n + 3)
                act.activation(out, e.pair(j), func).then_inc(S.f_evac, 1)

            act.preload_act_table(ACT.Sigmoid)
            prime(act, S.f_evac, S.silu_done)
            with act.Fori(0, GT) as c:
                act.wait_ge(S.u_ready, done(c - 1))
                evac(2 * c, 0, AS)
                evac(2 * c + 1, 1, EG, ACT.Sigmoid)
            with act.Fori(0, GT) as c:
                act.wait_ge(S.u_ready, GT + 2)
                act.wait_ge(S.sc_done, done(c - 1))
                evac(2 * GT + 3 * c, 0, cut(YSC, c))
                evac(2 * GT + 3 * c + 1, 1, SCC)
                evac(2 * GT + 3 * c + 2, 2, SCH)
            act.drain()

            def xbc(m, i, j):
                act.wait_ge(S.acc_ready, done(m - 2))
                evac(5 * GT + m, j, XR[j][:, SSP:SSP + SEQ])
                act.wait_ge(S.acc_ready, done(m))
                act.activation(cut(XBC, m) if not isinstance(m, int) else XBC[:, m, :], AC[j], ACT.Silu).then_inc(S.silu_done, 1)

            act.preload_act_table(ACT.Silu)
            act.activation(Z, Z, ACT.Silu)
            with act.Fori(0, XBC_T // 2) as i:
                for j in range(2):
                    xbc(2 * i + j, i, j)
            xbc(XBC_T - 1, XBC_T // 2, 0)

        @block.vector
        def _(v):
            def taps(out, src, w, K):
                for k in range(1, K):
                    v.drain()
                    ins = v.scalar_tensor_tensor(out, src(k), w(k), out, ALU.mult, ALU.add)
                return ins

            def col(name, at):
                return e.par[:, ds(PC[name] + at, 1)]

            prime(v, S.u_ready, S.sc_done, S.acc_ready)
            v.wait_ge(S.pads, 1)

            def gate(c):
                v.wait_ge(S.f_evac, 2 * c + 4)
                v.tensor_tensor(UP[:, ds(c, 1), CFP:CFP + SEQ].rearrange("p o n -> p (o n)"), AS, EG, ALU.mult).then_inc(S.u_ready, 1)
                v.drain()

            def conv_cf(c):
                u = lambda k: UP[:, ds(c, 1), k:k + SEQ].rearrange("p o n -> p (o n)")
                v.tensor_scalar(cut(U2, c), u(0), col("cf_w", c * CF_K), col("cf_b", c), ALU.mult, ALU.add)
                taps(cut(U2, c), u, lambda k: col("cf_w", c * CF_K + k), CF_K)
                v.drain()

            gate(0)
            with v.Fori(1, GT) as c:
                gate(c)
                conv_cf(c - 1)

            def short(c):
                v.wait_ge(S.f_evac, 2 * GT + 3 * c + 5)
                v.tensor_tensor(SP_[:, SCP:SCP + SEQ], SCC, SCH, ALU.mult)
                v.drain()
                v.tensor_scalar(SCT, SP_[:, 0:SEQ], col("sc_w", c * SC_K), None, ALU.mult)
                taps(SCT, lambda k: SP_[:, k:k + SEQ], lambda k: col("sc_w", c * SC_K + k), SC_K)
                v.drain()
                v.tensor_tensor(cut(YSC, c), cut(YSC, c), SCT, ALU.mult).then_inc(S.sc_done, 1)
                v.drain()

            short(0)
            conv_cf(GT - 1)
            with v.Fori(1, GT) as c:
                short(c)

            def xbc(m, j):
                v.wait_ge(S.f_evac, 5 * GT + m + 3)
                v.wait_ge(S.silu_done, done(m - 2))
                v.tensor_scalar(AC[j], XR[j][:, 0:SEQ], col("ssd_w", m * SSD_K), col("ssd_b", m), ALU.mult, ALU.add)
                taps(AC[j], lambda k: XR[j][:, k:k + SEQ], lambda k: col("ssd_w", m * SSD_K + k), SSD_K).then_inc(S.acc_ready, 1)
                v.drain()

            with v.Fori(0, XBC_T // 2) as i:
                for j in range(2):
                    xbc(2 * i + j, j)
            xbc(XBC_T - 1, 0)


def phase_ssd(nc, e):
    A = e.A
    XBC = A(e.at_XBC, XBC_T, SEQ)
    Z, DT = A(AT_Z, NT, GW), A(AT_DT, NT, HEADS)
    Y_T = A(e.at_CAT_SSD, GT, SEQ)
    at = e.at_XBC + XBC_T * SEQ
    XC = [A(at + 896 * p, XBC_T, P) for p in (0, 1)]; at += 1792
    XB = A(at, 640); at += 640
    RD = A(at, HEADS, P); at += 768
    EX = A(at, HEADS, P); at += 768
    MT = A(at, HEADS, P); at += 768
    CB = A(at, SSD_NG, P); at += 256
    XDT = A(at, HEADS, HD); at += GW
    XDD = A(at, HEADS, HD); at += GW
    Y = A(at, HEADS, HD); at += GW
    T2 = A(at, HEADS, HD); at += GW
    YN = A(at, GW); at += GW
    ST = A(at, HEADS, HD); at += GW
    TS = A(at, NT, HEADS); at += 48
    DA = A(at, NT, HEADS); at += 48
    AN = A(at, HEADS); at += 8
    CS = A(at, 3, HEADS); at += 24
    ssy, ry = A(at, 1), A(at + 1, 1); at += 2
    assert at <= ARENA
    S = e.sems("ssd", "dt_abs dt_exp dt_one dt_ln a_exp da_ready xc_ready tr_psum xb_ready rd_ready cb_psum cb_read d_psum d_exp "
               "cs_exp mt_ready xdt_ready xdd_ready y_psum yo_psum st_psum y_read st_ready ss_ready r_ready yn_ready yT_psum yT_done")
    PTR = e.PS[:, 0:2, :].rearrange("p a b -> p (a b)")[:, 0:640]
    PYT = e.PS[:, 1, P:P + GW]
    PCB = e.PS[:, 2, 0:SSD_NG * P]
    PCS = e.PS[:, 7, GW:GW + 3 * HEADS]
    PDD = e.PS[:, 3:5, 0:GW]
    PY, PYO, PST = e.PS[:, 5, 0:GW], e.PS[:, 6, 0:GW], e.PS[:, 7, 0:GW]
    JG = HEADS // SSD_NG
    JW = JG * HD

    with nc.Block() as block:
        @block.sync
        def _(sp):
            pass

        @block.gpsimd
        def _(g):
            prime(g, S.xc_ready)
            with g.Fori(0, NT // 2) as i:
                for p in (0, 1):
                    c = 2 * i + p
                    g.wait_ge(S.st_psum, done(c - 2))
                    g.tensor_copy(XC[p], XBC[:, :, ds(c * P, P)]).then_inc(S.xc_ready, 1)

        @block.scalar
        def _(act):
            act.preload_act_table_set(LN_EXP)
            act.wait_ge(S.dt_abs, 1)
            act.activation(TS, TS, ACT.Exp, scale=-1.0).then_inc(S.dt_exp, 1)
            act.activation(AN, e.rowp("a_log", HEADS), ACT.Exp).then_inc(S.a_exp, 1)
            act.wait_ge(S.dt_one, 1)
            act.activation(TS, TS, ACT.Ln).then_inc(S.dt_ln, 1)
            prime(act, S.xb_ready, S.d_exp, S.cs_exp, S.r_ready)
            with act.Fori(0, NT) as c:
                act.wait_ge(S.tr_psum, done(c))
                act.wait_ge(S.y_read, done(c - 1))
                act.wait_ge(S.st_psum, done(c - 1))
                act.activation(XB, PTR, ACT.Copy).then_inc(S.xb_ready, 1)
                act.wait_ge(S.cb_psum, done(c))
                act.activation(CS.rearrange("p a h -> p (a h)"), PCS, ACT.Exp).then_inc(S.cs_exp, 1)
                act.wait_ge(S.d_psum, done(c))
                act.wait_ge(S.mt_ready, done(c - 1))
                act.activation(EX.rearrange("p (a h) n -> p a (h n)", a=2), PDD, ACT.Exp).then_inc(S.d_exp, 1)
                act.wait_ge(S.ss_ready, done(c))
                rstd(act, ry, ssy, GW, e.eps_rms).then_inc(S.r_ready, 1)

        @block.tensor
        def _(pe):
            prime(pe, S.tr_psum, S.cb_psum, S.d_psum, S.y_psum, S.yo_psum, S.st_psum, S.yT_psum)

            def y_transposed(c, last=False):
                pe.wait_ge(S.yn_ready, done(c))
                pe.wait_ge(S.yT_done, done(c - 1))
                if not last:
                    pe.wait_ge(S.xb_ready, done(c + 1))
                for k in range(GT):
                    ins = pe.transpose(PYT[:, k * P:(k + 1) * P], YN[:, k * P:(k + 1) * P], e.ident)
                ins.then_inc(S.yT_psum, 1)

            def body(c, p, first):
                pe.wait_ge(S.xc_ready, done(c))
                pe.wait_ge(S.xb_ready, done(c - 1))
                pe.wait_ge(S.yT_done, done(c - 2))
                for k in range(5):
                    ins = pe.transpose(PTR[:, k * P:(k + 1) * P], XC[p][:, k, :], e.ident)
                ins.then_inc(S.tr_psum, 1)
                pe.wait_ge(S.cb_read, done(c - 1))
                pe.wait_ge(S.st_ready, done(c - 1))
                for g in range(SSD_NG):
                    pe.matmul(PCB[:, g * P:(g + 1) * P], XC[p][:, 3 + g, :], XC[p][:, 5 + g, :], start=True, stop=True)
                for n, m in enumerate((e.tri_le, e.tri_gt, e.ones)):
                    ins = pe.matmul(PCS[:, n * HEADS:(n + 1) * HEADS], m, cut(DA, c), start=True, stop=True)
                ins.then_inc(S.cb_psum, 1)
                pe.wait_ge(S.rd_ready, done(c))
                pe.wait_ge(S.d_exp, done(c - 1))
                for n in range(2):
                    ins = pe.matmul(PDD[:, n, :], e.tri_gt, RD[:, 3 * n:3 * n + 3, :].rearrange("p h n -> p (h n)"), start=True, stop=True)
                ins.then_inc(S.d_psum, 1)
                if not first:
                    y_transposed(c - 1)
                pe.wait_ge(S.y_read, done(c - 1))
                for g in range(SSD_NG):
                    ins = pe.matmul(PYO[:, g * JW:(g + 1) * JW], XC[p][:, 5 + g, :], ST[:, g * JG:(g + 1) * JG, :].rearrange("p h n -> p (h n)"), start=True, stop=True)
                ins.then_inc(S.yo_psum, 1)
                pe.wait_ge(S.mt_ready, done(c))
                pe.wait_ge(S.xdt_ready, done(c))
                for h in range(HEADS):
                    ins = pe.matmul(PY[:, h * HD:(h + 1) * HD], MT[:, h, :], XDT[:, h, :], start=True, stop=True)
                ins.then_inc(S.y_psum, 1)
                pe.wait_ge(S.xdd_ready, done(c))
                for g in range(SSD_NG):
                    ins = pe.matmul(PST[:, g * JW:(g + 1) * JW], XB[:, GW + g * P:GW + (g + 1) * P], XDD[:, g * JG:(g + 1) * JG, :].rearrange("p h n -> p (h n)"), start=True, stop=True)
                ins.then_inc(S.st_psum, 1)

            body(0, 0, True)
            body(1, 1, False)
            with pe.Fori(1, NT // 2) as i:
                for p in (0, 1):
                    body(2 * i + p, p, False)
            y_transposed(NT - 1, True)

        @block.vector
        def _(v):
            v.tensor_scalar(TS, DT, -1.0, None, ALU.mult)
            v.drain()
            v.tensor_tensor(TS, TS, DT, ALU.max).then_inc(S.dt_abs, 1)
            v.wait_ge(S.dt_exp, 1)
            v.tensor_scalar(TS, TS, 1.0, None, ALU.add).then_inc(S.dt_one, 1)
            v.wait_ge(S.dt_ln, 1)
            v.tensor_scalar(DT, DT, 0.0, None, ALU.max)
            v.drain()
            v.tensor_tensor(DT, DT, TS, ALU.add)
            v.wait_ge(S.a_exp, 1)
            v.tensor_scalar(AN, AN, -1.0, None, ALU.mult)
            v.memset(ST, 0.0)
            v.drain()
            v.tensor_tensor(DA, DT, bc(AN.unsqueeze(1), [P, NT, HEADS]), ALU.mult)
            v.drain()
            prime(v, S.rd_ready, S.cb_read, S.mt_ready, S.xdt_ready, S.xdd_ready, S.y_read, S.st_ready, S.ss_ready, S.yn_ready, S.yT_done)
            per_head = lambda ap, n: bc(ap.unsqueeze(2), [P, HEADS, n])

            def y_normed(c):
                v.wait_ge(S.r_ready, done(c))
                v.tensor_scalar(YN, Y.rearrange("p h n -> p (h n)"), ry, None, ALU.mult).then_inc(S.yn_ready, 1)

            def y_out(c):
                v.wait_ge(S.yT_psum, done(c))
                v.tensor_tensor(Y_T[:, :, ds(c * P, P)], PYT.rearrange("p (k n) -> p k n", n=P), bc(e.pcol("ssd_g", GT).unsqueeze(2), [P, GT, P]), ALU.mult).then_inc(S.yT_done, 1)

            def body(c, first):
                v.tensor_tensor(RD, bc(e.tri_le.unsqueeze(1), [P, HEADS, P]), per_head(cut(DA, c), P), ALU.mult).then_inc(S.rd_ready, 1)
                v.wait_ge(S.cb_psum, done(c))
                v.tensor_tensor(CB, PCB.rearrange("p (g n) -> p g n", n=P), bc(e.tri_le.unsqueeze(1), [P, SSD_NG, P]), ALU.mult).then_inc(S.cb_read, 1)
                if not first:
                    y_normed(c - 1)
                xs = XB[:, 0:GW].rearrange("p (h n) -> p h n", n=HD)
                v.wait_ge(S.xb_ready, done(c))
                v.wait_ge(S.y_psum, done(c - 1))
                v.tensor_tensor(XDT, xs, per_head(cut(DT, c), HD), ALU.mult).then_inc(S.xdt_ready, 1)
                v.drain()
                v.wait_ge(S.d_exp, done(c))
                for g in range(SSD_NG):
                    ins = v.tensor_tensor(MT[:, g * JG:(g + 1) * JG, :], EX[:, g * JG:(g + 1) * JG, :], bc(CB[:, g:g + 1, :], [P, JG, P]), ALU.mult)
                ins.then_inc(S.mt_ready, 1)
                if not first:
                    y_out(c - 1)
                v.wait_ge(S.cs_exp, done(c))
                v.wait_ge(S.st_psum, done(c - 1))
                v.tensor_tensor(XDD, XDT, per_head(CS[:, 1, :], HD), ALU.mult).then_inc(S.xdd_ready, 1)
                v.wait_ge(S.yo_psum, done(c))
                v.tensor_tensor(Y, PYO.rearrange("p (h n) -> p h n", n=HD), per_head(CS[:, 0, :], HD), ALU.mult)
                v.tensor_tensor(T2, xs, per_head(e.rowp("ssd_d", HEADS), HD), ALU.mult)
                v.drain()
                v.wait_ge(S.y_psum, done(c))
                v.tensor_tensor(Y, Y, PY.rearrange("p (h n) -> p h n", n=HD), ALU.add)
                v.drain()
                v.tensor_tensor(Y, Y, T2, ALU.add).then_inc(S.y_read, 1)
                v.tensor_tensor(ST, ST, per_head(CS[:, 2, :], HD), ALU.mult)
                v.drain()
                v.wait_ge(S.st_psum, done(c))
                v.tensor_tensor(ST, ST, PST.rearrange("p (h n) -> p h n", n=HD), ALU.add).then_inc(S.st_ready, 1)
                y = Y.rearrange("p h n -> p (h n)")
                v.tensor_tensor(y, y, cut(Z, c), ALU.mult)
                v.drain()
                v.wait_ge(S.yT_psum, done(c - 1))
                v.tensor_tensor_reduce(YN, y, y, 1.0, 0.0, ALU.mult, ALU.add, ssy).then_inc(S.ss_ready, 1)
                v.drain()

            body(0, True)
            with v.Fori(1, NT) as c:
                body(c, False)
            y_normed(NT - 1)
            y_out(NT - 1)


def phase_attention(nc, e):
    A = e.A
    QT, KT, V = A(AT_QT, GT, SEQ), A(AT_KT, GT, SEQ), A(AT_V, NT, GW)
    at = e.at_XBC
    ATT = A(at, NT, GW); at += NT * GW
    QP = A(at, SEQ); at += SEQ
    KP = A(at, SEQ); at += SEQ
    VP = A(at, NT, P); at += SEQ
    SM = [A(at + SEQ * p, SEQ) for p in (0, 1)]; at += 2 * SEQ
    PR = [A(at + SEQ * p, SEQ) for p in (0, 1)]; at += 2 * SEQ
    PT = [A(at + SEQ * p, SEQ) for p in (0, 1)]; at += 2 * SEQ
    mx = A(at, 2); den = A(at + 2, 8); rden = A(at + 10, 2); at += 12
    assert at <= ARENA
    S = e.sems("att", "settled qk_ready v_ready s_psum m_ready p_ready t_psum pt_ready o_psum o_read")
    PSS = [e.pair(0), e.pair(1)]
    PTT = e.pair(2)
    PO = [e.PS[:, 6, 0:HD], e.PS[:, 7, 0:HD]]
    NS = 2 * NT
    e.ATT = ATT

    with nc.Block() as block:
        @block.sync
        def _(sp):
            pass

        @block.gpsimd
        def _(g):
            with g.Fori(0, HEADS // 2) as j:
                g.wait_ge(S.s_psum, NS * j + 2)
                g.tensor_copy(QP, cut(QT, j)).then_inc(S.qk_ready, 1)
                g.tensor_copy(KP, cut(KT, j)).then_inc(S.qk_ready, 1)
                g.wait_ge(S.o_psum, NS * j + 2)
                g.tensor_copy(VP, V[:, :, ds(j * P, P)]).then_inc(S.v_ready, 1)

        @block.tensor
        def _(pe):
            def scores(j, s):
                h, i, p = s // NT, s % NT, s % 2
                g = NS * j + s
                pe.wait_ge(S.m_ready, done(g - 2))
                rows = slice(h * HD, (h + 1) * HD)
                n = (i + 1) * P
                for a in range(0, n, 512):
                    b = min(n, a + 512)
                    ins = pe.matmul(PSS[p][:, a:b], QP[rows, i * P:(i + 1) * P], KP[rows, a:b], start=True, stop=True)
                ins.then_inc(S.s_psum, 1)

            def transposes(j, s):
                i, p = s % NT, s % 2
                g = NS * j + s
                pe.wait_ge(S.p_ready, done(g))
                pe.wait_ge(S.pt_ready, done(g - 1))
                for k in range(i + 1):
                    ins = pe.transpose(PTT[:, k * P:(k + 1) * P], PR[p][:, k * P:(k + 1) * P], e.ident)
                ins.then_inc(S.t_psum, 1)

            def values(j, s):
                h, i, p = s // NT, s % NT, s % 2
                g = NS * j + s
                pe.wait_ge(S.pt_ready, done(g))
                pe.wait_ge(S.o_read, g + 7)
                for k in range(i + 1):
                    ins = pe.matmul(PO[p], PT[p][:, k * P:(k + 1) * P], VP[:, k, h * HD:(h + 1) * HD], start=k == 0, stop=k == i)
                ins.then_inc(S.o_psum, 1)

            prime(pe, S.s_psum, S.t_psum, S.o_psum)
            with pe.Fori(0, HEADS // 2) as j:
                pe.wait_ge(S.qk_ready, 2 * j + 2)
                for s in range(NS + 3):
                    if s < NS:
                        scores(j, s)
                    if 0 <= s - 2 < NS:
                        transposes(j, s - 2)
                    if s == 3:
                        pe.wait_ge(S.v_ready, j + 1)
                    if s >= 3:
                        values(j, s - 3)

        @block.vector
        def _(v):
            def maximum(j, s):
                i, p = s % NT, s % 2
                g = NS * j + s
                n = (i + 1) * P
                v.wait_ge(S.s_psum, done(g))
                v.wait_ge(S.p_ready, done(g - 2))
                v.sem_inc(S.settled, 1)
                v.tensor_tensor_reduce(SM[p][:, 0:n], PSS[p][:, 0:n], e.mask[:, SEQ - n:SEQ], 1.0, -BIG, ALU.add, ALU.max, mx[:, p:p + 1])
                v.drain()
                v.tensor_scalar(mx[:, p:p + 1], mx[:, p:p + 1], -1.0, None, ALU.mult).then_inc(S.m_ready, 1)

            def output(j, s):
                h, i, p = s // NT, s % NT, s % 2
                g = NS * j + s
                v.wait_ge(S.o_psum, done(g))
                v.reciprocal(rden[:, p:p + 1], den[:, s % 8:s % 8 + 1])
                v.drain()
                v.tensor_scalar(ATT[:, i, ds(j * P + h * HD, HD)], PO[p], rden[:, p:p + 1], None, ALU.mult).then_inc(S.o_read, 1)

            prime(v, S.m_ready)
            v.sem_inc(S.o_read, 8)
            with v.Fori(0, HEADS // 2) as j:
                for s in range(NS + 4):
                    if s < NS:
                        maximum(j, s)
                    if s >= 4:
                        output(j, s - 4)
                v.drain()

        @block.scalar
        def _(act):
            def probs(j, s):
                i, p = s % NT, s % 2
                g = NS * j + s
                n = (i + 1) * P
                act.wait_ge(S.m_ready, done(g))
                act.wait_ge(S.t_psum, done(g - 2))
                act.wait_ge(S.o_read, g + 1)
                act.activation(PR[p][:, 0:n], SM[p][:, 0:n], ACT.Exp, bias=mx[:, p:p + 1],
                               accum_out=den[:, s % 8:s % 8 + 1]).then_inc(S.p_ready, 1)

            def copy_out(j, s):
                i, p = s % NT, s % 2
                g = NS * j + s
                n = (i + 1) * P
                act.wait_ge(S.t_psum, done(g))
                act.wait_ge(S.o_psum, done(g - 2))
                act.activation(PT[p][:, 0:n], PTT[:, 0:n], ACT.Copy).then_inc(S.pt_ready, 1)

            prime(act, S.p_ready, S.pt_ready)
            with act.Fori(0, HEADS // 2) as j:
                for s in range(NS + 2):
                    if s >= 2:
                        copy_out(j, s - 2)
                    if s < NS:
                        probs(j, s)


def phase_norm_cf(nc, e):
    A = e.A
    U2 = A(e.at_U2, GT, SEQ)
    CF = A(e.at_CAT_CF, GT, SEQ)
    AT_T = A(e.at_CAT_ATT, GT, SEQ)
    ATT = e.ATT
    at = AT_QT
    XC = A(at, GT, SEQ); at += GT * SEQ
    SQ = A(at, GT, SEQ); at += GT * SEQ
    R = A(at, SEQ); at += SEQ
    assert at <= AT_Z
    e.W_out = A(e.at_XBC + NT * GW, len(e.CAT) * GT, D)
    e.XI = [A(e.at_work_out + D * p, D) for p in (0, 1)]
    e.out_ld = e.sems("out_ld", "w_ld x_ld0 x_ld1")
    S = e.sems("cf", "mu_psum xc_ready sq_ready var_psum r_ready n_ready at_psum at_done")
    with nc.Block() as block:
        @block.sync
        def _(sp):
            sp.dma_start(e.W_out, e.d.w_out.rearrange("(k p) n -> p k n", p=P)).then_inc(e.out_ld.w_ld, 16)
            for p in (0, 1):
                sp.dma_start(e.XI[p], e.d.x[p * P:(p + 1) * P, :]).then_inc((e.out_ld.x_ld0, e.out_ld.x_ld1)[p], 16)

        @block.gpsimd
        def _(g):
            pass

        @block.tensor
        def _(pe):
            for h in range(2):
                for k in range(GT):
                    ins = pe.matmul(e.PS[:, h, :], e.ones, U2[:, k, 512 * h:512 * h + 512], start=k == 0, stop=k == GT - 1)
            ins.then_inc(S.mu_psum, 1)
            for t in range(NT):
                q = 4 + t % 4
                if t >= 4:
                    pe.wait_ge(S.at_done, t - 3)
                for k in range(GT):
                    ins = pe.transpose(e.PS[:, q, k * P:(k + 1) * P], ATT[:, t, k * P:(k + 1) * P], e.ident)
                ins.then_inc(S.at_psum, 1)
            pe.wait_ge(S.sq_ready, 1)
            for h in range(2):
                for k in range(GT):
                    ins = pe.matmul(e.PS[:, 2 + h, :], e.ones, SQ[:, k, 512 * h:512 * h + 512], start=k == 0, stop=k == GT - 1)
            ins.then_inc(S.var_psum, 1)

        @block.vector
        def _(v):
            v.wait_ge(S.mu_psum, 1)
            for k in range(GT):
                v.scalar_tensor_tensor(XC[:, k, :], e.pair(0), -1.0 / GW, U2[:, k, :], ALU.mult, ALU.add)
            v.drain()
            v.tensor_tensor(SQ, XC, XC, ALU.mult).then_inc(S.sq_ready, 1)
            v.wait_ge(S.r_ready, 1)
            v.tensor_tensor(XC, XC, bc(R.unsqueeze(1), [P, GT, SEQ]), ALU.mult)
            v.drain()
            v.sem_inc(S.n_ready, 1)

        @block.scalar
        def _(act):
            for t in range(NT):
                act.wait_ge(S.at_psum, t + 1)
                act.activation(AT_T[:, :, t * P:(t + 1) * P], e.PS[:, 4 + t % 4, 0:GW].rearrange("p (k n) -> p k n", n=P), ACT.Copy).then_inc(S.at_done, 1)
            act.wait_ge(S.var_psum, 1)
            rstd(act, R, e.pair(1), GW, e.eps_ln).then_inc(S.r_ready, 1)
            act.wait_ge(S.n_ready, 1)
            act.preload_act_table(ACT.Silu)
            for k in range(GT):
                act.activation(CF[:, k, :], XC[:, k, :], ACT.Silu, scale=e.pcol("ln_g", GT)[:, k:k + 1], bias=e.pcol("ln_b", GT)[:, k:k + 1])


def phase_out(nc, e):
    A = e.A
    X1 = A(e.at_X1, NT, D)
    CAT = e.CAT
    NC = len(CAT) * GT
    W, XI = e.W_out, e.XI
    CC = [A(e.at_work_out + 2 * D + NC * P * p, NC, P) for p in (0, 1)]
    S = e.sems("out", "cc_ready o_psum x1_ready")
    x_ld = [e.out_ld.x_ld0, e.out_ld.x_ld1]
    e.W_mem, e.X_mem = A(e.at_ca, KD, 512), [A(e.at_X1 - 2 * D + D * p, D) for p in (0, 1)]
    e.mem_ld = e.sems("mem_ld", "x_ld w_ld0")
    with nc.Block() as block:
        @block.sync
        def _(sp):
            for p in (0, 1):
                sp.dma_start(e.X_mem[p], e.d.mem[p * P:(p + 1) * P, :]).then_inc(e.mem_ld.x_ld, 16)
            sp.dma_start(e.W_mem, e.d.ca_wkv.rearrange("(k p) n -> p k n", p=P)[:, :, 0:512]).then_inc(e.mem_ld.w_ld0, 16)
            with sp.Fori(1, NT // 2) as i:
                for p in (0, 1):
                    t = 2 * i + p
                    sp.wait_ge(S.x1_ready, done(t - 2))
                    sp.dma_start(XI[p], e.d.x[ds(t * P, P), :]).then_inc(x_ld[p], 16)

        @block.gpsimd
        def _(g):
            prime(g, (S.cc_ready, len(CAT)))
            with g.Fori(0, NT // 2) as i:
                for p in (0, 1):
                    t = 2 * i + p
                    g.wait_ge(S.o_psum, done(t - 2))
                    for n, c in enumerate(CAT):
                        g.tensor_copy(CC[p][:, n * GT:(n + 1) * GT, :], c[:, :, ds(t * P, P)]).then_inc(S.cc_ready, 1)

        @block.scalar
        def _(act):
            pass

        @block.tensor
        def _(pe):
            prime(pe, S.o_psum)
            pe.wait_ge(e.out_ld.w_ld, 16)
            with pe.Fori(0, NT // 2) as i:
                for p in (0, 1):
                    t = 2 * i + p
                    pe.wait_ge(S.cc_ready, done(t, len(CAT)))
                    pe.wait_ge(S.x1_ready, done(t - 2))
                    for h in range(2):
                        for k in range(NC):
                            ins = pe.matmul(e.PS[:, 2 * p + h, :], CC[p][:, k, :], W[:, k, 512 * h:512 * h + 512], start=k == 0, stop=k == NC - 1)
                    ins.then_inc(S.o_psum, 1)

        @block.vector
        def _(v):
            prime(v, S.x1_ready)
            with v.Fori(0, NT // 2) as i:
                for p in (0, 1):
                    t = 2 * i + p
                    v.wait_ge(S.o_psum, done(t))
                    v.wait_ge(x_ld[p], 16 * i + 16)
                    v.tensor_tensor(cut(X1, t), e.pair(p), XI[p], ALU.add).then_inc(S.x1_ready, 1)


def phase_memory(nc, e):
    A = e.A
    KM, VM = A(e.at_KM, KD, MEM), A(e.at_VM, 2, D)
    at = ARENA - KD * (2 * D + NG + NE)
    e.ca = A(at, KD, D), A(at + KD * D, KD, D), A(at + 2 * KD * D, KD, NG + NE)
    WQ, WO, WR = e.ca
    e.end_ca = at
    at = e.at_ca
    W, X = [e.W_mem, A(at + 4096, KD, 512)], e.X_mem; at += 8192
    H = [A(at + D * p, D) for p in (0, 1)]; at += 2 * D
    MT = A(at, KD, MEM); at += KD * MEM
    K = [A(at + D * p, D) for p in (0, 1)]; at += 2 * D
    SQ = A(at, D); at += D
    ss, rs = A(at, 2), A(at + 2, 2)
    ks, kr, kt = [A(at + 4 + 12 * p, 4) for p in (0, 1)], [A(at + 8 + 12 * p, 4) for p in (0, 1)], A(at + 28, 4)
    assert at + 32 <= e.end_ca
    S = e.sems("mem", "w_ld1 r_ready h_ready T_psum mT_ready kv_psum kv_out kss_ready kr_ready kn_ready kT_psum kT_done")
    w_ld = [e.mem_ld.w_ld0, S.w_ld1]
    e.ca_ld = e.sems("ca_ld", "wq_ld wo_ld wr_ld")
    with nc.Block() as block:
        @block.sync
        def _(sp):
            for n in range(1, 4):
                if n >= 2:
                    sp.wait_ge(S.kv_psum, 2 * (n - 2) + 2)
                sp.dma_start(W[n % 2], e.d.ca_wkv.rearrange("(k p) n -> p k n", p=P)[:, :, 512 * n:512 * n + 512]).then_inc(w_ld[n % 2], 16)

        @block.gpsimd
        def _(g):
            g.dma_start(WR[:, :, 0:NG], e.d.wg.rearrange("(k p) n -> p k n", p=P)).then_inc(e.ca_ld.wr_ld, 16)
            g.dma_start(WR[:, :, NG:], e.d.we.rearrange("(k p) n -> p k n", p=P)).then_inc(e.ca_ld.wr_ld, 16)
            g.wait_ge(w_ld[1], 16)
            g.dma_start(WQ, e.d.ca_wq.rearrange("(k p) n -> p k n", p=P)).then_inc(e.ca_ld.wq_ld, 16)
            g.dma_start(WO, e.d.ca_wo.rearrange("(k p) n -> p k n", p=P)).then_inc(e.ca_ld.wo_ld, 16)

        @block.scalar
        def _(act):
            act.preload_act_table_set(LN_EXP)
            act.wait_ge(e.mem_ld.x_ld, 32)
            for p in (0, 1):
                act.activation(SQ, X[p], ACT.Square, accum_out=ss[:, p:p + 1])
                act.drain()
            rstd(act, rs, ss, D, e.eps_rms).then_inc(S.r_ready, 1)
            for n in range(4):
                for m in range(2):
                    act.wait_ge(S.kv_psum, 2 * n + m + 1)
                    out = K[m][:, 512 * n:512 * n + 512] if n < 2 else VM[:, m, 512 * (n - 2):512 * (n - 1)]
                    act.activation(out, e.PS[:, 4 + (2 * n + m) % 2, :], ACT.Copy).then_inc(S.kv_out, 1)
            for m in range(2):
                act.wait_ge(S.kss_ready, m + 1)
                rstd(act, kr[m], ks[m], CA_D, e.eps_rms).then_inc(S.kr_ready, 1)

        @block.tensor
        def _(pe):
            for m in range(2):
                pe.wait_ge(S.h_ready, m + 1)
                for k in range(KD):
                    ins = pe.transpose(e.pair(m)[:, k * P:(k + 1) * P], H[m][:, k * P:(k + 1) * P], e.ident)
                ins.then_inc(S.T_psum, 1)
            pe.wait_ge(S.mT_ready, 2)
            for n in range(4):
                pe.wait_ge(w_ld[n % 2], 16 * (n // 2) + 16)
                for m in range(2):
                    if 2 * n + m >= 2:
                        pe.wait_ge(S.kv_out, 2 * n + m - 1)
                    for k in range(KD):
                        ins = pe.matmul(e.PS[:, 4 + (2 * n + m) % 2, :], MT[:, k, m * P:(m + 1) * P], W[n % 2][:, k, :], start=k == 0, stop=k == KD - 1)
                    ins.then_inc(S.kv_psum, 1)
            for m in range(2):
                pe.wait_ge(S.kn_ready, m + 1)
                for k in range(KD):
                    ins = pe.transpose(e.pair(m)[:, k * P:(k + 1) * P], K[m][:, k * P:(k + 1) * P], e.ident)
                ins.then_inc(S.kT_psum, 1)

        @block.vector
        def _(v):
            v.wait_ge(S.r_ready, 1)
            for m in range(2):
                v.tensor_scalar(H[m], X[m], rs[:, m:m + 1], None, ALU.mult).then_inc(S.h_ready, 1)
            for m in range(2):
                v.wait_ge(S.T_psum, m + 1)
                v.tensor_tensor(MT[:, :, m * P:(m + 1) * P], e.pair(m).rearrange("p (k n) -> p k n", n=P),
                                bc(e.pcol("g_mem", KD).unsqueeze(2), [P, KD, P]), ALU.mult).then_inc(S.mT_ready, 1)
            v.wait_ge(S.kv_out, 4)
            for m in range(2):
                v.drain()
                v.tensor_tensor(H[m], K[m], K[m], ALU.mult)
                v.drain()
                v.tensor_reduce(ks[m], H[m].rearrange("p (h n) -> p h n", n=CA_D), AX, ALU.add).then_inc(S.kss_ready, 1)
                v.wait_ge(S.kr_ready, m + 1)
                newton(v, kr[m], ks[m], kt, CA_D)
                kh = K[m].rearrange("p (h n) -> p h n", n=CA_D)
                v.tensor_tensor(kh, kh, bc(kr[m].unsqueeze(2), [P, CA_H, CA_D]), ALU.mult).then_inc(S.kn_ready, 1)
            for m in range(2):
                v.wait_ge(S.kT_psum, m + 1)
                for q in range(2):
                    v.tensor_scalar(KM.rearrange("p (h q) m -> p q h m", q=2)[:, q, :, m * P:(m + 1) * P],
                                    e.pair(m).rearrange("p (h q n) -> p q h n", q=2, n=P)[:, q], e.pcol("ca_k", 2)[:, q:q + 1], None, ALU.mult)


def phase_cross(nc, e):
    A = e.A
    X1, KM, VM = A(e.at_X1, NT, D), A(e.at_KM, KD, MEM), A(e.at_VM, 2, D)
    LG = A(e.at_LG, NT, NG + NE)
    WQ, WO, WR = e.ca
    at = e.at_ca
    H = A(at, D); at += D
    HT = A(at, KD, P); at += D
    Q = A(at, D); at += D
    SQ = A(at, D); at += D
    QT = A(at, KD, P); at += D
    PR = A(at, D); at += D
    PT = A(at, KD, P); at += D
    O = A(at, D); at += D
    OT = A(at, KD, P); at += D
    H3 = [A(at + D * p, D) for p in (0, 1)]; at += 2 * D
    RT = A(at, KD, P); at += D
    junk = A(at, D); at += D
    ss, rs, ss3, rs3 = A(at, 1), A(at + 1, 1), A(at + 2, 1), A(at + 3, 1)
    qs, qr, qt, mx, den = (A(at + 4 + 4 * n, 4) for n in range(5))
    assert at + 32 <= e.end_ca, at
    S = e.sems("ca", "settled r_ready h_ready hT_psum hT_ready qa_psum q_psum q_out qss_ready qr_ready qn_ready qT_psum qT_ready "
               "s_psum sm_ready p_ready den_ready pT_psum pT_ready o_psum on_ready oT_psum oT_ready wo_psum x_ready r3_ready h3_ready "
               "h3T_psum h3T_ready lg_psum lg_done h3_st0 h3_st1")
    h3_st = [S.h3_st0, S.h3_st1]
    heads = lambda ap: ap.rearrange("p (h n) -> p h n", n=CA_D)
    T_, Q_, S_, W_ = e.pair(0), e.pair(1), e.pair(2), e.pair(3)

    def steps(eng, start, body):
        start()
        with eng.Fori(0, NT // 2 - 1) as i:
            for p in (0, 1):
                body(2 * i + p, p, i, True, True)
        body(NT - 2, 0, NT // 2 - 1, True, False)
        body(NT - 1, 1, NT // 2 - 1, False, False)

    with nc.Block() as block:
        @block.sync
        def _(sp):
            with sp.Fori(0, NT // 2) as i:
                for p in (0, 1):
                    t = 2 * i + p
                    sp.wait_ge(S.h3_ready, done(t))
                    sp.dma_start(e.d.h3[ds(t * P, P), :], H3[p]).then_inc(h3_st[p], 16)
            for p in (0, 1):
                sp.wait_ge(h3_st[p], 16 * (NT // 2 + 1))

        @block.gpsimd
        def _(g):
            pass

        @block.scalar
        def _(act):
            def norm_h(t):
                act.wait_ge(S.h_ready, done(t - 1))
                act.sem_inc(S.settled, 1)
                act.activation(junk, cut(X1, t) if not isinstance(t, int) else X1[:, t, :], ACT.Square, accum_out=ss)
                act.drain()
                rstd(act, rs, ss, D, e.eps_rms).then_inc(S.r_ready, 1)

            def q_out(t, h):
                act.wait_ge((S.qa_psum, S.q_psum)[h], done(t))
                act.activation(Q[:, 512 * h:512 * h + 512], Q_[:, 512 * h:512 * h + 512], ACT.Copy).then_inc(S.q_out, 1)

            def q_norm(t):
                act.wait_ge(S.qss_ready, done(t))
                rstd(act, qr, qs, CA_D, e.eps_rms).then_inc(S.qr_ready, 1)

            def exp(t):
                act.wait_ge(S.sm_ready, done(t))
                act.activation(PR, PR, ACT.Exp).then_inc(S.p_ready, 1)

            def start():
                act.preload_act_table_set(LN_EXP)
                prime(act, S.r_ready, (S.q_out, 2), S.qr_ready, S.p_ready, S.pT_ready, S.oT_ready, S.r3_ready)
                norm_h(0)
                q_out(0, 0)
                q_out(0, 1)
                q_norm(0)
                norm_h(1)
                exp(0)

            def body(t, p, i, nxt, nxt2):
                act.wait_ge(S.pT_psum, done(t))
                act.activation(PT.rearrange("p k n -> p (k n)"), W_, ACT.Copy).then_inc(S.pT_ready, 1)
                if nxt:
                    act.wait_ge(S.qT_psum, done(t))
                    q_out(t + 1, 0)
                act.wait_ge(S.oT_psum, done(t))
                act.activation(OT.rearrange("p k n -> p (k n)"), T_, ACT.Copy).then_inc(S.oT_ready, 1)
                if nxt:
                    q_out(t + 1, 1)
                    q_norm(t + 1)
                if nxt2:
                    norm_h(t + 2)
                act.wait_ge(S.x_ready, done(t))
                act.sem_inc(S.settled, 1)
                act.activation(junk, cut(X1, t) if not isinstance(t, int) else X1[:, t, :], ACT.Square, accum_out=ss3)
                act.drain()
                rstd(act, rs3, ss3, D, e.eps_rms).then_inc(S.r3_ready, 1)
                if nxt:
                    exp(t + 1)

            steps(act, start, body)

        @block.tensor
        def _(pe):
            def transposes(out, src, sem):
                for k in range(KD):
                    ins = pe.transpose(out[:, k * P:(k + 1) * P], src[:, k * P:(k + 1) * P], e.ident)
                ins.then_inc(sem, 1)

            def h_transposed(t):
                pe.wait_ge(S.h_ready, done(t))
                pe.wait_ge(S.q_out, done(t - 1, 2))
                transposes(Q_, H, S.hT_psum)

            def project(out, src, w, h, k0=0, k1=KD):
                for k in range(k0, k1):
                    ins = pe.matmul(out[:, 512 * h:512 * h + 512], src[:, k, :], w[:, k, 512 * h:512 * h + 512], start=k == 0, stop=k == KD - 1)
                return ins

            def q_transposed(t):
                pe.wait_ge(S.qn_ready, done(t))
                pe.wait_ge(S.oT_ready, done(t - 1))
                transposes(T_, Q, S.qT_psum)

            def scores(t):
                pe.wait_ge(S.qT_ready, done(t))
                pe.wait_ge(S.on_ready, done(t - 1))
                pe.wait_ge(S.lg_done, done(t - 2))
                for h in range(CA_H):
                    for q in range(2):
                        ins = pe.matmul(S_[:, MEM * h:MEM * h + MEM], QT[:, 2 * h + q, :], KM[:, 2 * h + q, :], start=q == 0, stop=q == 1)
                ins.then_inc(S.s_psum, 1)

            def start():
                prime(pe, S.hT_psum, S.qa_psum, S.q_psum, S.qT_psum, S.s_psum, S.pT_psum, S.o_psum, S.oT_psum, S.wo_psum, S.h3T_psum, S.lg_psum)
                h_transposed(0)
                pe.wait_ge(S.hT_ready, done(0))
                pe.wait_ge(e.ca_ld.wq_ld, 16)
                project(Q_, HT, WQ, 0).then_inc(S.qa_psum, 1)
                project(Q_, HT, WQ, 1).then_inc(S.q_psum, 1)
                q_transposed(0)
                h_transposed(1)
                scores(0)
                pe.wait_ge(e.ca_ld.wo_ld, 16)
                pe.wait_ge(e.ca_ld.wr_ld, 32)

            def body(t, p, i, nxt, nxt2):
                pe.wait_ge(S.p_ready, done(t))
                pe.wait_ge(S.x_ready, done(t - 1))
                transposes(W_, PR, S.pT_psum)
                if nxt:
                    pe.wait_ge(S.hT_ready, done(t + 1))
                    project(Q_, HT, WQ, 0).then_inc(S.qa_psum, 1)
                pe.wait_ge(S.pT_ready, done(t))
                pe.wait_ge(S.sm_ready, done(t))
                pe.wait_ge(S.lg_done, done(t - 1))
                for h in range(CA_H):
                    for m in range(2):
                        ins = pe.matmul(S_[:, CA_D * h:CA_D * h + CA_D], PT[:, 2 * h + m, :], VM[:, m, CA_D * h:CA_D * h + CA_D], start=m == 0, stop=m == 1)
                ins.then_inc(S.o_psum, 1)
                if nxt:
                    project(Q_, HT, WQ, 1, 0, KD // 2)
                pe.wait_ge(S.on_ready, done(t))
                pe.wait_ge(S.h3T_ready, done(t - 1))
                transposes(T_, O, S.oT_psum)
                if nxt:
                    project(Q_, HT, WQ, 1, KD // 2).then_inc(S.q_psum, 1)
                pe.wait_ge(S.oT_ready, done(t))
                for h in range(2):
                    ins = project(W_, OT, WO, h)
                ins.then_inc(S.wo_psum, 1)
                if nxt:
                    q_transposed(t + 1)
                if nxt2:
                    h_transposed(t + 2)
                pe.wait_ge(S.h3_ready, done(t))
                if nxt:
                    pe.wait_ge(S.qT_ready, done(t + 1))
                transposes(T_, H3[p], S.h3T_psum)
                if nxt:
                    scores(t + 1)
                pe.wait_ge(S.h3T_ready, done(t))
                if nxt:
                    pe.wait_ge(S.sm_ready, done(t + 1))
                for k in range(KD):
                    ins = pe.matmul(LP, RT[:, k, :], WR[:, k, :], start=k == 0, stop=k == KD - 1)
                ins.then_inc(S.lg_psum, 1)

            LP = S_[:, 0:NG + NE]
            steps(pe, start, body)

        @block.vector
        def _(v):
            def gain(ap, ps, name):
                return v.tensor_tensor(ap, ps.rearrange("p (k n) -> p k n", n=P), bc(e.pcol(name, KD).unsqueeze(2), [P, KD, P]), ALU.mult)

            def x(t):
                return X1[:, t, :] if isinstance(t, int) else cut(X1, t)

            def scale_h(t):
                v.wait_ge(S.r_ready, done(t))
                v.wait_ge(S.hT_psum, done(t - 1))
                v.tensor_scalar(H, x(t), rs, None, ALU.mult).then_inc(S.h_ready, 1)

            def gain_h(t):
                v.wait_ge(S.hT_psum, done(t))
                v.wait_ge(S.q_psum, done(t - 1))
                gain(HT, Q_, "g_ca").then_inc(S.hT_ready, 1)

            def q_norm(t):
                v.wait_ge(S.q_out, done(t, 2))
                v.tensor_tensor(SQ, Q, Q, ALU.mult)
                v.drain()
                v.tensor_reduce(qs, heads(SQ), AX, ALU.add).then_inc(S.qss_ready, 1)
                v.wait_ge(S.qr_ready, done(t))
                newton(v, qr, qs, qt, CA_D)
                v.tensor_tensor(heads(Q), heads(Q), bc(qr.unsqueeze(2), [P, CA_H, CA_D]), ALU.mult).then_inc(S.qn_ready, 1)

            def q_gain(t):
                v.wait_ge(S.qT_psum, done(t))
                v.wait_ge(S.s_psum, done(t - 1))
                v.tensor_tensor(QT.rearrange("p (h q) n -> p h q n", q=2), T_.rearrange("p (h q n) -> p h q n", q=2, n=P),
                                bc(e.pcol("ca_q", 2).unsqueeze(1).unsqueeze(3), [P, CA_H, 2, P]), ALU.mult).then_inc(S.qT_ready, 1)

            def shift(t):
                v.wait_ge(S.s_psum, done(t))
                v.tensor_reduce(mx, heads(S_), AX, ALU.max)
                v.drain()
                v.wait_ge(S.pT_psum, done(t - 1))
                v.tensor_tensor(heads(PR), heads(S_), bc(mx.unsqueeze(2), [P, CA_H, MEM]), ALU.subtract).then_inc(S.sm_ready, 1)

            def denominators(t):
                v.wait_ge(S.p_ready, done(t))
                v.tensor_reduce(den, heads(PR), AX, ALU.add)
                v.drain()
                v.reciprocal(den, den)
                v.drain()

            def start():
                prime(v, S.h_ready, S.hT_ready, S.qss_ready, S.qn_ready, S.qT_ready, S.sm_ready, S.on_ready, S.x_ready, S.h3_ready, S.h3T_ready, S.lg_done)
                for p in (0, 1):
                    v.sem_inc(h3_st[p], 16)
                scale_h(0)
                gain_h(0)
                q_norm(0)
                scale_h(1)
                q_gain(0)
                gain_h(1)
                shift(0)

            def body(t, p, i, nxt, nxt2):
                denominators(t)
                v.wait_ge(S.o_psum, done(t))
                v.wait_ge(S.oT_psum, done(t - 1))
                v.tensor_tensor(heads(O), heads(S_), bc(den.unsqueeze(2), [P, CA_H, CA_D]), ALU.mult).then_inc(S.on_ready, 1)
                if nxt:
                    q_norm(t + 1)
                if nxt2:
                    scale_h(t + 2)
                v.drain()
                v.wait_ge(S.wo_psum, done(t))
                v.tensor_tensor(x(t), x(t), W_, ALU.add).then_inc(S.x_ready, 1)
                v.drain()
                if nxt:
                    q_gain(t + 1)
                v.drain()
                v.wait_ge(S.r3_ready, done(t))
                v.wait_ge(S.h3T_psum, done(t - 2))
                v.wait_ge(h3_st[p], 16 * i + 16)
                v.tensor_scalar(H3[p], x(t), rs3, None, ALU.mult).then_inc(S.h3_ready, 1)
                if nxt2:
                    gain_h(t + 2)
                v.wait_ge(S.h3T_psum, done(t))
                v.wait_ge(S.lg_psum, done(t - 1))
                gain(RT, T_, "g_ffn").then_inc(S.h3T_ready, 1)
                if nxt:
                    shift(t + 1)
                v.wait_ge(S.lg_psum, done(t))
                v.tensor_tensor(LG[:, t, :] if isinstance(t, int) else cut(LG, t), S_[:, 0:NG + NE], e.rowp("r_b", NG + NE), ALU.add).then_inc(S.lg_done, 1)
                v.drain()

            steps(v, start, body)


def phase_route(nc, e):
    A = e.A
    LG = A(e.at_LG, NT, NG + NE)
    at = e.at_ca
    e.W_exp = []
    for p in (0, 1):
        e.W_exp.append((A(at, KD, EH), A(at + 4096, KD, EH), A(at + 8192, EH // P, D)))
        at += 12288
    e.at_exp = at
    e.exp_ld = e.sems("exp_ld", "wg_ld0 wg_ld1 wu_ld0 wu_ld1 wd_ld0 wd_ld1")
    def new(*s):
        nonlocal at
        n = int(np.prod(s))
        r = A(at, *s)
        at += n
        return r
    EL, OH1, OH2, AS, CUM, T = (new(NT, NE) for _ in range(6))
    OG, EG, TG = new(NT, NG), new(NT, NG), new(NT, NG)
    gmax, gsum, rank, l1, l2, r, g1, g2, i1, i2, p1, p2, s1, s2 = (new(NT) for _ in range(14))
    ROW = new(2, NT, 4)
    SLOT = new(2, NT)
    CNT, CNI, NO, CO, TO, OL = new(NE), new(NE), new(NE), new(NE), new(NE, MAX_OVER + 1), new(4, MAX_OVER + 1)
    rowi, sloti = ROW.bitcast(I32), SLOT.bitcast(I32)
    PG, PN = e.PS[:, 0, 0:NT * NE], e.PS[:, 1, 0:NE]
    S = e.sems("route", "iota_done g_ready g_exp e_ready e_exp a_ready pos_psum row_ready tab_st cnt_psum")
    OV = A(e.at_over, 4, MAX_OVER + 1)
    assert at <= ARENA
    with nc.Block() as block:
        @block.sync
        def _(sp):
            for p in (0, 1):
                for n, (src, ld) in enumerate(((e.d.w_gate, (e.exp_ld.wg_ld0, e.exp_ld.wg_ld1)), (e.d.w_up, (e.exp_ld.wu_ld0, e.exp_ld.wu_ld1)),
                                               (e.d.w_down, (e.exp_ld.wd_ld0, e.exp_ld.wd_ld1)))):
                    w = e.W_exp[p][n]
                    sp.dma_start(w, src[p:p + 1].rearrange("o p (k n) -> p (o k) n", n=w.shape[2])).then_inc(ld[p], 16)

        @block.gpsimd
        def _(g):
            for k in range(2):
                g.iota(rowi[:, k, :, 0:1], pattern=[[P, NT], [0, 1]], base=0, channel_multiplier=1)
                g.iota(rowi[:, k, :, 1:2], pattern=[[P, NT], [0, 1]], base=k * SEQ, channel_multiplier=1)
                g.memset(rowi[:, k, :, 3:4], 0)
            g.iota(OL.bitcast(I32)[:, 0, :], pattern=[[1, MAX_OVER + 1]], base=0, channel_multiplier=0)
            g.iota(OL.bitcast(I32)[:, 1, 0:1], pattern=[[1, 1]], base=0, channel_multiplier=0)
            g.drain()
            g.sem_inc(S.iota_done, 1)
            g.wait_ge(S.row_ready, 1)
            for k in range(2):
                for t in range(NT):
                    g.indirect_dma_start(out=e.d.tab, out_offset=bass.IndirectOffsetOnAxis(ap=sloti[:, k, t:t + 1], axis=0),
                                         in_=rowi[:, k, t, :], in_offset=None).then_inc(S.tab_st, 16)
            g.wait_ge(S.tab_st, 16 * 2 * NT)

        @block.scalar
        def _(act):
            act.wait_ge(S.g_ready, 1)
            act.activation(EG, EG, ACT.Exp).then_inc(S.g_exp, 1)
            act.wait_ge(S.e_ready, 1)
            act.activation(r, r, ACT.Exp).then_inc(S.e_exp, 1)

        @block.tensor
        def _(pe):
            pe.wait_ge(S.a_ready, 1)
            flat = lambda ap: ap.rearrange("p t n -> p (t n)")
            pe.matmul(PG, e.tri_lt, flat(AS), start=True, stop=False)
            pe.matmul(PG, e.ones, flat(CUM), start=False, stop=True).then_inc(S.pos_psum, 1)
            pe.matmul(PN, e.ones, CUM[:, NT - 1, :], start=True, stop=False)
            pe.matmul(PN, e.ones, AS[:, NT - 1, :], start=False, stop=True).then_inc(S.cnt_psum, 1)

        @block.vector
        def _(v):
            over = lambda ap, n: bc(ap.unsqueeze(2), [P, NT, n])
            def op(out, a, b, o):
                v.tensor_tensor(out, a, b, o)
                v.drain()
            def red(out, a, o):
                v.tensor_reduce(out, a, AX, o)
                v.drain()
            def first(onehot, x, best, n, ranks, tmp):
                op(onehot, x, over(best, n), ALU.is_equal)
                op(tmp, onehot, bc(ranks.unsqueeze(1), [P, NT, n]), ALU.mult)
                red(rank, tmp, ALU.max)
                op(onehot, over(rank, n), bc(ranks.unsqueeze(1), [P, NT, n]), ALU.is_equal)

            GL, XL = LG[:, :, 0:NG], LG[:, :, NG:]
            red(gmax, GL, ALU.max)
            first(OG, GL, gmax, NG, e.rowp("rank_g", NG), TG)
            v.tensor_tensor(EG, GL, over(gmax, NG), ALU.subtract).then_inc(S.g_ready, 1)
            v.wait_ge(S.g_exp, 1)
            red(gsum, EG, ALU.add)
            v.tensor_scalar(TG, OG, BIG, -BIG, ALU.mult, ALU.add)
            v.drain()
            eg = lambda ap: ap.rearrange("p t (g n) -> p t g n", g=NG)
            for t in range(NT):
                v.tensor_tensor(eg(T)[:, t], eg(XL)[:, t], bc(OG[:, t, :].unsqueeze(2), [P, NG, EPG]), ALU.mult)
            v.drain()
            for t in range(NT):
                v.tensor_tensor(eg(EL)[:, t], eg(T)[:, t], bc(TG[:, t, :].unsqueeze(2), [P, NG, EPG]), ALU.add)
            v.drain()
            red(l1, EL, ALU.max)
            first(OH1, EL, l1, NE, e.rowp("rank_e", NE), T)
            v.tensor_scalar(i1, rank, -1.0, float(NE), ALU.mult, ALU.add)
            v.scalar_tensor_tensor(EL, OH1, -2.0 * BIG, EL, ALU.mult, ALU.add)
            v.drain()
            red(l2, EL, ALU.max)
            first(OH2, EL, l2, NE, e.rowp("rank_e", NE), T)
            v.tensor_scalar(i2, rank, -1.0, float(NE), ALU.mult, ALU.add)
            v.tensor_tensor(r, l2, l1, ALU.subtract).then_inc(S.e_ready, 1)
            op(AS, OH1, OH2, ALU.add)
            v.memset(CUM[:, 0, :], 0.0)
            v.drain()
            for t in range(1, NT):
                op(CUM[:, t, :], CUM[:, t - 1, :], AS[:, t - 1, :], ALU.add)
            v.sem_inc(S.a_ready, 1)
            v.wait_ge(S.e_exp, 1)
            v.tensor_scalar(g1, r, 1.0, None, ALU.add)
            v.drain()
            op(g1, g1, gsum, ALU.mult)
            v.reciprocal(g1, g1)
            v.drain()
            op(g2, g1, r, ALU.mult)
            v.wait_ge(S.pos_psum, 1)
            pos = PG.rearrange("p (t n) -> p t n", n=NE)
            v.wait_ge(S.iota_done, 1)
            for k, (oh, i, g) in enumerate(((OH1, i1, g1), (OH2, i2, g2))):
                op(T, oh, pos, ALU.mult)
                red(p1, T, ALU.add)
                v.scalar_tensor_tensor(s1, i, float(SEQ), p1, ALU.mult, ALU.add)
                v.drain()
                v.tensor_copy(sloti[:, k, :], s1)
                v.tensor_copy(ROW[:, k, :, 2:3].rearrange("p t o -> p (t o)"), g)
                v.drain()
            v.sem_inc(S.row_ready, 1)
            v.wait_ge(S.cnt_psum, 1)
            v.tensor_scalar(CNT, PN, float(P), None, ALU.is_gt)
            v.drain()
            v.tensor_copy(NO, CNT)
            v.drain()
            for b in range(2, MAX_BLOCKS):
                v.tensor_scalar(CNT, PN, float(P * b), None, ALU.is_gt)
                v.drain()
                op(NO, NO, CNT, ALU.add)
            v.tensor_copy(CO[:, 0:1], NO[:, 0:1])
            v.drain()
            for x in range(1, NE):
                op(CO[:, x:x + 1], CO[:, x - 1:x], NO[:, x:x + 1], ALU.add)
            N = OL[:, 2, :]
            v.tensor_copy(N, OL.bitcast(I32)[:, 0, :])
            v.drain()
            nb = MAX_OVER + 1
            before = TO
            op(before, bc(CO.unsqueeze(2), [P, NE, nb]), bc(N.unsqueeze(1), [P, NE, nb]), ALU.is_le)
            red(OV[:, 3, :], before.rearrange("p x n -> p n x"), ALU.add)
            op(before, before, bc(NO.unsqueeze(2), [P, NE, nb]), ALU.mult)
            red(OL[:, 3, :], before.rearrange("p x n -> p n x"), ALU.add)
            op(N, N, OL[:, 3, :], ALU.subtract)
            v.tensor_scalar(N, N, float(P), float(P), ALU.mult, ALU.add)
            v.tensor_scalar(OV[:, 3, :], OV[:, 3, :], float(NE - 1), None, ALU.min)
            v.drain()
            v.scalar_tensor_tensor(N, OV[:, 3, :], float(SEQ), N, ALU.mult, ALU.add)
            v.drain()
            v.tensor_scalar(N, N, float(NE * SEQ - P), None, ALU.min)
            v.drain()
            v.tensor_copy(OV.bitcast(I32)[:, 0, :], OV[:, 3, :])
            v.tensor_copy(OV.bitcast(I32)[:, 1, :], N)
            v.tensor_copy(OV.bitcast(I32)[:, 2, 0:1], CO[:, NE - 1:NE])
            v.drain()


def phase_experts(nc, e):
    A = e.A
    W, at = e.W_exp, e.at_exp
    XT = [A(at + D * p, KD, P) for p in (0, 1)]; at += 2 * D
    E_ = A(at, EH); at += EH
    HID = [A(at + EH * p, EH) for p in (0, 1)]; at += 2 * EH
    HT = [A(at + EH * p, EH // P, P) for p in (0, 1)]; at += 2 * EH
    Y = [A(at + D * p, D) for p in (0, 1)]; at += 2 * D
    assert at <= ARENA, at
    at = AT_HT
    XG = [A(at + D * p, D) for p in (0, 1)]; at += 2 * D
    IX = A(at, NE, 4); at += NE * 4
    IG = [A(at + 4 * p, 4) for p in (0, 1)]; at += 8
    IS = [A(at + 4 * p, 4) for p in (0, 1)]; at += 8
    assert at <= e.at_X1
    IXI = IX.bitcast(I32)
    IGI, ISI = [a.bitcast(I32) for a in IG], [a.bitcast(I32) for a in IS]
    S = e.sems("exp", "settled ig_ready is_ready ix_ld xg_ld0 xg_ld1 y_st0 y_st1 xT_psum xT_ready gu_psum g_silu gu_read "
               "hT_psum hT_ready y_psum y_out")
    wg_ld, wu_ld, wd_ld = e.exp_ld[0:2], e.exp_ld[2:4], e.exp_ld[4:6]
    xg_ld, y_st = (S.xg_ld0, S.xg_ld1), (S.y_st0, S.y_st1)
    PX, PY = e.pair(0), e.pair(3)
    PH = e.PS[:, 0, :]
    PGU = [(e.PS[:, 2 + 2 * p, :], e.PS[:, 3 + 2 * p, :]) for p in (0, 1)]
    last = NE // 2 - 1

    def steps(eng, step):
        for x in range(4):
            step(x, x // 2, x % 2, x == 0, False)
        with eng.Fori(2, last) as i:
            for p in (0, 1):
                step(2 * i + p, i, p, False, False)
        for p in (0, 1):
            step(2 * last + p, last, p, False, p == 1)

    with nc.Block() as block:
        @block.sync
        def _(sp):
            w = lambda src, x, n: src[ds(x, 1)].rearrange("o p (k n) -> p (o k) n", n=n)

            def load(x, p):
                sp.dma_start(W[p][0], w(e.d.w_gate, x, EH)).then_inc(wg_ld[p], 16)
                sp.dma_start(W[p][1], w(e.d.w_up, x, EH)).then_inc(wu_ld[p], 16)

            def load_down(x, p):
                sp.dma_start(W[p][2], w(e.d.w_down, x, D)).then_inc(wd_ld[p], 16)

            with sp.Fori(1, NE // 2) as i:
                for p in (0, 1):
                    x = 2 * i + p
                    sp.wait_ge(S.gu_psum, done(x - 2))
                    load(x, p)
                    sp.wait_ge(S.y_psum, done(x - 2))
                    load_down(x, p)

        @block.gpsimd
        def _(g):
            def gather(x, p):
                g.wait_ge(S.xT_psum, done(x - 2))
                g.tensor_copy(IGI[p], IXI[:, ds(x, 1), :].rearrange("p o n -> p (o n)")).then_inc(S.ig_ready, 1)
                g.wait_ge(S.ig_ready, x + 1)
                g.sem_inc(S.settled, 1)
                g.indirect_dma_start(out=XG[p], out_offset=None, in_=e.d.h3,
                                     in_offset=bass.IndirectOffsetOnAxis(ap=IGI[p][:, 0:1], axis=0)).then_inc(xg_ld[p], 16)

            def scatter(x, p):
                g.wait_ge(S.y_out, done(x))
                g.tensor_copy(ISI[p], IXI[:, ds(x, 1), :].rearrange("p o n -> p (o n)")).then_inc(S.is_ready, 1)
                g.wait_ge(S.is_ready, x + 1)
                g.sem_inc(S.settled, 1)
                g.indirect_dma_start(out=e.d.yc, out_offset=bass.IndirectOffsetOnAxis(ap=ISI[p][:, 1:2], axis=0), in_=Y[p],
                                     in_offset=None, bounds_check=2 * SEQ - 1, oob_is_err=False).then_inc(y_st[p], 16)

            g.dma_start(IXI, e.d.tab.rearrange("(x r) c -> r x c", r=SEQ)[0:P]).then_inc(S.ix_ld, 16)
            g.wait_ge(S.ix_ld, 16)

            def step(x, i, p, first, end):
                if not (isinstance(i, int) and i == last):
                    g.wait_ge(xg_ld[p], 16 * i + 16)
                    gather(x + 2, p)
                if not first:
                    if not (isinstance(x, int) and x <= 2):
                        g.wait_ge(y_st[1 - p], 16 * i - 16 + 16 * p)
                    scatter(x - 1, 1 - p)

            gather(0, 0)
            gather(1, 1)
            steps(g, step)
            g.wait_ge(y_st[1], 16 * last)
            scatter(NE - 1, 1)
            for p in (0, 1):
                g.wait_ge(y_st[p], 16 * (NE // 2))

        @block.scalar
        def _(act):
            def hidden_out(x, p):
                act.wait_ge(S.hT_psum, done(x))
                act.wait_ge(S.y_psum, done(x - 2))
                act.activation(HT[p].rearrange("p k n -> p (k n)"), PH, ACT.Copy).then_inc(S.hT_ready, 1)

            def y_out(x, p, stores):
                act.wait_ge(S.y_psum, done(x))
                if stores is not None:
                    act.wait_ge(y_st[p], stores)
                act.activation(Y[p], PY, ACT.Copy, scale=IX[:, ds(x, 1), 2:3].rearrange("p o n -> p (o n)")).then_inc(S.y_out, 1)

            def step(x, i, p, first, end):
                if not first:
                    hidden_out(x - 1, 1 - p)
                act.wait_ge(S.gu_psum, done(x))
                act.wait_ge(S.gu_read, done(x - 1))
                act.activation(E_, PGU[p][0], ACT.Silu).then_inc(S.g_silu, 1)
                if not first:
                    y_out(x - 1, 1 - p, None if isinstance(x, int) and x <= 2 else 16 * i - 16 + 16 * p)

            act.preload_act_table(ACT.Silu)
            prime(act, S.hT_ready, S.g_silu, S.y_out)
            act.wait_ge(S.ix_ld, 16)
            steps(act, step)
            hidden_out(NE - 1, 1)
            y_out(NE - 1, 1, 16 * last)

        @block.tensor
        def _(pe):
            def tokens(x, p, loads):
                pe.wait_ge(xg_ld[p], loads)
                pe.wait_ge(S.hT_ready, done(x - 2))
                for k in range(KD):
                    ins = pe.transpose(PX[:, k * P:(k + 1) * P], XG[p][:, k * P:(k + 1) * P], e.ident)
                ins.then_inc(S.xT_psum, 1)

            def hidden(x, p):
                pe.wait_ge(S.gu_read, done(x))
                for k in range(EH // P):
                    ins = pe.transpose(PH[:, k * P:(k + 1) * P], HID[p][:, k * P:(k + 1) * P], e.ident)
                ins.then_inc(S.hT_psum, 1)

            def down(x, p, loads):
                pe.wait_ge(wd_ld[p], loads)
                pe.wait_ge(S.hT_ready, done(x))
                pe.wait_ge(S.y_out, done(x - 1))
                for h in range(2):
                    for k in range(EH // P):
                        ins = pe.matmul(PY[:, 512 * h:512 * h + 512], HT[p][:, k, :], W[p][2][:, k, 512 * h:512 * h + 512], start=k == 0, stop=k == EH // P - 1)
                ins.then_inc(S.y_psum, 1)

            def step(x, i, p, first, end):
                pe.wait_ge(S.xT_ready, done(x))
                if not first:
                    hidden(x - 1, 1 - p)
                for n, ld in enumerate((wg_ld, wu_ld)):
                    pe.wait_ge(ld[p], 16 * i + 16)
                    if n == 0:
                        pe.wait_ge(S.gu_read, done(x - 2))
                    for k in range(KD):
                        ins = pe.matmul(PGU[p][n], XT[p][:, k, :], W[p][n][:, k, :], start=k == 0, stop=k == KD - 1)
                ins.then_inc(S.gu_psum, 1)
                if not end:
                    tokens(x + 1, 1 - p, 16 * i + 16 + 16 * p)
                if not first:
                    down(x - 1, 1 - p, 16 * i + 16 * p)

            prime(pe, S.xT_psum, S.gu_psum, S.hT_psum, S.y_psum)
            tokens(0, 0, 16)
            steps(pe, step)
            hidden(NE - 1, 1)
            down(NE - 1, 1, 16 * (NE // 2))

        @block.vector
        def _(v):
            def tokens_out(x, p):
                v.wait_ge(S.xT_psum, done(x))
                v.wait_ge(S.gu_psum, done(x - 2))
                v.tensor_tensor(XT[p], PX.rearrange("p (k n) -> p k n", n=P), bc(e.pcol("g_ffn", KD).unsqueeze(2), [P, KD, P]), ALU.mult).then_inc(S.xT_ready, 1)

            def step(x, i, p, first, end):
                if not end:
                    tokens_out(x + 1, 1 - p)
                v.wait_ge(S.g_silu, done(x))
                v.wait_ge(S.hT_psum, done(x - 2))
                v.tensor_tensor(HID[p], E_, PGU[p][1], ALU.mult).then_inc(S.gu_read, 1)
                v.drain()

            prime(v, S.xT_ready, S.gu_read)
            tokens_out(0, 0)
            steps(v, step)
    e.exp = dict(W=W[0], XT=XT[0], E=E_, HID=HID[0], HT=HT[0], Y=Y[0], XG=XG[0], IX=IX[:, 0, :])


def phase_overflow(nc, e):
    A = e.A
    b = e.exp
    W, XT, E_, HID, HT, Y, XG, IX = (b[k] for k in ("W", "XT", "E", "HID", "HT", "Y", "XG", "IX"))
    OV = A(e.at_over, 4, MAX_OVER + 1).bitcast(I32)
    PX, PY = e.pair(0), e.pair(3)
    G, U, PH = e.PS[:, 2, :], e.PS[:, 3, :], e.PS[:, 4, :]
    S = e.sems("over", "settled w_ld ix_ld xg_ld y_st xT_psum xT_ready gu_psum g_silu hid_ready hT_psum hT_ready y_psum y_out")
    number = lambda eng: eng.value_load(OV[0:1, 2, 0:1], min_val=0, max_val=MAX_OVER)

    def loop(eng, body):
        n_over = number(eng)
        with eng.Fori(0, MAX_OVER) as n:
            with eng.If(n_over > n):
                body(n)

    with nc.Block() as block:
        @block.sync
        def _(sp):
            def body(n):
                x = sp.value_load(OV[0:1, 0, ds(n, 1)], min_val=0, max_val=NE - 1)
                sp.wait_ge(S.y_out, n + 1)
                for m, (src, w) in enumerate(((e.d.w_gate, EH), (e.d.w_up, EH), (e.d.w_down, D))):
                    sp.dma_start(W[m], src[ds(x, 1)].rearrange("o p (k n) -> p (o k) n", n=w)).then_inc(S.w_ld, 16)
            loop(sp, body)

        @block.gpsimd
        def _(g):
            def body(n):
                row = g.value_load(OV[0:1, 1, ds(n, 1)], min_val=0, max_val=NE * SEQ - P)
                g.wait_ge(S.y_out, n + 1)
                g.dma_start(IX.bitcast(I32), e.d.tab[ds(row, P), :]).then_inc(S.ix_ld, 16)
                g.wait_ge(S.ix_ld, 16 * n + 16)
                g.sem_inc(S.settled, 1)
                g.indirect_dma_start(out=XG, out_offset=None, in_=e.d.h3,
                                     in_offset=bass.IndirectOffsetOnAxis(ap=IX.bitcast(I32)[:, 0:1], axis=0)).then_inc(S.xg_ld, 16)
                g.wait_ge(S.y_out, n + 2)
                g.sem_inc(S.settled, 1)
                g.indirect_dma_start(out=e.d.yc, out_offset=bass.IndirectOffsetOnAxis(ap=IX.bitcast(I32)[:, 1:2], axis=0), in_=Y,
                                     in_offset=None, bounds_check=2 * SEQ - 1, oob_is_err=False).then_inc(S.y_st, 16)
                g.wait_ge(S.y_st, 16 * n + 16)
                g.sem_inc(S.settled, 1)
            loop(g, body)

        @block.scalar
        def _(act):
            def body(n):
                act.wait_ge(S.gu_psum, n + 1)
                act.activation(E_, G, ACT.Silu).then_inc(S.g_silu, 1)
                act.wait_ge(S.hT_psum, n + 1)
                act.activation(HT.rearrange("p k n -> p (k n)"), PH, ACT.Copy).then_inc(S.hT_ready, 1)
                act.wait_ge(S.y_psum, n + 1)
                act.activation(Y, PY, ACT.Copy, scale=IX[:, 2:3]).then_inc(S.y_out, 1)
            act.sem_inc(S.y_out, 1)
            loop(act, body)

        @block.tensor
        def _(pe):
            def body(n):
                pe.wait_ge(S.xg_ld, 16 * n + 16)
                for k in range(KD):
                    ins = pe.transpose(PX[:, k * P:(k + 1) * P], XG[:, k * P:(k + 1) * P], e.ident)
                ins.then_inc(S.xT_psum, 1)
                pe.wait_ge(S.xT_ready, n + 1)
                pe.wait_ge(S.w_ld, 48 * n + 48)
                for m, out in enumerate((G, U)):
                    for k in range(KD):
                        ins = pe.matmul(out, XT[:, k, :], W[m][:, k, :], start=k == 0, stop=k == KD - 1)
                ins.then_inc(S.gu_psum, 1)
                pe.wait_ge(S.hid_ready, n + 1)
                for k in range(EH // P):
                    ins = pe.transpose(PH[:, k * P:(k + 1) * P], HID[:, k * P:(k + 1) * P], e.ident)
                ins.then_inc(S.hT_psum, 1)
                pe.wait_ge(S.hT_ready, n + 1)
                for h in range(2):
                    for k in range(EH // P):
                        ins = pe.matmul(PY[:, 512 * h:512 * h + 512], HT[:, k, :], W[2][:, k, 512 * h:512 * h + 512], start=k == 0, stop=k == EH // P - 1)
                ins.then_inc(S.y_psum, 1)
            loop(pe, body)

        @block.vector
        def _(v):
            def body(n):
                v.wait_ge(S.xT_psum, n + 1)
                v.tensor_tensor(XT, PX.rearrange("p (k n) -> p k n", n=P), bc(e.pcol("g_ffn", KD).unsqueeze(2), [P, KD, P]), ALU.mult).then_inc(S.xT_ready, 1)
                v.wait_ge(S.g_silu, n + 1)
                v.tensor_tensor(HID, E_, U, ALU.mult).then_inc(S.hid_ready, 1)
            loop(v, body)


def phase_final(nc, e):
    A = e.A
    X1 = A(e.at_X1, NT, D)
    at = e.at_ca
    YC = [A(at + 2 * D * p, 2, D) for p in (0, 1)]; at += 4 * D
    O = [A(at + D * p, D) for p in (0, 1)]
    S = e.sems("fin", "y_ld0 y_ld1 added out_st0 out_st1")
    y_ld, out_st = (S.y_ld0, S.y_ld1), (S.out_st0, S.out_st1)
    yc = e.d.yc.rearrange("(k r) n -> r k n", k=2)
    with nc.Block() as block:
        @block.sync
        def _(sp):
            for p in (0, 1):
                sp.dma_start(YC[p], yc[p * P:(p + 1) * P]).then_inc(y_ld[p], 16)
            with sp.Fori(1, NT // 2) as i:
                for p in (0, 1):
                    t = 2 * i + p
                    sp.wait_ge(S.added, t - 1)
                    sp.dma_start(YC[p], yc[ds(t * P, P)]).then_inc(y_ld[p], 16)

        @block.scalar
        def _(act):
            with act.Fori(0, NT // 2) as i:
                for p in (0, 1):
                    t = 2 * i + p
                    act.wait_ge(S.added, t + 1)
                    act.dma_start(e.d.out[ds(t * P, P), :], O[p]).then_inc(out_st[p], 16)
            for p in (0, 1):
                act.wait_ge(out_st[p], 16 * (NT // 2))

        @block.gpsimd
        def _(g):
            pass

        @block.tensor
        def _(pe):
            pass

        @block.vector
        def _(v):
            def body(t, p, loads):
                v.wait_ge(y_ld[p], loads)
                v.tensor_tensor(O[p], cut(X1, t), YC[p][:, 0, :], ALU.add)
                v.drain()
                v.tensor_tensor(O[p], O[p], YC[p][:, 1, :], ALU.add).then_inc(S.added, 1)

            body(0, 0, 16)
            body(1, 1, 16)
            with v.Fori(1, NT // 2) as i:
                for p in (0, 1):
                    v.wait_ge(out_st[p], 16 * i)
                    body(2 * i + p, p, 16 * i + 16)


def build(nc, d):
    e = Env()
    e.d = d
    ctx = ExitStack()
    with ctx:
        e.arena = ctx.enter_context(nc.sbuf_tensor("arena", [P, ARENA], F32))
        e.PS = ctx.enter_context(nc.psum_tensor("psum", [P, 8, 512], F32))

        def A(at, *shape):
            n = int(np.prod(shape))
            ap = e.arena[:, at:at + n]
            if len(shape) == 2:
                ap = ap.rearrange("p (a b) -> p a b", a=shape[0])
            elif len(shape) == 3:
                ap = ap.rearrange("p (a b c) -> p a b c", a=shape[0], b=shape[1])
            return ap

        def sems(phase, names):
            s = namedtuple(phase, names)(*[nc.alloc_semaphore(f"{phase}_{n}") for n in names.split()])
            e.used += list(s)
            return s

        e.A, e.sems = A, sems
        e.pair = lambda n: e.PS[:, 2 * n:2 * n + 2, :].rearrange("p a b -> p (a b)")
        e.ident, e.tri_le, e.tri_gt, e.ones, e.tri_lt = (A(AT_CONST + P * n, P) for n in range(5))
        e.mask = A(AT_CONST + 5 * P, SEQ)
        e.par, e.row = A(AT_PAR, NPAR), A(AT_ROW, NROW)
        e.pcol = lambda n, w: e.par[:, PC[n]:PC[n] + w]
        e.rowp = lambda n, w: e.row[:, RC[n]:RC[n] + w]
        e.eps_rms, e.eps_ln = e.rowp("eps_rms", 1), e.rowp("eps_ln", 1)
        e.at_U2 = AT_B + GT * (SEQ + 32)
        e.at_YSC = e.at_U2 + GT * SEQ
        e.at_XBC = e.at_YSC + GT * SEQ
        e.at_CAT_SSD, e.at_CAT_ATT, e.at_CAT_CF = AT_HT, AT_HT + GT * SEQ, AT_B
        e.CAT = [A(a, GT, SEQ) for a in (e.at_CAT_SSD, e.at_YSC, e.at_CAT_ATT, e.at_CAT_CF)]
        e.at_X1 = AT_QT
        e.at_work_out = e.at_XBC + NT * GW + 12 * D
        e.at_KM, e.at_VM = AT_HT, AT_HT + KD * MEM
        e.at_LG = e.at_VM + 2 * D
        e.at_over = e.at_LG + NT * (NG + NE)
        e.at_ca = e.at_X1 + NT * D
        e.used = []
        for phase in PHASES:
            if phase == phase_route:
                nc.clear_and_free_semaphores(e.used)
                nc.all_engine_barrier()
                e.used = []
            phase(nc, e)


PHASES = [phase_tokens, phase_features, phase_ssd, phase_attention, phase_norm_cf, phase_out, phase_memory, phase_cross,
          phase_route, phase_experts, phase_overflow, phase_final]


def constants():
    k, n = np.arange(P)[:, None], np.arange(P)[None, :]
    delta = 7 * P + k - np.arange(SEQ)[None, :]
    count = ((delta >= 0) & (delta <= 128)) * 1 + ((delta >= 0) & (delta <= 512) & (delta % 4 == 0)) * 1 \
        + ((delta >= 0) & (delta <= 2048) & (delta % 16 == 0)) * 1
    mask = np.where(count > 0, np.log(np.maximum(count, 1)), -BIG)
    parts = [k == n, k <= n, k > n, np.ones((P, P)), k < n, mask]
    return np.concatenate([np.asarray(a, np.float32) for a in parts], axis=1)


def kernel(**a):
    import concourse.bacc as bacc
    from concourse.bass_utils import run_bass_kernel_spmd

    f = {n: np.asarray(v) for n, v in a.items()}
    cols = lambda v: v.reshape(-1, P).T
    w_in = f["w_in"][0]
    sizes = [GW, XBC_T * P, HEADS, GW, GW, GW, GW, GW, GW, GW, GW]
    o = np.concatenate([[0], np.cumsum(sizes)])
    z, xbc, dt, sb, sc, sh, q, k, v, ca, cg = (w_in[:, o[n]:o[n + 1]] for n in range(11))
    w_tok = np.concatenate([q, k, v, z, dt], axis=1).reshape(KD, P, TOK_COLS).transpose(1, 0, 2)
    tile = lambda w, n: w[:, n * P:(n + 1) * P]
    feats = [tile(w, n) for n in range(GT) for w in (ca, cg)] + [tile(w, n) for n in range(GT) for w in (sb, sc, sh)] \
        + [tile(xbc, n) for n in range(XBC_T)]
    w_feat = np.stack(feats).reshape(NFEAT, KD, P, P).transpose(0, 2, 1, 3).reshape(NFEAT, P, KD * P)
    taps = lambda w: w.reshape(w.shape[0], -1, P).transpose(2, 1, 0).reshape(P, -1)
    twice = lambda g: np.concatenate([g, g]).reshape(P, 1)
    par = np.concatenate([cols(f["norm_mix"][0]), cols(f["norm_ca"][0]), cols(f["norm_mem"][0]), cols(f["norm_ffn"][0]),
                          taps(f["cf_conv_w"][0]), cols(f["cf_conv_b"][0]), cols(f["cf_ln_g"][0]), cols(f["cf_ln_b"][0]),
                          taps(f["ssd_conv_w"][0]), cols(f["ssd_conv_b"][0]), taps(f["sc_conv_w"][0]), cols(f["ssd_norm"][0]),
                          twice(f["attn_q_norm"][0]), twice(f["attn_k_norm"][0]), cols(f["ca_q_norm"][0]), cols(f["ca_k_norm"][0])], axis=1)
    rank = np.concatenate([NG - np.arange(NG), NE - np.arange(NE), [RMS_EPS, LN_EPS]]).astype(np.float32)
    row = np.concatenate([f["ssd_dt_bias"][0], f["ssd_a_log"][0], f["ssd_d"][0], f["router_group_b"][0], f["router_expert_b"][0], rank])
    rows = lambda w: np.swapaxes(w.reshape(*w.shape[:-2], -1, P, w.shape[-1]), -3, -2).reshape(*w.shape[:-2], P, -1)
    arrays = dict(x=f["x"][0], mem=f["mem"][0], consts=constants(), par=par, row=row, w_tok=w_tok, w_feat=w_feat,
                  w_out=f["w_out"][0], ca_wq=f["ca_wq"][0], ca_wkv=f["ca_wkv"][0], ca_wo=f["ca_wo"][0],
                  wg=f["router_group_w"][0], we=f["router_expert_w"][0],
                  w_gate=rows(f["exp_w_gate"][0]), w_up=rows(f["exp_w_up"][0]), w_down=rows(f["exp_w_down"][0]))
    arrays = {n: np.ascontiguousarray(x) for n, x in arrays.items()}
    nc = bacc.Bacc("TRN2", target_bir_lowering=False, num_devices=1)
    dram = {n: nc.dram_tensor(n, x.shape, F32, kind="ExternalInput").ap() for n, x in arrays.items()}
    dram["tab"] = nc.dram_tensor("tab", [NE * SEQ, 4], I32, kind="Internal").ap()
    dram["h3"] = nc.dram_tensor("h3", [SEQ + 1, D], F32, kind="Internal").ap()
    dram["yc"] = nc.dram_tensor("yc", [2 * SEQ, D], F32, kind="Internal").ap()
    dram["out"] = nc.dram_tensor("out", [SEQ, D], F32, kind="ExternalOutput").ap()
    d = namedtuple("Dram", list(dram))(**dram)
    build(nc, d)
    r = run_bass_kernel_spmd(nc, [arrays], core_ids=[0])
    return r.results[0]["out"].reshape(1, SEQ, D)
```
